# Optimizing a Trainium2 kernel written in Bass

```python
import math
import jax, jax.numpy as jnp
from jax import lax
import numpy as np

D_MODEL = 1024
BATCH = 1
SEQ = 1024
DEPTH = 1
DEC_BATCH = 8
DEC_SEQ = 1
PAST_LEN = 1024
PAGE_SIZE = 128

GROUPS = ((128, 1), (512, 4), (2048, 16))
N_GROUPS = 3
HD_A = 64
H_G = D_MODEL // 256
A_QKV = N_GROUPS * 3 * H_G * HD_A
A_OUT = H_G * HD_A
Q_BLOCK = 128
ATTN_SCALE = HD_A ** -0.5
N_BUCKETS = 32
REL_MAX_DIST = 2048
HB = D_MODEL // 128
DK = 128
DV = 128
B_QK = HB * DK
B_V = HB * DV
CONV_W = 4
CONV_DIM = 2 * B_QK + B_V
CHUNK = 64
N_IN = A_QKV + CONV_DIM + B_V + 2 * HB + 2 * D_MODEL
SPLIT_IDX = [A_QKV, A_QKV + CONV_DIM, A_QKV + CONV_DIM + B_V, A_QKV + CONV_DIM + B_V + HB,
             A_QKV + CONV_DIM + B_V + 2 * HB, A_QKV + CONV_DIM + B_V + 2 * HB + D_MODEL]
D_FF = -(-8 * D_MODEL // (3 * 256)) * 256
EPS = 1e-6

kernel_name = "hybrid_dilated_attn_gated_deltanet_decode_step"

def _rms_norm(x, w):
    x32 = x.astype(jnp.float32)
    y = x32 * lax.rsqrt(jnp.mean(x32 * x32, axis=-1, keepdims=True) + EPS)
    return (y * w.astype(jnp.float32)).astype(x.dtype)

def _l2norm(t):
    t = t.astype(jnp.float32)
    return t * lax.rsqrt(jnp.sum(t * t, axis=-1, keepdims=True) + EPS)

def _t5_bucket(dist):
    max_exact = N_BUCKETS // 2
    d = np.maximum(dist, 1).astype(np.float32)
    large = max_exact + (np.log(d / max_exact) / np.log(REL_MAX_DIST / max_exact)
                         * (N_BUCKETS - max_exact)).astype(np.int32)
    large = np.minimum(large, N_BUCKETS - 1)
    return np.where(dist < max_exact, dist, large).astype(np.int32)

def _dilated_attention(q_list, kv_list, rel_bias):
    B, L = q_list[0].shape[:2]
    qb = min(Q_BLOCK, L)
    n_blk = -(-L // qb)
    pad = n_blk * qb - L
    q_pad = [jnp.pad(q, ((0, 0), (0, pad), (0, 0), (0, 0))) for q in q_list]
    biases = []
    for g, (win, dil) in enumerate(GROUPS):
        bucket = _t5_bucket(np.arange(win // dil + 1) * dil)
        biases.append(rel_bias[bucket][:, g * H_G:(g + 1) * H_G].T.astype(jnp.float32))

    def block(b):
        start = b * qb
        i = start + jnp.arange(qb)
        outs, lses = [], []
        for g, (win, dil) in enumerate(GROUPS):
            kv = kv_list[g]
            l_tot = kv.shape[1]
            lb = l_tot - L
            n_keys = win // dil + 1
            idx = lb + i[:, None] - dil * jnp.arange(n_keys)[None, :]
            valid = idx >= 0
            kv_sel = jnp.take(kv, jnp.clip(idx, 0, l_tot - 1), axis=1)
            qg = lax.dynamic_slice_in_dim(q_pad[g], start, qb, axis=1)
            s = (jnp.einsum('bqhd,bqjhd->bhqj', qg, kv_sel[:, :, :, 0]).astype(jnp.float32) * ATTN_SCALE
                 + biases[g][None, :, None, :])
            s = jnp.where(valid[None, None], s, -jnp.inf)
            m = jnp.max(s, axis=-1, keepdims=True)
            p = jnp.exp(s - m)
            den = jnp.sum(p, axis=-1, keepdims=True)
            o = jnp.einsum('bhqj,bqjhd->bqhd', (p / den).astype(kv.dtype), kv_sel[:, :, :, 1])
            outs.append(o.astype(jnp.float32))
            lses.append(jnp.transpose((m + jnp.log(den))[..., 0], (0, 2, 1)))
        wts = jax.nn.softmax(jnp.stack(lses), axis=0)
        o = jnp.einsum('gbqh,gbqhd->bqhd', wts, jnp.stack(outs))
        return o.astype(q_list[0].dtype)

    o = lax.map(block, jnp.arange(n_blk))
    o = jnp.moveaxis(o, 0, 1).reshape(B, n_blk * qb, H_G, HD_A)
    return o[:, :L]

def _causal_conv(x, buf, w):
    L = x.shape[1]
    xc = jnp.concatenate([buf.astype(x.dtype), x], axis=1)
    y = xc[:, 0:L] * w[0]
    for j in range(1, CONV_W):
        y = y + xc[:, j:j + L] * w[j]
    return jax.nn.silu(y), xc[:, -(CONV_W - 1):]

def _gated_delta_rule(q, k, v, g, beta, S0):
    f32 = jnp.float32
    B, L = q.shape[:2]
    C = min(CHUNK, L)
    n = -(-L // C)
    pad = n * C - L

    def prep(t):
        t = t.astype(f32)
        t = jnp.pad(t, [(0, 0), (0, pad)] + [(0, 0)] * (t.ndim - 2))
        t = t.reshape((B, n, C) + t.shape[2:])
        return jnp.moveaxis(t, 3, 1)

    q, k, v, g, beta = prep(q), prep(k), prep(v), prep(g), prep(beta)
    q = q * (DK ** -0.5)
    kb = k * beta[..., None]
    vb = v * beta[..., None]
    gc = jnp.cumsum(g, axis=-1)
    tril = jnp.tril(jnp.ones((C, C), dtype=bool))
    strict = jnp.tril(jnp.ones((C, C), dtype=bool), -1)
    decay = jnp.exp(jnp.where(tril, gc[..., :, None] - gc[..., None, :], -jnp.inf))
    A = jnp.where(strict, jnp.einsum('bhncd,bhnmd->bhncm', kb, k) * decay, 0.0)
    eye = jnp.eye(C, dtype=f32)
    T = lax.linalg.triangular_solve(A + eye, jnp.broadcast_to(eye, A.shape), left_side=True,
                                    lower=True, unit_diagonal=True)
    u = T @ vb
    w = T @ (kb * jnp.exp(gc)[..., None])
    attn = jnp.einsum('bhncd,bhnmd->bhncm', q, k) * decay

    def step(S, xs):
        q_c, k_c, u_c, w_c, attn_c, gc_c = xs
        v_new = u_c - w_c @ S
        o_c = (q_c * jnp.exp(gc_c)[..., None]) @ S + attn_c @ v_new
        g_last = gc_c[..., -1]
        S = (S * jnp.exp(g_last)[..., None, None]
             + jnp.einsum('bhck,bhcv->bhkv', k_c * jnp.exp(g_last[..., None] - gc_c)[..., None], v_new))
        return S, o_c

    xs = tuple(jnp.moveaxis(t, 2, 0) for t in (q, k, u, w, attn, gc))
    S, o = lax.scan(step, S0.astype(f32), xs)
    o = jnp.moveaxis(o, 0, 2).reshape(B, -1, n * C, DV)[:, :, :L]
    return jnp.transpose(o, (0, 2, 1, 3)), S

def _gated_rmsnorm(o, z, w):
    o32 = o.astype(jnp.float32)
    o32 = o32 * lax.rsqrt(jnp.mean(o32 * o32, axis=-1, keepdims=True) + EPS) * w.astype(jnp.float32)
    return o32 * jax.nn.silu(z.astype(jnp.float32))

def _layer(x, kv_bufs, S0, conv_buf, p, l):
    Bsz, L, _ = x.shape
    h = _rms_norm(x, p['norm_pre_mix'][l])
    proj = h @ p['w_in'][l]
    a_qkv, b_qkv, z, b_pre, a_pre, gate_a, gate_b = jnp.split(proj, SPLIT_IDX, axis=-1)
    a_qkv = a_qkv.reshape(Bsz, L, N_GROUPS, 3, H_G, HD_A)
    q_list = [a_qkv[:, :, g, 0] for g in range(N_GROUPS)]
    kv_new = [a_qkv[:, :, g, 1:] for g in range(N_GROUPS)]
    kv_all = [jnp.concatenate([kv_bufs[g].astype(x.dtype), kv_new[g]], axis=1) for g in range(N_GROUPS)]
    o_a = _dilated_attention(q_list, kv_all, p['rel_bias']).reshape(Bsz, L, A_OUT)
    conv_out, conv_new = _causal_conv(b_qkv, conv_buf, p['conv_w'][l])
    qd, kd, vd = jnp.split(conv_out, [B_QK, 2 * B_QK], axis=-1)
    qd = _l2norm(qd.reshape(Bsz, L, HB, DK))
    kd = _l2norm(kd.reshape(Bsz, L, HB, DK))
    vd = vd.reshape(Bsz, L, HB, DV)
    beta = jax.nn.sigmoid(b_pre.astype(jnp.float32))
    g = -jnp.exp(p['a_log'][l].astype(jnp.float32)) * jax.nn.softplus(
        a_pre.astype(jnp.float32) + p['dt_bias'][l].astype(jnp.float32))
    o_b, S = _gated_delta_rule(qd, kd, vd, g, beta, S0)
    o_b = _gated_rmsnorm(o_b, z.reshape(Bsz, L, HB, DV), p['norm_delta'][l]).reshape(Bsz, L, B_V).astype(x.dtype)
    mix = (jax.nn.sigmoid(gate_a) * (o_a @ p['w_branch_a'][l])
           + jax.nn.sigmoid(gate_b) * (o_b @ p['w_branch_b'][l]))
    x = x + _rms_norm(mix @ p['w_out'][l], p['norm_post_mix'][l])
    h = _rms_norm(x, p['norm_pre_ffn'][l])
    gt, up = jnp.split(h @ p['w_ffn_in'][l], 2, axis=-1)
    x = x + _rms_norm((jax.nn.silu(gt) * up) @ p['w_ffn_out'][l], p['norm_post_ffn'][l])
    return x, kv_new, S.astype(x.dtype), conv_new

def _trunk(x, kv_caches, S_cache, conv_cache, p, is_prompt):
    Bsz = x.shape[0]
    kv_out = [[] for _ in range(N_GROUPS)]
    S_out, conv_out = [], []
    for l in range(DEPTH):
        if is_prompt:
            bufs = [jnp.zeros((Bsz, 0, 2, H_G, HD_A), x.dtype) for _ in range(N_GROUPS)]
            S0 = jnp.zeros((Bsz, HB, DK, DV), jnp.float32)
            cb = jnp.zeros((Bsz, CONV_W - 1, CONV_DIM), x.dtype)
        else:
            bufs = [kv_caches[g][l] for g in range(N_GROUPS)]
            S0 = S_cache[l]
            cb = conv_cache[l]
        x, kv_new, S, cb_new = _layer(x, bufs, S0, cb, p, l)
        for g, (win, _) in enumerate(GROUPS):
            rows = kv_new[g]
            kv_out[g].append(rows[:, -min(win, rows.shape[1]):] if is_prompt else rows)
        S_out.append(S)
        conv_out.append(cb_new)
    return (x, jnp.stack(kv_out[0]), jnp.stack(kv_out[1]), jnp.stack(kv_out[2]),
            jnp.stack(S_out), jnp.stack(conv_out))

def setup_inputs(seed: int = 0) -> dict:
    key = jax.random.key(seed)
    ks = jax.random.split(key, 22)
    f32 = jnp.float32
    nrm = lambda k, shape: jax.random.normal(k, shape, f32)
    lens = [min(w, PAST_LEN) for (w, _) in GROUPS]
    dt = jnp.exp(jax.random.uniform(ks[12], (DEPTH, HB), f32, math.log(1e-3), math.log(1e-1)))
    return {
        'x_prompt': nrm(ks[0], (BATCH, SEQ, D_MODEL)),
        'x_sample': nrm(ks[1], (DEC_BATCH, DEC_SEQ, D_MODEL)),
        'cache_kv_w128': nrm(ks[2], (DEPTH, DEC_BATCH, lens[0], 2, H_G, HD_A)),
        'cache_kv_w512': nrm(ks[3], (DEPTH, DEC_BATCH, lens[1], 2, H_G, HD_A)),
        'cache_kv_w2048': nrm(ks[4], (DEPTH, DEC_BATCH, lens[2], 2, H_G, HD_A)),
        'state_delta': 0.1 * nrm(ks[5], (DEPTH, DEC_BATCH, HB, DK, DV)),
        'state_conv': nrm(ks[6], (DEPTH, DEC_BATCH, CONV_W - 1, CONV_DIM)),
        'rel_bias': 0.5 * nrm(ks[7], (N_BUCKETS, N_GROUPS * H_G)),
        'norm_pre_mix': 1.0 + 0.02 * nrm(ks[8], (DEPTH, D_MODEL)),
        'w_in': nrm(ks[9], (DEPTH, D_MODEL, N_IN)) * D_MODEL ** -0.5,
        'conv_w': nrm(ks[10], (DEPTH, CONV_W, CONV_DIM)) * CONV_W ** -0.5,
        'a_log': jnp.log(jax.random.uniform(ks[11], (DEPTH, HB), f32, 1.0, 16.0)),
        'dt_bias': dt + jnp.log(-jnp.expm1(-dt)),
        'norm_delta': 1.0 + 0.02 * nrm(ks[13], (DEPTH, DV)),
        'w_branch_a': nrm(ks[14], (DEPTH, A_OUT, D_MODEL)) * A_OUT ** -0.5,
        'w_branch_b': nrm(ks[15], (DEPTH, B_V, D_MODEL)) * B_V ** -0.5,
        'w_out': nrm(ks[16], (DEPTH, D_MODEL, D_MODEL)) * D_MODEL ** -0.5,
        'norm_post_mix': 1.0 + 0.02 * nrm(ks[17], (DEPTH, D_MODEL)),
        'norm_pre_ffn': 1.0 + 0.02 * nrm(ks[18], (DEPTH, D_MODEL)),
        'w_ffn_in': nrm(ks[19], (DEPTH, D_MODEL, 2 * D_FF)) * D_MODEL ** -0.5,
        'w_ffn_out': nrm(ks[20], (DEPTH, D_FF, D_MODEL)) * D_FF ** -0.5,
        'norm_post_ffn': 1.0 + 0.02 * nrm(ks[21], (DEPTH, D_MODEL)),
    }

def reference(x_prompt, x_sample, cache_kv_w128, cache_kv_w512, cache_kv_w2048, state_delta, state_conv,
              rel_bias, norm_pre_mix, w_in, conv_w, a_log, dt_bias, norm_delta, w_branch_a, w_branch_b,
              w_out, norm_post_mix, norm_pre_ffn, w_ffn_in, w_ffn_out, norm_post_ffn):
    p = {'rel_bias': rel_bias, 'norm_pre_mix': norm_pre_mix, 'w_in': w_in, 'conv_w': conv_w,
         'a_log': a_log, 'dt_bias': dt_bias, 'norm_delta': norm_delta, 'w_branch_a': w_branch_a,
         'w_branch_b': w_branch_b, 'w_out': w_out, 'norm_post_mix': norm_post_mix,
         'norm_pre_ffn': norm_pre_ffn, 'w_ffn_in': w_ffn_in, 'w_ffn_out': w_ffn_out,
         'norm_post_ffn': norm_post_ffn}
    y_prompt, kv128_p, kv512_p, kv2048_p, delta_p, conv_p = _trunk(
        x_prompt, None, None, None, p, True)
    y_sample, kv128_s, kv512_s, kv2048_s, delta_s, conv_s = _trunk(
        x_sample, (cache_kv_w128, cache_kv_w512, cache_kv_w2048), state_delta, state_conv, p, False)
    return (y_prompt, y_sample, kv128_p, kv512_p, kv2048_p, delta_p, conv_p,
            kv128_s, kv512_s, kv2048_s, delta_s, conv_s)


_drawn_inputs = setup_inputs


def setup_inputs(seed=0):
    import zlib

    import numpy as np

    out = dict(_drawn_inputs(seed))
    spreads = {}
    factors = {'norm_delta': 3.446, 'norm_post_mix': 3.485, 'norm_pre_ffn': 3.508, 'norm_post_ffn': 4.752}
    for name, (base, spread) in spreads.items():
        noise = np.random.default_rng([zlib.crc32(name.encode()), seed]).standard_normal(out[name].shape)
        drawn = base * np.exp(spread * noise) if base else spread * noise
        out[name] = __import__('jax').numpy.asarray(drawn.astype(out[name].dtype))
    for name, factor in factors.items():
        out[name] = (out[name] * factor).astype(out[name].dtype)
    return out
```

```python
import math
from contextlib import ExitStack

import concourse.bass as bass
from concourse import mybir

FP = mybir.dt.float32
FR = mybir.dt.float32r
ACT = mybir.ActivationFunctionType
ALU = mybir.AluOpType
AX = mybir.AxisListType

P = 128
D = 1024
L = 1024
NS = 8
NT = L // P
T = L + NS
KT = D // P
NG, HA, HD = 3, 4, 64
HB, DK = 8, 128
C = 64
FF = 2816
FT = FF // P
G3 = T // 3
A_QKV = NG * 3 * HA * HD
CONV0 = A_QKV
Z0 = CONV0 + 3 * D
BA0 = Z0 + D
GATE0 = BA0 + 2 * HB
EPS = 1e-6
CS = 28


class Event:

    def __init__(self, sem, per=1):
        self.sem, self.per = sem, per

    def at(self, turn, step=1):
        return turn * self.per + step


def build(nc, a, o):
    ctx = ExitStack()
    with ctx:
        n_names = [0]

        def sb(stack, name, shape, dt=FP):
            return stack.enter_context(nc.sbuf_tensor(name, shape, dt))

        def pb(stack, name):
            return stack.enter_context(nc.psum_tensor(name, [P, 512], FP))

        live = []

        def sem(name):
            n_names[0] += 1
            live.append(nc.alloc_semaphore(name=f"{name}_{n_names[0]}"))
            return live[-1]

        def clear_semaphores():
            with nc.Block() as block:
                @block.gpsimd
                def _(pool):
                    for x in live:
                        pool.sem_clear(x)
            for x in live:
                nc.release_semaphore(x)
            live.clear()

        def ev(name, per=1):
            return Event(sem(name), per)

        def dram(name, shape):
            return nc.dram_tensor(name, shape, FP, kind="Internal").ap()

        gate_scr = dram("gate_scr", (2, HB, P, T))
        ob_scr = dram("ob_scr", (HB, P, T))
        x1_scr = dram("x1_scr", (T, D))
        mix_scr = dram("mix_scr", (KT, P, T))
        act_scr = dram("act_scr", (FT, P, T))
        bias_scr = dram("bias_scr", (NG * HA, P, 3 * P))

        early = ExitStack()
        xT_hi = sb(early, "xT_hi", [P, KT, T], FR)
        xT_lo = sb(early, "xT_lo", [P, KT, T], FR)
        ident = sb(early, "ident", [P, P])
        norm_dv = sb(early, "norm_dv", [P, 1])
        conv_new = sb(early, "conv_new", [P, 24, 3 + NS])
        ident_ones = sb(early, "ones", [P, P])
        oaT = sb(early, "oaT", [P, 2, T])
        banks = [pb(ctx, f"bank{i}") for i in range(8)]

        def norm_block(row_tile, weight, tag=""):
            with ExitStack() as s:
                rows = [sb(s, f"rows{j}{tag}", [P, D]) for j in range(2)]
                normed = [sb(s, f"normed{j}{tag}", [P, D]) for j in range(2)]
                sq = sb(s, f"sq{tag}", [P, D])
                wrow = sb(s, f"wrow{tag}", [P, D])
                stat = sb(s, f"stat{tag}", [P, 2, 4])
                loaded = [ev("loaded"), ev("loaded")]
                const, squared = sem("const"), [ev("squared", 3), ev("squared", 3)]
                made = [ev("made"), ev("made")]
                turned = [ev("turned", 2), ev("turned", 2)]
                hi_done = [ev("hi", 2), ev("hi", 2)]
                lo_done = [ev("lo", 2), ev("lo", 2)]
                eps = sem("eps")

                def both(step):
                    def run(eng):
                        with eng.Fori(0, NT // 2) as i:
                            for j in range(2):
                                step(eng, i, j, P, i * 2 + j)
                        step(eng, NT // 2, 0, NS, NT)
                    return run

                def load(sp, i, j, n, t):
                    sp.wait_ge(made[j].sem, made[j].at(i, 0))
                    sp.dma_start(rows[j][:n], row_tile(t)).then_inc(loaded[j].sem, 16)

                def stats(act, i, j, n, t):
                    act.wait_ge(loaded[j].sem, i * 16 + 16)
                    if j == 0:
                        act.wait_ge(squared[1].sem, squared[1].at(i, 0))
                    else:
                        act.wait_ge(squared[0].sem, squared[0].at(i, 3))
                    nc.scalar.activation(sq[:n], rows[j][:n], ACT.Square,
                                         accum_out=stat[:n, j, 0:1]).then_inc(squared[j].sem, 1)
                    act.wait_ge(squared[j].sem, squared[j].at(i, 1))
                    nc.scalar.activation(stat[:n, j, 1:2], stat[:n, j, 0:1], ACT.Ln, scale=1.0 / D,
                                         bias=stat[:n, 0, 3:4]).then_inc(squared[j].sem, 1)
                    act.wait_ge(squared[j].sem, squared[j].at(i, 2))
                    nc.scalar.activation(stat[:n, j, 2:3], stat[:n, j, 1:2], ACT.Exp,
                                         scale=-0.5).then_inc(squared[j].sem, 1)
                    for half in range(2):
                        act.wait_ge(turned[j].sem, turned[j].at(i, half + 1))
                        src = banks[2 * j + half][:].rearrange("p (k c) -> p k c", k=4)[:, :, :n]
                        nc.scalar.activation(
                            xT_hi[:, 4 * half:4 * half + 4, bass.ds(t * P, n)], src,
                            ACT.Copy).then_inc(hi_done[j].sem, 1)

                def center(v, i, j, n, t):
                    v.wait_ge(squared[j].sem, squared[j].at(i, 3))
                    v.wait_ge(turned[j].sem, turned[j].at(i, 0))
                    nc.vector.scalar_tensor_tensor(normed[j][:n], rows[j][:n], stat[:n, j, 2:3],
                                                   wrow[:n], ALU.mult, ALU.mult).then_inc(made[j].sem, 1)
                    for half in range(2):
                        v.wait_ge(hi_done[j].sem, hi_done[j].at(i, half + 1))
                        src = banks[2 * j + half][:].rearrange("p (k c) -> p k c", k=4)[:, :, :n]
                        at = (slice(None), slice(4 * half, 4 * half + 4), bass.ds(t * P, n))
                        nc.vector.tensor_tensor(xT_lo[at], src, xT_hi[at].bitcast(FP),
                                                ALU.subtract).then_inc(lo_done[j].sem, 1)

                def turn(pe, i, j, n, t):
                    pe.wait_ge(made[j].sem, made[j].at(i))
                    for half in range(2):
                        pe.wait_ge(lo_done[j].sem, lo_done[j].at(i, half - 1) if half else lo_done[j].at(i, 0))
                        for k in range(4):
                            last = nc.tensor.transpose(banks[2 * j + half][:, k * P:k * P + n],
                                                       normed[j][:n, (4 * half + k) * P:(4 * half + k + 1) * P],
                                                       ident[:n, :n])
                        last.then_inc(turned[j].sem, 1)

                with nc.Block() as block:
                    @block.sync
                    def _(sp):
                        sp.dma_start(wrow[:], weight.partition_broadcast(P)).then_inc(const, 16)
                        sp.dma_start(ident[:], a["c_ident"]).then_inc(const, 16)
                        both(load)(sp)

                    @block.vector
                    def _(v):
                        nc.vector.memset(stat[:, :, 3:4], EPS).then_inc(eps, 1)
                        v.wait_ge(const, 32)
                        both(center)(v)

                    @block.scalar
                    def _(act):
                        nc.scalar.preload_act_table_set("natural_log_exp_and_others")
                        act.wait_ge(eps, 1)
                        both(stats)(act)

                    @block.tensor
                    def _(pe):
                        pe.wait_ge(const, 32)
                        both(turn)(pe)

        xs = a["x_sample"].rearrange("b s d -> (b s) d")
        xp = a["x_prompt"][0]
        norm_block(lambda t: xs if isinstance(t, int) and t == NT else xp[bass.ds(t * P, P)],
                   a["norm_pre_mix"][0])

        beta_all = sb(early, "beta_all", [P, HB, NT + 1])
        gcol = sb(early, "gcol", [P, HB, NT + 1])
        stage_g = sb(early, "stage_g", [P, 4, HB, NT])
        eglast = sb(early, "eglast", [P, HB, 2 * NT])
        eg_s = sb(early, "eg_s", [P, 2, HB, NS])
        ob_s = sb(early, "ob_s", [P, HB, NS])
        samp = sb(early, "samp", [P, 4, HB, NS])

        def split_weights_hi(act, dst, src):
            return nc.scalar.activation(dst, src, ACT.Copy)

        def split_lo(v, dst, src, hi):
            return nc.vector.tensor_tensor(dst, src, hi.bitcast(FP), ALU.subtract)

        def passes(out, stat_hi, stat_lo, mov_hi, mov_lo, start, stop):
            nc.tensor.matmul(out, stat_lo, mov_hi, start=start, stop=False)
            nc.tensor.matmul(out, stat_hi, mov_lo, start=False, stop=False)
            return nc.tensor.matmul(out, stat_hi, mov_hi, start=False, stop=stop)

        w_in = a["w_in"][0].rearrange("(k p) n -> p k n", p=P)

        def beta_decay_block():
            with ExitStack() as s, nc.Block() as block:
                raw = sb(s, "ba_raw", [P, KT, 16]); hi = sb(s, "ba_hi", [P, KT, 16], FR)
                lo = sb(s, "ba_lo", [P, KT, 16], FR)
                ch = sb(s, "ba_ch", [16, T]); tok = sb(s, "ba_tok", [P, NT + 1, 16])
                par = sb(s, "ba_par", [P, 2, HB]); ea = sb(s, "ba_ea", [P, HB])
                x = sb(s, "ba_x", [P, 16, NT + 1]); t = sb(s, "ba_t", [P, 16, NT + 1])
                lnb = sb(s, "ba_lnb", [P, HB, NT + 1])
                tri = sb(s, "ba_tri", [P, 4, P])
                half = sb(s, "ba_half", [P, 2, HB, NT])
                gls = sb(s, "ba_gls", [P, HB, NT])
                smp = sb(s, "ba_smp", [NS, 2, HB, NS])
                ld, sp_hi, sp_lo, pj, evac, tr, tk = (sem(n) for n in ("ld", "shi", "slo", "pj", "ev", "tr", "tk"))
                dv, ac, mm = sem("dve_step"), sem("act_step"), sem("mm")

                @block.sync
                def _(sp):
                    with nc.allow_non_contiguous_dma(reason="16 columns"):
                        sp.dma_start(raw[:], w_in[:, :, BA0:BA0 + 16]).then_inc(ld, 16)
                    sp.dma_start(par[:, 0], a["a_log"][0].partition_broadcast(P)).then_inc(ld, 16)
                    sp.dma_start(par[:, 1], a["dt_bias"][0].partition_broadcast(P)).then_inc(ld, 16)
                    sp.dma_start(tri[:], a["c_sums"].rearrange("n p f -> p n f")).then_inc(ld, 16)

                @block.tensor
                def _(pe):
                    pe.wait_ge(sp_lo, 1)
                    for g in range(3):
                        c = slice(g * G3, (g + 1) * G3)
                        for k in range(KT):
                            last = passes(banks[g][:16, :G3], hi[:, k], lo[:, k], xT_hi[:, k, c], xT_lo[:, k, c],
                                          k == 0, k == KT - 1)
                        last.then_inc(pj, 1)
                    pe.wait_ge(evac, 3)
                    for i in range(NT + 1):
                        n = P if i < NT else NS
                        last = nc.tensor.transpose(banks[3][:n, 16 * i:16 * i + 16], ch[:, i * P:i * P + n],
                                                   ident[:16, :16])
                    last.then_inc(tr, 1)
                    pe.wait_ge(dv, 8)
                    g_in = gcol[:, :, :NT]
                    for i in range(4):
                        last = nc.tensor.matmul(banks[4][:, 64 * i:64 * i + 64], tri[:, i], g_in, start=True, stop=True)
                    pe.wait_ge(dv, 9)
                    last = nc.tensor.matmul(banks[5][:, :2 * HB * NS], ident_ones[:NS],
                                            smp[:].rearrange("b n h c -> b (n h c)"), start=True, stop=True)
                    last.then_inc(mm, 1)

                @block.scalar
                def _(act):
                    nc.scalar.preload_act_table_set("natural_log_exp_and_others")
                    act.wait_ge(ld, 64)
                    split_weights_hi(act, hi[:], raw[:]).then_inc(sp_hi, 1)
                    nc.scalar.activation(ea[:], par[:, 0], ACT.Exp).then_inc(ac, 1)
                    for g in range(3):
                        act.wait_ge(pj, g + 1)
                        nc.scalar.activation(ch[:, g * G3:(g + 1) * G3], banks[g][:16, :G3], ACT.Copy).then_inc(evac, 1)
                    act.wait_ge(dv, 3)
                    nc.scalar.activation(t[:], t[:], ACT.Exp).then_inc(ac, 1)
                    act.wait_ge(ac, 2)
                    nc.scalar.activation(t[:], t[:], ACT.Ln, bias=1.0).then_inc(ac, 1)
                    act.wait_ge(dv, 6)
                    nc.scalar.activation(beta_all[:], lnb[:], ACT.Exp).then_inc(ac, 1)
                    act.wait_ge(dv, 12)
                    nc.scalar.activation(eglast[:].rearrange("p h (c r) -> p r h c", r=2), half[:], ACT.Exp).then_inc(ac, 1)
                    act.wait_ge(mm, 1)
                    nc.scalar.activation(eg_s[:].rearrange("p n h b -> p (n h b)"), banks[5][:, :2 * HB * NS], ACT.Copy).then_inc(ac, 1)
                    act.wait_ge(ac, 6)
                    nc.scalar.activation(eg_s[:, 0], eg_s[:, 0], ACT.Exp).then_inc(ac, 1)

                @block.vector
                def _(v):
                    v.wait_ge(sp_hi, 1)
                    split_lo(v, lo[:], raw[:], hi[:]).then_inc(sp_lo, 1)
                    nc.vector.memset(x[:], 0.0).then_inc(dv, 1)
                    v.wait_ge(dv, 1)
                    v.wait_ge(tr, 1)
                    src = banks[3][:, :16 * NT].rearrange("p (i c) -> p c i", c=16)
                    nc.vector.tensor_copy(x[:, :, :NT], src)
                    nc.vector.tensor_copy(x[:NS, :, NT], banks[3][:NS, 16 * NT:16 * NT + 16]).then_inc(dv, 1)
                    v.wait_ge(dv, 2)
                    nc.vector.tensor_scalar(x[:, :HB], x[:, :HB], -1.0, None, ALU.mult)
                    nc.vector.tensor_tensor(x[:, HB:], x[:, HB:], par[:, 1].unsqueeze(2).to_broadcast([P, HB, NT + 1]),
                                            ALU.add).then_inc(tk, 1)
                    v.wait_ge(tk, 1)
                    nc.vector.scalar_tensor_tensor(t[:], x[:], -1.0, x[:], ALU.mult, ALU.min).then_inc(dv, 1)
                    v.wait_ge(dv, 3)
                    nc.vector.tensor_scalar(x[:], x[:], 0.0, None, ALU.max).then_inc(dv, 1)
                    v.wait_ge(dv, 4)
                    v.wait_ge(ac, 3)
                    nc.vector.tensor_tensor(x[:], x[:], t[:], ALU.add).then_inc(dv, 1)
                    v.wait_ge(dv, 5)
                    nc.vector.tensor_scalar(lnb[:], x[:, :HB], -1.0, None, ALU.mult).then_inc(dv, 1)
                    nc.vector.tensor_scalar(ea[:], ea[:], -1.0, None, ALU.mult).then_inc(dv, 1)
                    v.wait_ge(dv, 7)
                    nc.vector.tensor_tensor(gcol[:], x[:, HB:], ea[:].unsqueeze(2).to_broadcast([P, HB, NT + 1]),
                                            ALU.mult).then_inc(dv, 1)
                    v.wait_ge(dv, 8)
                    v.wait_ge(ac, 4)
                    eye = ident[:NS, :NS].unsqueeze(1).to_broadcast([NS, HB, NS])
                    nc.vector.tensor_tensor(smp[:, 0], gcol[:NS, :, NT:].to_broadcast([NS, HB, NS]), eye, ALU.mult)
                    nc.vector.tensor_tensor(smp[:, 1], beta_all[:NS, :, NT:].to_broadcast([NS, HB, NS]), eye,
                                            ALU.mult).then_inc(dv, 1)
                    v.wait_ge(mm, 1)
                    part = [banks[4][:, 64 * i:64 * i + 64].rearrange("p (h c) -> p h c", h=HB) for i in range(4)]
                    nc.vector.tensor_copy(stage_g[:, 1], part[0]).then_inc(dv, 1)
                    nc.vector.tensor_copy(half[:, 0], part[2])
                    nc.vector.tensor_copy(half[:, 1], part[3])
                    nc.vector.tensor_copy(gls[:], part[1]).then_inc(dv, 1)
                    v.wait_ge(dv, 11)
                    nc.vector.tensor_scalar(stage_g[:, 2], stage_g[:, 1], -0.5 * math.log(DK), None, ALU.add).then_inc(dv, 1)
                    nc.vector.tensor_tensor(stage_g[:, 0], stage_g[:, 1], lnb[:, :, :NT], ALU.add)
                    nc.vector.tensor_tensor(stage_g[:, 3], gls[:], stage_g[:, 1], ALU.subtract).then_inc(dv, 1)
                    v.wait_ge(dv, 13)
                    nc.vector.tensor_scalar(stage_g[:, 1], stage_g[:, 1], -1.0, None, ALU.mult).then_inc(dv, 1)

        with nc.Block() as block:
            ones_set = sem("ones_set")

            @block.vector
            def _(v):
                nc.vector.memset(ident_ones[:], 1.0).then_inc(ones_set, 1)
                v.wait_ge(ones_set, 1)
        beta_decay_block()

        att_scr = dram("att_scr", (NG, L, HA * (HD + 2)))
        HS = HD + 2
        att_stack = ExitStack()
        kv_s = sb(att_stack, "kv_s", [NS, NG, 2 * HA * HD])
        qT_s = sb(att_stack, "qT_s", [P, NG, 2, NS])

        def key_rows(g, t):
            if g == 0:
                return lambda x: x[:, t * P:(t + 1) * P]
            if g == 1:
                c, n = t // 2, t % 2
                return lambda x: x[:, c + 4 * P * n:c + 4 * P * n + 4 * P - 3:4]
            return lambda x: x[:, t:L - NT + t + 1:NT]

        def dram_rows(g, t, x):
            if g == 0:
                return x[t * P:(t + 1) * P]
            if g == 1:
                c, n = t // 2, t % 2
                return x[c + 4 * P * n:c + 4 * P * n + 4 * P - 3:4]
            return x[t::NT]

        def bias_block():
            with ExitStack() as s, nc.Block() as block:
                table = sb(s, "bias_table", [33, NG * HA]); onehot = sb(s, "onehot", [33, NG, 3 * P])
                wide = sb(s, "bias_wide", [33, NG * HA, P])
                res = sb(s, "bias_res", [P, NG * HA, 3 * P])
                ld, spread, mm, cp, out = sem("b_ld"), sem("b_spread"), sem("b_mm"), sem("b_cp"), sem("b_out")

                @block.sync
                def _(sp):
                    sp.dma_start(table[:32], a["rel_bias"]).then_inc(ld, 16)
                    sp.dma_start(table[32:33], a["c_ones"][0:1, :NG * HA]).then_inc(ld, 16)
                    sp.dma_start(onehot[:], a["c_onehot"]).then_inc(ld, 16)
                    sp.wait_ge(cp, NG * HA)
                    sp.dma_start(bias_scr.rearrange("n p x -> p n x"), res[:]).then_inc(out, 16)
                    sp.wait_ge(out, 16)

                @block.tensor
                def _(pe):
                    pe.wait_ge(spread, 1)
                    for n in range(NG * HA):
                        if n >= 8:
                            pe.wait_ge(cp, n - 7)
                        nc.tensor.matmul(banks[n % 8][:, :3 * P], wide[:, n], onehot[:, n // HA],
                                         start=True, stop=True).then_inc(mm, 1)

                @block.vector
                def _(v):
                    v.wait_ge(ld, 48)
                    nc.vector.tensor_copy(wide[:], table[:].unsqueeze(2).to_broadcast([33, NG * HA, P])).then_inc(spread, 1)
                    for n in range(NG * HA):
                        v.wait_ge(mm, n + 1)
                        nc.vector.tensor_copy(res[:, n], banks[n % 8][:, :3 * P]).then_inc(cp, 1)

        def attention_block():
            with ExitStack() as s, nc.Block() as block:
                W5 = 2 * HA * HD
                raw = sb(s, "a_raw", [P, KT, W5])
                whi = sb(s, "a_hi", [P, KT, W5], FR); wlo = sb(s, "a_lo", [P, KT, W5], FR)
                kv = sb(s, "a_kv", [P, NT, W5]); kT = sb(s, "a_kT", [P, 2, L]); qT = sb(s, "a_qT", [P, 2, T])
                bias = sb(s, "a_bias", [P, HA, 2 * P])
                sc = [sb(s, f"a_sc{j}", [P, HA, 2 * P]) for j in range(2)]
                pT = [sb(s, f"a_pT{j}", [P, HA * 2 * P]) for j in range(2)]
                os_ = sb(s, "a_os", [P, NT, HA, HS]); nm = sb(s, "a_nm", [P, 2, HA])
                N = dict(w_ld=2, w_hi=2, w_lo=2, kvd=9, kv_ev=9, ktd=8, kt_ev=8, qd=6, q_ev=6, qs=1,
                         sd=8, st=16, mx=8, nm=8, ex=8, ptd=8, pt_ev=8, pv=8, oe=8)
                E = {k: ev("a_" + k, n) for k, n in N.items()}
                bld, kvo, oso = sem("a_bld"), sem("a_kvo"), sem("a_oso")
                KVO = (2, 2 + 5, 2 + 5 + 9)

                def inc(ins, name):
                    ins.then_inc(E[name].sem, 16 if name == "w_ld" else 1)

                def wt(eng, name, g, k):
                    n = E[name].at(g, k) * (16 if name == "w_ld" else 1)
                    if n > 0:
                        eng.wait_ge(E[name].sem, n)

                def blocks(g, t):
                    if g == 2 or (g == 0 and t == 0) or (g == 1 and t % 2 == 0):
                        return [t]
                    return [t - 1, t]

                @block.sync
                def _(sp):
                    for g in range(NG):
                        c0 = g * 3 * HA * HD
                        wt(sp, "w_lo", g, 0)
                        inc(sp.dma_start(raw[:], w_in[:, :, c0 + HA * HD:c0 + 3 * HA * HD]), "w_ld")
                        wt(sp, "w_lo", g, 1)
                        wt(sp, "w_ld", g, 1)
                        inc(sp.dma_start(raw[:, :, :HA * HD], w_in[:, :, c0:c0 + HA * HD]), "w_ld")
                        wt(sp, "st", g, 0)
                        sp.dma_start(bias[:], bass.AP(bias_scr.tensor, g * HA * P * 3 * P + P - 1,
                                                      [[3 * P - 1, P], [P * 3 * P, HA], [1, 2 * P]])).then_inc(bld, 16)
                        out = o[("kv128_p", "kv512_p", "kv2048_p")[g]][0, 0].rearrange("r s h d -> r (s h d)")
                        for t in range(NT + 1):
                            if t == NT:
                                wt(sp, "kv_ev", g, t + 1)
                                dst = o[("kv128_s", "kv512_s", "kv2048_s")[g]][0, :, 0].rearrange("b s h d -> b (s h d)")
                                sp.dma_start(dst, kv_s[:, g]).then_inc(kvo, 16)
                            elif g == 2:
                                wt(sp, "kv_ev", g, t + 1)
                                sp.dma_start(dram_rows(2, t, out), kv[:, t]).then_inc(kvo, 16)
                            elif (g == 0 and t == NT - 1):
                                wt(sp, "kv_ev", g, t + 1)
                                sp.dma_start(out, kv[:, t]).then_inc(kvo, 16)
                            elif g == 1 and t % 2:
                                wt(sp, "kv_ev", g, t + 1)
                                sp.dma_start(out[t // 2::4], kv[:, t]).then_inc(kvo, 16)
                        for t in range(NT):
                            wt(sp, "oe", g, t + 1)
                            wt(sp, "ex", g, t + 1)
                            sp.dma_start(dram_rows(g, t, att_scr[g]),
                                         os_[:, t].rearrange("p h w -> p (h w)")).then_inc(oso, 16)
                    sp.wait_ge(oso, NG * NT * 16)
                    sp.wait_ge(kvo, KVO[2] * 16)

                @block.tensor
                def _(pe):
                    def turn_keys(g, t):
                        wt(pe, "kv_ev", g, t + 1)
                        wt(pe, "kt_ev", g, max(t - 1, 0))
                        for m in range(2):
                            last = nc.tensor.transpose(banks[2 + t % 2][:, m * P:(m + 1) * P],
                                                       kv[:, t, m * P:(m + 1) * P], ident[:])
                        inc(last, "ktd")

                    def scores(g, t):
                        wt(pe, "st", g, 2 * max(t - 1, 0))
                        ks = blocks(g, t)
                        sel = key_rows(g, t)
                        for h in range(HA):
                            m, r = h // 2, 64 * (h % 2)
                            dst = banks[(0, 6)[t % 2] + h % 2][:, m * 256 + 256 - P * len(ks):m * 256 + 256]
                            last = nc.tensor.matmul(dst, sel(qT[r:r + 64, m]), kT[r:r + 64, m, ks[0] * P:(t + 1) * P],
                                                    start=True, stop=True)
                        inc(last, "sd")

                    for g in range(NG):
                        wt(pe, "w_lo", g, 1)
                        wt(pe, "st", g, 0); wt(pe, "pt_ev", g, 0); wt(pe, "oe", g, 0)
                        for t in range(NT + 1):
                            n = P if t < NT else NS
                            wt(pe, "kv_ev", g, max(t - 1, 0))
                            sel = key_rows(g, t) if t < NT else (lambda x: x[:, L:])
                            for k in range(KT):
                                last = passes(banks[t % 2][:n, :], sel(xT_hi[:, k]), sel(xT_lo[:, k]), whi[:, k],
                                              wlo[:, k], k == 0, k == KT - 1)
                            inc(last, "kvd")
                            if t:
                                turn_keys(g, t - 1)
                        wt(pe, "w_lo", g, 2)
                        for m in range(2):
                            for c in range(3):
                                n = 3 * m + c
                                if n >= 3:
                                    wt(pe, "q_ev", g, n - 2)
                                cs = slice(c * G3, (c + 1) * G3)
                                for k in range(KT):
                                    last = passes(banks[4 + c][:, :G3], whi[:, k, m * P:(m + 1) * P],
                                                  wlo[:, k, m * P:(m + 1) * P], xT_hi[:, k, cs], xT_lo[:, k, cs],
                                                  k == 0, k == KT - 1)
                                inc(last, "qd")
                        wt(pe, "q_ev", g, 6); wt(pe, "kt_ev", g, 8); wt(pe, "kv_ev", g, 9)
                        scores(g, 0)
                        for t in range(NT):
                            if t + 1 < NT:
                                scores(g, t + 1)
                            nk = len(blocks(g, t))
                            wt(pe, "ex", g, t + 1)
                            wt(pe, "pt_ev", g, t)
                            for h in range(HA):
                                for b in range(nk):
                                    x = (h * nk + b) * P
                                    last = nc.tensor.transpose(banks[2 + x // 512][:, x % 512:x % 512 + P],
                                                               sc[t % 2][:, h, (2 - nk + b) * P:(3 - nk + b) * P], ident[:])
                            inc(last, "ptd")
                            wt(pe, "pt_ev", g, t + 1)
                            wt(pe, "oe", g, max(t - 1, 0))
                            for h in range(HA):
                                for b, kt_ in enumerate(blocks(g, t)):
                                    last = nc.tensor.matmul(banks[4 + t % 2][:, h * P:(h + 1) * P],
                                                            pT[t % 2][:, (h * nk + b) * P:(h * nk + b + 1) * P],
                                                            kv[:, kt_, 256 + (h // 2) * P:256 + (h // 2 + 1) * P],
                                                            start=(b == 0), stop=(b == nk - 1))
                            inc(last, "pv")

                @block.scalar
                def _(act):
                    nc.scalar.preload_act_table_set("natural_log_exp_and_others")

                    def exps(g, t):
                        wt(act, "nm", g, t + 1)
                        if t == 0 and g:
                            act.wait_ge(oso, g * NT * 16)
                        nk = len(blocks(g, t))
                        for h in range(HA):
                            x = sc[t % 2][:, h, (2 - nk) * P:]
                            last = nc.scalar.activation(x, x, ACT.Exp, bias=nm[:, t % 2, h:h + 1],
                                                        accum_out=os_[:, t, h, HD:HD + 1])
                        inc(last, "ex")

                    for g in range(NG):
                        wt(act, "w_ld", g, 1)
                        wt(act, "qd", g, 0)
                        inc(nc.scalar.activation(whi[:], raw[:], ACT.Copy), "w_hi")
                        if g:
                            act.wait_ge(kvo, KVO[g - 1] * 16)
                        wt(act, "pv", g, 0)
                        for t in range(NT + 1):
                            wt(act, "kvd", g, t + 1)
                            dst = kv[:, t] if t < NT else kv_s[:, g]
                            inc(nc.scalar.activation(dst, banks[t % 2][:P if t < NT else NS, :], ACT.Copy), "kv_ev")
                        wt(act, "w_ld", g, 2)
                        inc(nc.scalar.activation(whi[:, :, :256], raw[:, :, :256], ACT.Copy), "w_hi")
                        for n in range(6):
                            wt(act, "qd", g, n + 1)
                            c = n % 3
                            inc(nc.scalar.activation(qT[:, n // 3, c * G3:(c + 1) * G3], banks[4 + c][:, :G3],
                                                     ACT.Copy), "q_ev")
                        wt(act, "q_ev", g, 6)
                        inc(nc.scalar.activation(qT_s[:, g], qT[:, :, L:], ACT.Copy), "qs")
                        exps(g, 0)
                        for t in range(NT):
                            if t + 1 < NT:
                                exps(g, t + 1)
                            wt(act, "ptd", g, t + 1)
                            nk = len(blocks(g, t))
                            wt(act, "pv", g, max(t - 1, 0))
                            for b in range(nk):
                                last = nc.scalar.activation(pT[t % 2][:, 512 * b:512 * b + 512], banks[2 + b][:], ACT.Copy)
                            inc(last, "pt_ev")

                @block.vector
                def _(v):
                    def out_copy(g, t):
                        wt(v, "pv", g, t + 1)
                        for e in range(2):
                            src = banks[4 + t % 2][:].rearrange("p (m e w) -> p m e w", m=2, e=2)[:, :, e, 64 * e:64 * e + 64]
                            last = nc.vector.tensor_copy(os_[:, t, e::2, :HD], src)
                        inc(last, "oe")

                    for g in range(NG):
                        wt(v, "w_hi", g, 1)
                        inc(split_lo(v, wlo[:], raw[:], whi[:]), "w_lo")
                        for t in range(NT):
                            wt(v, "ktd", g, t + 1)
                            if t == 0:
                                wt(v, "sd", g, 0)
                            inc(nc.vector.tensor_copy(kT[:, :, t * P:(t + 1) * P],
                                                      banks[2 + t % 2][:, :256].rearrange("p (m c) -> p m c", m=2)), "kt_ev")
                        wt(v, "w_hi", g, 2)
                        inc(split_lo(v, wlo[:, :, :256], raw[:, :, :256], whi[:, :, :256]), "w_lo")
                        v.wait_ge(bld, (g + 1) * 16)
                        if g:
                            v.wait_ge(oso, g * NT * 16)
                        for t in range(NT):
                            nk = len(blocks(g, t))
                            ks = slice((2 - nk) * P, 2 * P)
                            wt(v, "sd", g, t + 1)
                            wt(v, "ptd", g, max(t - 1, 0))
                            for e in range(2):
                                src = banks[(0, 6)[t % 2] + e][:].rearrange("p (h k) -> p h k", h=2)[:, :, ks]
                                inc(nc.vector.scalar_tensor_tensor(sc[t % 2][:, e::2, ks], src, HD ** -0.5,
                                                                   bias[:, e::2, ks], ALU.mult, ALU.add), "st")
                            wt(v, "st", g, 2 * t + 2)
                            inc(nc.vector.reduce_max(os_[:, t, :, HD + 1], sc[t % 2][:, :, ks], AX.X), "mx")
                            wt(v, "mx", g, t + 1)
                            wt(v, "ex", g, max(t - 1, 0))
                            inc(nc.vector.tensor_scalar(nm[:, t % 2], os_[:, t, :, HD + 1], -1.0, None, ALU.mult), "nm")
                            if t:
                                out_copy(g, t - 1)
                        out_copy(g, NT - 1)

        def merge_block():
            with ExitStack() as s, nc.Block() as block:
                x = sb(s, "m_x", [P, NG, NT, HA, HS]); top = sb(s, "m_top", [P, NT, HA])
                f = sb(s, "m_f", [P, NG, NT, HA]); z = sb(s, "m_z", [P, NG, NT, HA])
                y = sb(s, "m_y", [P, NT, HA, HD]); y2 = sb(s, "m_y2", [P, NT, HA, HD])
                ld, dv, ac, tr = sem("m_ld"), sem("m_dv"), sem("m_ac"), sem("m_tr")

                @block.sync
                def _(sp):
                    for g in range(NG):
                        sp.dma_start(x[:, g].rearrange("p t h w -> p t (h w)"),
                                     att_scr[g].rearrange("(t p) w -> p t w", p=P)).then_inc(ld, 16)

                @block.scalar
                def _(act):
                    act.wait_ge(dv, 3)
                    nc.scalar.activation(f[:], f[:], ACT.Exp).then_inc(ac, 1)

                @block.tensor
                def _(pe):
                    pe.wait_ge(dv, 12)
                    for m in range(2):
                        for t in range(NT):
                            last = nc.tensor.transpose(banks[2 * m + t // 4][:, (t % 4) * P:(t % 4 + 1) * P],
                                                       y[:, t, 2 * m:2 * m + 2].rearrange("p h d -> p (h d)"), ident[:])
                    last.then_inc(tr, 1)

                @block.vector
                def _(v):
                    n = [0]

                    def step(ins):
                        n[0] += 1
                        ins.then_inc(dv, 1)
                        v.wait_ge(dv, n[0])
                    v.wait_ge(ld, 48)
                    mx = x[:, :, :, :, HD + 1]
                    step(nc.vector.tensor_tensor(top[:], mx[:, 0], mx[:, 1], ALU.max))
                    step(nc.vector.tensor_tensor(top[:], top[:], mx[:, 2], ALU.max))
                    for g in range(NG):
                        last = nc.vector.tensor_tensor(f[:, g], mx[:, g], top[:], ALU.subtract)
                    step(last)
                    v.wait_ge(ac, 1)
                    for g in range(NG):
                        last = nc.vector.tensor_tensor(z[:, g], f[:, g], x[:, g, :, :, HD], ALU.mult)
                    step(last)
                    step(nc.vector.tensor_tensor(top[:], z[:, 0], z[:, 1], ALU.add))
                    step(nc.vector.tensor_tensor(top[:], top[:], z[:, 2], ALU.add))
                    step(nc.vector.reciprocal(top[:], top[:]))
                    for g in range(NG):
                        last = nc.vector.tensor_tensor(f[:, g], f[:, g], top[:], ALU.mult)
                    step(last)
                    F4 = [P, NT * HA, HD]

                    def part(g):
                        return (x[:, g, :, :, :HD].rearrange("p t h d -> p (t h) d"),
                                f[:, g].rearrange("p t h -> p (t h)").unsqueeze(2).to_broadcast(F4))
                    yy, yy2 = y[:].rearrange("p t h d -> p (t h) d"), y2[:].rearrange("p t h d -> p (t h) d")
                    nc.vector.tensor_tensor(yy, *part(0), ALU.mult)
                    step(nc.vector.tensor_tensor(yy2, *part(1), ALU.mult))
                    step(nc.vector.tensor_tensor(yy, yy, yy2, ALU.add))
                    step(nc.vector.tensor_tensor(yy2, *part(2), ALU.mult))
                    step(nc.vector.tensor_tensor(yy, yy, yy2, ALU.add))
                    v.wait_ge(tr, 1)
                    for m in range(2):
                        for b in range(2):
                            last = nc.vector.tensor_copy(oaT[:, m, 512 * b:512 * b + 512], banks[2 * m + b][:])
                    step(last)


        def load_constants_block():
            with ExitStack() as s, nc.Block() as block:
                rows = sb(s, "cs_rows", [CS, 3 * D])
                ld, tr, ev_ = sem("cs_ld"), sem("cs_tr"), sem("cs_ev")

                @block.sync
                def _(sp):
                    sp.dma_start(rows[:24], a["state_conv"][0].rearrange("b j c -> (b j) c")).then_inc(ld, 16)
                    sp.dma_start(rows[24:28], a["conv_w"][0]).then_inc(ld, 16)
                    sp.dma_start(mask[:], a["c_mask"].rearrange("n p f -> p n f")).then_inc(ld, 16)
                    sp.dma_start(level_mask[:], a["c_levels"].rearrange("n p f -> p n f")).then_inc(ld, 16)
                    sp.dma_start(norm_dv[:], a["norm_delta"].rearrange("o d -> d o")).then_inc(ld, 16)

                @block.tensor
                def _(pe):
                    pe.wait_ge(ld, 80)
                    for k in range(24):
                        last = nc.tensor.transpose(banks[k // 12][:, (k % 12) * CS:(k % 12 + 1) * CS],
                                                   rows[:, k * P:(k + 1) * P], ident[:CS, :CS])
                    last.then_inc(tr, 1)

                @block.vector
                def _(v):
                    nc.vector.memset(eps_col[:], EPS).then_inc(ev_, 1)
                    for m in range(3):
                        nc.vector.memset(pre[m][:, 0:3], 0.0)
                    v.wait_ge(tr, 1)
                    for b in range(2):
                        src = banks[b][:, :12 * CS].rearrange("p (k c) -> p k c", c=CS)
                        nc.vector.tensor_copy(conv_state[:, 12 * b:12 * b + 12], src[:, :, :24])
                        last = nc.vector.tensor_scalar(conv_wt[:, 12 * b:12 * b + 12], src[:, :, 24:], 0.5, None,
                                                       ALU.mult)
                    last.then_inc(ev_, 1)
                    v.wait_ge(ev_, 2)

        class Chain:

            def __init__(self, eng, sem_):
                self.eng, self.sem, self.n, self.marks = eng, sem_, 0, {}

            def step(self, ins, mark=None):
                self.n += 1
                ins.then_inc(self.sem, 1)
                self.eng.wait_ge(self.sem, self.n)
                if mark:
                    self.marks[mark] = self.n

            def reached(self, eng, mark):
                eng.wait_ge(self.sem, self.marks[mark])

        def sample_attention_block():
            with ExitStack() as s, nc.Block() as block:
                W5 = 2 * HA * HD
                R = NS * HA
                NKEY = (P, P, 64)
                cache = [sb(s, f"sa_cache{g}", [P, NS, W5]) for g in range(NG)]
                q_row = sb(s, "sa_qrow", [NS, NG, HA * HD]); sel = sb(s, "sa_sel", [NS, NS, P])
                prod = sb(s, "sa_prod", [P, NS, HA * HD]); sc = sb(s, "sa_sc", [P, NG, R])
                S = sb(s, "sa_S", [R, NG, P + 1]); bias = sb(s, "sa_bias", [R, NG, P + 1])
                self_r = sb(s, "sa_selfr", [R, NG]); pself_r = sb(s, "sa_pselfr", [R, NG])
                table = sb(s, "sa_table", [33, NG * HA]); trep = sb(s, "sa_trep", [33, NG, NS, HA])
                onehot = sb(s, "sa_onehot", [33, NG, P + 1])
                sprod = sb(s, "sa_sprod", [NS, NG, HA * HD]); self_ = sb(s, "sa_self", [NS, NG, HA])
                pself = sb(s, "sa_pself", [NS, NG, HA]); pd = sb(s, "sa_pd", [NS, NG, 2, NS, 2])
                st = sb(s, "sa_st", [R, 4]); pT = sb(s, "sa_pT", [P, NG, R])
                cache_ld = [sem("sa_cache_ld") for _ in range(NG)]
                const_ld, moved, expd = sem("sa_const"), sem("sa_moved"), sem("sa_exp")
                q_turned, q_spread, sc_turned = sem("sa_qt"), sem("sa_qs"), sem("sa_sct")
                p_turned, pv_done, dve = sem("sa_pt"), sem("sa_pv"), sem("sa_dve")
                scr = dram("sa_scr", (2, NS, NG, HA))
                ch = [None]

                @block.vector
                def _(v):
                    c = ch[0] = Chain(v, dve)
                    v.wait_ge(const_ld, 48)
                    c.step(nc.vector.tensor_copy(sel[:], ident[:NS, :NS].unsqueeze(2).to_broadcast([NS, NS, P])))
                    for g in range(NG):
                        last = nc.vector.tensor_copy(trep[:, g], table[:, g * HA:(g + 1) * HA].unsqueeze(1)
                                                     .to_broadcast([33, NS, HA]))
                    c.step(last)
                    v.wait_ge(q_turned, 1)
                    nc.vector.memset(S[:], 0.0)
                    nc.vector.tensor_copy(q_row[:, 0:2].rearrange("p g c -> p (g c)"), banks[0][:NS, :])
                    c.step(nc.vector.tensor_copy(q_row[:, 2], banks[1][:NS, :256]), "q_row")
                    c.step(nc.vector.tensor_tensor(sprod[:], q_row[:], kv_s[:, :, :256], ALU.mult))
                    c.step(nc.vector.reduce_sum(self_[:].rearrange("p g h -> p (g h)"),
                                                sprod[:].rearrange("p g (h d) -> p (g h) d", h=HA), AX.X), "self")
                    for g in range(NG):
                        k = NKEY[g]
                        v.wait_ge(cache_ld[g], 16)
                        v.wait_ge(q_spread, 1 + g)
                        for b in range(4):
                            last = nc.vector.tensor_tensor(
                                prod[:k, 2 * b:2 * b + 2], cache[g][:k, 2 * b:2 * b + 2, :256],
                                banks[2 + b][:k, :].rearrange("p (b c) -> p b c", b=2), ALU.mult)
                        c.step(last, f"prod{g}")
                        c.step(nc.vector.reduce_sum(sc[:k, g], prod[:k].rearrange("p b (h d) -> p (b h) d", h=HA),
                                                    AX.X), "sc")
                    v.wait_ge(sc_turned, 1)
                    v.wait_ge(moved, 16 * 9)
                    for g in range(NG):
                        nc.vector.tensor_copy(S[:, g, :NKEY[g]], banks[6][:R, g * P:g * P + NKEY[g]])
                        nc.vector.tensor_copy(S[:, g, P:], self_r[:, g:g + 1])
                        last = nc.vector.tensor_copy(bias[:, g], banks[7][:R, g * 132:g * 132 + P + 1])
                    c.step(last)
                    c.step(nc.vector.scalar_tensor_tensor(S[:], S[:], HD ** -0.5, bias[:], ALU.mult, ALU.add))
                    c.step(nc.vector.reduce_max(st[:, 0:1], S[:].rearrange("p g c -> p (g c)"), AX.X))
                    c.step(nc.vector.tensor_scalar(st[:, 1:2], st[:, 0:1], -1.0, None, ALU.mult), "max")
                    v.wait_ge(expd, 1)
                    c.step(nc.vector.reciprocal(st[:, 3:4], st[:, 2:3]))
                    c.step(nc.vector.tensor_scalar(S[:], S[:], st[:, 3:4], None, ALU.mult))
                    c.step(nc.vector.tensor_copy(pself_r[:], S[:, :, P]), "probs")
                    v.wait_ge(p_turned, 1)
                    for g in range(NG):
                        last = nc.vector.tensor_copy(pT[:NKEY[g], g], banks[0][:NKEY[g], g * R:(g + 1) * R])
                    c.step(last)
                    v.wait_ge(moved, 16 * 18)
                    for g in range(NG):
                        for m in range(2):
                            src = pself[:, g, 2 * m:2 * m + 2].unsqueeze(1).to_broadcast([NS, NS, 2])
                            last = nc.vector.tensor_tensor(pd[:, g, m], src, ident[:NS, :NS].unsqueeze(2)
                                                           .to_broadcast([NS, NS, 2]), ALU.mult)
                    c.step(last, "pT")
                    v.wait_ge(pv_done, 1)
                    for m in range(2):
                        for e in range(2):
                            rows = slice(64 * e, 64 * e + 64)
                            src = banks[1 + m][rows, :2 * NS].rearrange("p (b e) -> p b e", e=2)[:, :, e]
                            last = nc.vector.tensor_copy(oaT[rows, m, L:], src)
                    c.step(last)
                c = ch[0]

                @block.sync
                def _(sp):
                    sp.dma_start(table[:32], a["rel_bias"]).then_inc(const_ld, 16)
                    sp.dma_start(table[32:33], a["c_ones"][0:1, :NG * HA]).then_inc(const_ld, 16)
                    sp.dma_start(onehot[:], a["c_onehot_s"]).then_inc(const_ld, 16)
                    for g, (name, step) in enumerate((("cache_kv_w128", 1), ("cache_kv_w512", 4), ("cache_kv_w2048", 16))):
                        rows = a[name][0].rearrange("b r s h d -> r b (s h d)")[::step]
                        sp.dma_start(cache[g][:NKEY[g]], rows).then_inc(cache_ld[g], 16)
                    with nc.allow_non_contiguous_dma(reason="96 scores change partitions"):
                        c.reached(sp, "self")
                        sp.dma_start(scr[0], self_[:]).then_inc(moved, 16)
                        sp.wait_ge(moved, 16)
                        for b in range(NS):
                            sp.dma_start(self_r[HA * b:HA * b + HA], scr[0, b].rearrange("g h -> h g")).then_inc(moved, 16)
                        sp.wait_ge(moved, 16 * 9)
                        c.reached(sp, "probs")
                        for b in range(NS):
                            sp.dma_start(scr[1, b].rearrange("g h -> h g"), pself_r[HA * b:HA * b + HA]).then_inc(moved, 16)
                        sp.wait_ge(moved, 16 * 17)
                        sp.dma_start(pself[:], scr[1]).then_inc(moved, 16)
                        sp.wait_ge(moved, 16 * 18)

                @block.tensor
                def _(pe):
                    for g in range(NG):
                        for m in range(2):
                            x = (2 * g + m) * P
                            last = nc.tensor.transpose(banks[x // 512][:NS, x % 512:x % 512 + P], qT_s[:, g, m], ident[:])
                    last.then_inc(q_turned, 1)
                    c.reached(pe, "q_row")
                    for g in range(NG):
                        if g:
                            c.reached(pe, f"prod{g - 1}")
                        for b in range(NS):
                            last = nc.tensor.matmul(banks[2 + b // 2][:, (b % 2) * 256:(b % 2) * 256 + 256], sel[:, b],
                                                    q_row[:, g], start=True, stop=True)
                        last.then_inc(q_spread, 1)
                    c.reached(pe, "sc")
                    for g in range(NG):
                        k = NKEY[g]
                        nc.tensor.transpose(banks[6][:R, g * P:g * P + k], sc[:k, g], ident[:k, :k])
                        last = nc.tensor.matmul(banks[7][:R, g * 132:g * 132 + P + 1],
                                                trep[:, g].rearrange("p b h -> p (b h)"), onehot[:, g],
                                                start=True, stop=True)
                    last.then_inc(sc_turned, 1)
                    c.reached(pe, "probs")
                    for g in range(NG):
                        k = NKEY[g]
                        last = nc.tensor.transpose(banks[0][:k, g * R:(g + 1) * R], S[:, g, :k], ident[:R, :R])
                    last.then_inc(p_turned, 1)
                    c.reached(pe, "pT")
                    for m in range(2):
                        bank = banks[1 + m]
                        for g in range(NG):
                            nc.tensor.matmul(bank[:, :2 * NS], kv_s[:, g, 256 + m * P:256 + (m + 1) * P],
                                             pd[:, g, m].rearrange("p b e -> p (b e)"), start=(g == 0), stop=False,
                                             skip_group_check=True)
                        for b in range(NS):
                            for g in range(NG):
                                k = NKEY[g]
                                last = nc.tensor.matmul(bank[:, 2 * b:2 * b + 2],
                                                        cache[g][:k, b, 256 + m * P:256 + (m + 1) * P],
                                                        pT[:k, g, HA * b + 2 * m:HA * b + 2 * m + 2], start=False,
                                                        stop=(b == NS - 1 and g == NG - 1), skip_group_check=True)
                    last.then_inc(pv_done, 1)

                @block.scalar
                def _(act):
                    nc.scalar.preload_act_table_set("natural_log_exp_and_others")
                    c.reached(act, "max")
                    nc.scalar.activation(S[:], S[:], ACT.Exp, bias=st[:, 1:2], accum_out=st[:, 2:3]).then_inc(expd, 1)

        def sample_delta_block():
            with ExitStack() as s, nc.Block() as block:
                U = HB * NS
                S0 = sb(s, "sd_S0", [P, U, P])
                sq = sb(s, "sd_sq", [P, 2, U]); r = sb(s, "sd_r", [P, 2, U]); kq = sb(s, "sd_kq", [P, U, 2])
                skq = sb(s, "sd_skq", [P, U, 2]); qk = sb(s, "sd_qk", [P, U]); vn = sb(s, "sd_vn", [P, U])
                ov = sb(s, "sd_ov", [P, U]); t1 = sb(s, "sd_t1", [P, U]); k_c = sb(s, "sd_kc", [P, U])
                vn_r = sb(s, "sd_vnr", [U, P]); k_r = sb(s, "sd_kr", [U, P])
                blk = [sb(s, f"sd_blk{j}", [U, 4, P]) for j in range(2)]
                ld, norm_mm, lnexp, sk_mm, qk_mm, turned, rms_mm, rank1, blkd, st_out = (
                    sem("sd_" + x) for x in ("ld", "norm", "lnexp", "sk", "qk", "tr", "rms", "r1", "blk", "out"))
                dve = sem("sd_dve")
                add_done = sem("sd_add")
                eps2 = sb(s, "sd_eps", [P, 1])
                ch = [None]
                flat = lambda x: x.rearrange("p h b -> p (h b)")
                q_, k_, v_, z_ = (flat(samp[:, n]) for n in range(4))
                eg, beta = flat(eg_s[:, 0]), flat(eg_s[:, 1])

                @block.vector
                def _(v):
                    c = ch[0] = Chain(v, dve)
                    nc.vector.memset(eps2[:], EPS)
                    nc.vector.tensor_tensor(sq[:, 0], q_, q_, ALU.mult)
                    c.step(nc.vector.tensor_tensor(sq[:, 1], k_, k_, ALU.mult), "sq")
                    v.wait_ge(lnexp, 2)
                    nc.vector.scalar_tensor_tensor(kq[:, :, 1], q_, DK ** -0.5, r[:, 0], ALU.mult, ALU.mult)
                    nc.vector.tensor_tensor(k_c[:], k_, r[:, 1], ALU.mult)
                    c.step(nc.vector.tensor_tensor(kq[:, :, 0], k_, r[:, 1], ALU.mult), "kq")
                    c.step(nc.vector.tensor_tensor(sq[:, 0], kq[:, :, 0], kq[:, :, 1], ALU.mult), "qk")
                    v.wait_ge(qk_mm, 1)
                    nc.vector.tensor_copy(qk[:], banks[1][:, :U])
                    v.wait_ge(sk_mm, 1)
                    c.step(nc.vector.tensor_copy(skq[:].rearrange("p u e -> p (u e)"), banks[2][:, :2 * U]))
                    c.step(nc.vector.tensor_tensor(t1[:], skq[:, :, 0], eg, ALU.mult))
                    c.step(nc.vector.tensor_tensor(t1[:], v_, t1[:], ALU.subtract))
                    c.step(nc.vector.tensor_tensor(vn[:], t1[:], beta, ALU.mult), "vn")
                    nc.vector.tensor_tensor(ov[:], skq[:, :, 1], eg, ALU.mult)
                    c.step(nc.vector.tensor_tensor(t1[:], vn[:], qk[:], ALU.mult))
                    c.step(nc.vector.tensor_tensor(ov[:], ov[:], t1[:], ALU.add))
                    c.step(nc.vector.tensor_tensor(sq[:, 1], ov[:], ov[:], ALU.mult), "o2")
                    v.wait_ge(lnexp, 4)
                    c.step(nc.vector.tensor_tensor(ov[:], ov[:], r[:, 0], ALU.mult))
                    c.step(nc.vector.scalar_tensor_tensor(flat(ob_s[:]), ov[:], norm_dv[:], z_, ALU.mult, ALU.mult))
                    v.wait_ge(turned, 1)
                    nc.vector.tensor_copy(vn_r[:], banks[3][:U, :P])
                    c.step(nc.vector.tensor_copy(k_r[:], banks[3][:U, P:2 * P]))
                    v.wait_ge(sk_mm, 1)
                    c.step(nc.vector.tensor_tensor(S0[:], S0[:], eg.unsqueeze(2).to_broadcast([P, U, P]), ALU.mult))
                    for n in range(U // 4):
                        if n >= 2:
                            v.wait_ge(rank1, n - 1)
                        nc.vector.tensor_tensor(blk[n % 2][:], vn_r[:].unsqueeze(1).to_broadcast([U, 4, P]),
                                                ident[:U, 4 * n:4 * n + 4].unsqueeze(2).to_broadcast([U, 4, P]),
                                                ALU.mult).then_inc(blkd, 1)
                        if n:
                            v.wait_ge(rank1, n)
                            nc.vector.tensor_tensor(S0[:, 4 * n - 4:4 * n], S0[:, 4 * n - 4:4 * n],
                                                    banks[4 + (n - 1) % 2][:].rearrange("p (u c) -> p u c", u=4),
                                                    ALU.add).then_inc(add_done, 1)
                    n = U // 4
                    v.wait_ge(rank1, n)
                    nc.vector.tensor_tensor(S0[:, 4 * n - 4:4 * n], S0[:, 4 * n - 4:4 * n],
                                            banks[4 + (n - 1) % 2][:].rearrange("p (u c) -> p u c", u=4),
                                            ALU.add).then_inc(add_done, 1)
                c = ch[0]

                @block.sync
                def _(sp):
                    for h in range(HB):
                        sp.dma_start(S0[:, h * NS:(h + 1) * NS],
                                     a["state_delta"][0, :, h].rearrange("b k v -> k b v")).then_inc(ld, 16)
                    for h in range(HB):
                        sp.wait_ge(add_done, 2 * h + 2)
                        sp.dma_start(o["delta_s"][0, :, h].rearrange("b k v -> k b v"),
                                     S0[:, h * NS:(h + 1) * NS]).then_inc(st_out, 16)
                    sp.wait_ge(st_out, HB * 16)

                @block.tensor
                def _(pe):
                    c.reached(pe, "sq")
                    nc.tensor.matmul(banks[0][:, :2 * U], ident_ones[:], sq[:].rearrange("p n u -> p (n u)"),
                                     start=True, stop=True).then_inc(norm_mm, 1)
                    c.reached(pe, "kq")
                    c.reached(pe, "qk")
                    nc.tensor.matmul(banks[1][:, :U], ident_ones[:], sq[:, 0], start=True, stop=True).then_inc(qk_mm, 1)
                    pe.wait_ge(ld, HB * 16)
                    for u in range(U):
                        last = nc.tensor.matmul(banks[2][:, 2 * u:2 * u + 2], S0[:, u], kq[:, u], start=True, stop=True)
                    last.then_inc(sk_mm, 1)
                    c.reached(pe, "vn")
                    nc.tensor.transpose(banks[3][:U, :P], vn[:], ident[:])
                    nc.tensor.transpose(banks[3][:U, P:2 * P], k_c[:], ident[:]).then_inc(turned, 1)
                    c.reached(pe, "o2")
                    nc.tensor.matmul(banks[6][:, :U], ident_ones[:], sq[:, 1], start=True, stop=True).then_inc(rms_mm, 1)
                    for n in range(U // 4):
                        pe.wait_ge(blkd, n + 1)
                        if n >= 2:
                            pe.wait_ge(add_done, n - 1)
                        nc.tensor.matmul(banks[4 + n % 2][:], k_r[:], blk[n % 2][:].rearrange("p u c -> p (u c)"),
                                         start=True, stop=True).then_inc(rank1, 1)

                @block.scalar
                def _(act):
                    nc.scalar.preload_act_table_set("natural_log_exp_and_others")
                    act.wait_ge(norm_mm, 1)
                    nc.scalar.activation(r[:].rearrange("p n u -> p (n u)"), banks[0][:, :2 * U], ACT.Ln,
                                         bias=eps2[:]).then_inc(lnexp, 1)
                    act.wait_ge(lnexp, 1)
                    nc.scalar.activation(r[:], r[:], ACT.Exp, scale=-0.5).then_inc(lnexp, 1)
                    act.wait_ge(rms_mm, 1)
                    nc.scalar.activation(r[:, 0], banks[6][:, :U], ACT.Ln, scale=1.0 / DK, bias=eps2[:]).then_inc(lnexp, 1)
                    act.wait_ge(lnexp, 3)
                    nc.scalar.activation(r[:, 0], r[:, 0], ACT.Exp, scale=-0.5).then_inc(lnexp, 1)

        def conv_out_block():
            with ExitStack() as s, nc.Block() as block:
                rows = sb(s, "co_rows", [3 + NS, 3 * D])
                tr, cp, out = sem("co_tr"), sem("co_cp"), sem("co_out")

                @block.tensor
                def _(pe):
                    for k in range(24):
                        last = nc.tensor.transpose(banks[k // 4][:3 + NS, (k % 4) * P:(k % 4 + 1) * P], conv_new[:, k], ident[:])
                    last.then_inc(tr, 1)

                @block.vector
                def _(v):
                    v.wait_ge(tr, 1)
                    for b in range(6):
                        last = nc.vector.tensor_copy(rows[:, 512 * b:512 * b + 512], banks[b][:3 + NS, :])
                    last.then_inc(cp, 1)

                @block.sync
                def _(sp):
                    sp.dma_start(o["conv_s"][0, :, 0:2], a["state_conv"][0, :, 1:3]).then_inc(out, 16)
                    sp.wait_ge(cp, 1)
                    sp.dma_start(o["conv_p"][0, 0], rows[:3]).then_inc(out, 16)
                    sp.dma_start(o["conv_s"][0, :, 2], rows[3:]).then_inc(out, 16)
                    sp.wait_ge(out, 48)

        def pair_block(name, turns, nk_a, rhs_a, rhs_b, w_a, w_b, gates, out_scr):
            nk = nk_a + KT
            with ExitStack() as s, nc.Block() as block:
                raw = [sb(s, f"{name}_raw{j}", [P, nk, P]) for j in range(2)]
                hi = [sb(s, f"{name}_hi{j}", [P, nk, P], FR) for j in range(2)]
                lo = [sb(s, f"{name}_lo{j}", [P, nk, P], FR) for j in range(2)]
                ta = [sb(s, f"{name}_ta{j}", [P, T]) for j in range(2)]
                tb = [sb(s, f"{name}_tb{j}", [P, T]) for j in range(2)] if gates else ta
                y = [sb(s, f"{name}_y{j}", [P, T]) for j in range(2)]
                y2 = [sb(s, f"{name}_y2{j}", [P, T]) for j in range(2)] if gates else ta
                loaded = [sem("p_loaded") for _ in range(2)]; gate_in = [sem("p_gates") for _ in range(2)]
                hi_done = [sem("p_hi") for _ in range(2)]; lo_done = [sem("p_lo") for _ in range(2)]
                group = [sem("p_group") for _ in range(2)]; tile_done = [sem("p_tile") for _ in range(2)]
                drained = [sem("p_drained") for _ in range(3)]
                joined = [sem("p_joined") for _ in range(2)]; stored = [sem("p_stored") for _ in range(2)]
                tanh_done, silu_done = sem("p_tanh"), sem("p_silu")
                cs = [slice(c * G3, (c + 1) * G3) for c in range(3)]

                def turns_of(eng, split, join):
                    split(eng, 0, 0)
                    with eng.Fori(0, turns // 2 - 1) as i:
                        split(eng, i, 1)
                        join(eng, i, 0)
                        split(eng, i + 1, 0)
                        join(eng, i, 1)
                    split(eng, turns // 2 - 1, 1)
                    join(eng, turns // 2 - 1, 0)
                    join(eng, turns // 2 - 1, 1)

                def group_done(eng, i, j, c):
                    if c < 2:
                        eng.wait_ge(group[c], 2 * i + j + 1)
                    else:
                        eng.wait_ge(tile_done[j], i + 1)

                @block.sync
                def _(sp):
                    with sp.Fori(0, turns // 2) as i:
                        for j in range(2):
                            n = 2 * i + j
                            sp.wait_ge(lo_done[j], i)
                            sp.dma_start(raw[j][:, :nk_a], w_a(n)).then_inc(loaded[j], 16)
                            sp.dma_start(raw[j][:, nk_a:], w_b(n)).then_inc(loaded[j], 16)
                            if gates:
                                sp.wait_ge(joined[j], i)
                                for g, dst in ((0, ta[j]), (1, tb[j])):
                                    sp.dma_start(dst[:], gate_scr[g, bass.ds(n, 1)].rearrange("o p t -> (o p) t")
                                                 ).then_inc(gate_in[j], 16)

                @block.tensor
                def _(pe):
                    with pe.Fori(0, turns // 2) as i:
                        for j in range(2):
                            n = 2 * i + j
                            pe.wait_ge(lo_done[j], i + 1)
                            for c in range(3):
                                pe.wait_ge(drained[c], n)
                                for k in range(nk_a):
                                    passes(banks[c][:, :G3], hi[j][:, k], lo[j][:, k], rhs_a[0][:, k, cs[c]],
                                           rhs_a[1][:, k, cs[c]], k == 0, k == nk_a - 1)
                                for k in range(KT):
                                    last = passes(banks[3 + c][:, :G3], hi[j][:, nk_a + k], lo[j][:, nk_a + k],
                                                  rhs_b[0][:, k, cs[c]], rhs_b[1][:, k, cs[c]], k == 0, k == KT - 1)
                                last.then_inc(group[c] if c < 2 else tile_done[j], 1)

                def act_split(act, i, j):
                    act.wait_ge(tile_done[j], i)
                    act.wait_ge(loaded[j], 32 * i + 32)
                    nc.scalar.activation(hi[j][:], raw[j][:], ACT.Copy).then_inc(hi_done[j], 1)

                def act_join(act, i, j):
                    if not gates:
                        act.wait_ge(joined[j], i)
                        for c in range(3):
                            group_done(act, i, j, c)
                            nc.scalar.activation(ta[j][:, cs[c]], banks[c][:, :G3], ACT.Tanh, scale=0.5
                                                 ).then_inc(tanh_done, 1)
                    act.wait_ge(joined[j], i + 1)
                    act.dma_start(out_scr[bass.ds(2 * i + j, 1)].rearrange("o p t -> (o p) t"), y[j][:]
                                  ).then_inc(stored[j], 16)

                @block.scalar
                def _(act):
                    nc.scalar.preload_act_table(ACT.Tanh)
                    turns_of(act, act_split, act_join)
                    for j in range(2):
                        act.wait_ge(stored[j], 16 * (turns // 2))

                def dve_split(v, i, j):
                    v.wait_ge(hi_done[j], i + 1)
                    split_lo(v, lo[j][:], raw[j][:], hi[j][:]).then_inc(lo_done[j], 1)

                def dve_join(v, i, j):
                    n = 2 * i + j
                    v.wait_ge(stored[j], 16 * i)
                    if gates:
                        v.wait_ge(gate_in[j], 32 * i + 32)
                    for c in range(3):
                        if gates:
                            group_done(v, i, j, c)
                            nc.vector.tensor_tensor(y[j][:, cs[c]], banks[c][:, :G3], ta[j][:, cs[c]], ALU.mult)
                            nc.vector.tensor_tensor(y2[j][:, cs[c]], banks[3 + c][:, :G3], tb[j][:, cs[c]],
                                                    ALU.mult).then_inc(drained[c], 1)
                        else:
                            v.wait_ge(tanh_done, 3 * n + c + 1)
                            nc.vector.scalar_tensor_tensor(y[j][:, cs[c]], ta[j][:, cs[c]], 1.0, banks[c][:, :G3],
                                                           ALU.add, ALU.mult).then_inc(silu_done, 1)
                            v.wait_ge(silu_done, 3 * n + c + 1)
                            last = nc.vector.scalar_tensor_tensor(y[j][:, cs[c]], y[j][:, cs[c]], 0.5,
                                                                  banks[3 + c][:, :G3], ALU.mult, ALU.mult
                                                                  ).then_inc(drained[c], 1)
                    v.wait_ge(drained[2], n + 1)
                    if gates:
                        nc.vector.tensor_tensor(y[j][:], y[j][:], y2[j][:], ALU.add).then_inc(joined[j], 1)
                    else:
                        nc.vector.tensor_copy(mark[:], mark[:]).then_inc(joined[j], 1)

                mark = sb(s, f"{name}_mark", [P, 1])
                marked = sem("p_mark")

                @block.vector
                def _(v):
                    nc.vector.memset(mark[:], 0.0).then_inc(marked, 1)
                    v.wait_ge(marked, 1)
                    turns_of(v, dve_split, dve_join)

        def split_ob_block():
            with nc.Block() as block, ExitStack() as s:
                buf = [sb(s, f"so_buf{j}", [P, T]) for j in range(2)]
                ld = [sem("so_ld"), sem("so_ld")]
                hi_d, lo_d = sem("so_hi"), sem("so_lo")

                @block.sync
                def _(sp):
                    for h in range(HB):
                        if h >= 2:
                            sp.wait_ge(lo_d, h - 1)
                        sp.dma_start(buf[h % 2][:, :L], ob_scr[h, :, :L]).then_inc(ld[h % 2], 16)

                @block.scalar
                def _(act):
                    for h in range(HB):
                        act.wait_ge(ld[h % 2], 16 * (h // 2 + 1))
                        nc.scalar.activation(xT_hi[:, h, :L], buf[h % 2][:, :L], ACT.Copy)
                        nc.scalar.activation(xT_hi[:, h, L:], ob_s[:, h], ACT.Copy).then_inc(hi_d, 1)
                    nc.scalar.activation(oa_hi[:], oaT[:], ACT.Copy).then_inc(hi_d, 1)

                @block.vector
                def _(v):
                    for h in range(HB):
                        v.wait_ge(hi_d, h + 1)
                        split_lo(v, xT_lo[:, h, :L], buf[h % 2][:, :L], xT_hi[:, h, :L])
                        split_lo(v, xT_lo[:, h, L:], ob_s[:, h], xT_hi[:, h, L:]).then_inc(lo_d, 1)
                    v.wait_ge(hi_d, HB + 1)
                    split_lo(v, oa_lo[:], oaT[:], oa_hi[:]).then_inc(lo_d, 1)

        def row_block(name, src_scr, nk, chunks, weight, norm_w, resid, out):
            kc = nk // chunks
            kp = 1
            pieces = kc // kp
            with ExitStack() as s, nc.Block() as block:
                w_raw = [sb(s, f"{name}_wr{j}", [P, kp, D]) for j in range(2)]
                w_hi = sb(s, f"{name}_wh", [P, kc, D], FR); w_lo = sb(s, f"{name}_wl", [P, kc, D], FR)
                st_raw = [sb(s, f"{name}_sr{j}", [P, kc, P]) for j in range(2)]
                st_hi = [sb(s, f"{name}_sh{j}", [P, kc, P], FR) for j in range(2)]
                st_lo = [sb(s, f"{name}_sl{j}", [P, kc, P], FR) for j in range(2)]
                part = sb(s, f"{name}_part", [P, NT + 1, D]) if chunks > 1 else None
                y = [sb(s, f"{name}_y{j}", [P, D]) for j in range(2)]
                xr = [sb(s, f"{name}_x{j}", [P, D]) for j in range(2)]
                junk = sb(s, f"{name}_junk", [P, D])
                wrow = sb(s, f"{name}_wrow", [P, D]); stat = sb(s, f"{name}_stat", [P, 2, 4])
                w_ld = [sem("r_wld") for _ in range(2)]; w_hid, w_lod = sem("r_whi"), sem("r_wlo")
                st_ld = [sem("r_stld") for _ in range(2)]
                hi_d = [sem("r_hi") for _ in range(2)]; lo_d = [sem("r_lo") for _ in range(2)]
                prod = [sem("r_prod") for _ in range(2)]; drained = [sem("r_drained") for _ in range(2)]
                xld = [sem("r_xld") for _ in range(2)]; const = sem("r_const")
                normed = [sem("r_norm") for _ in range(2)]
                stats = [sem("r_stats") for _ in range(2)]; stored = [sem("r_stored") for _ in range(2)]
                eps_set = sem("r_eps")
                USES = (NT // 2 + 1, NT // 2)
                src = src_scr.rearrange("k p t -> p k t")
                wv = weight.rearrange("(k p) n -> p k n", p=P)

                def tiles_of(eng, q, stage, finish):
                    def run(i):
                        stage(eng, q, i, 1, P)
                        finish(eng, q, i, 0, P)
                        stage(eng, q, i + 1, 0, NS if isinstance(i, int) else P)
                        finish(eng, q, i, 1, P)
                    stage(eng, q, 0, 0, P)
                    with eng.Fori(0, NT // 2 - 1) as i:
                        run(i)
                    run(NT // 2 - 1)
                    finish(eng, q, NT // 2, 0, NS)

                def use(q, i, j):
                    return q * USES[j] + i

                def nothing(*_):
                    pass

                @block.sync
                def _(sp):
                    sp.dma_start(wrow[:], norm_w.partition_broadcast(P)).then_inc(const, 16)

                    def load(sp, q, i, j, n):
                        sp.wait_ge(lo_d[j], use(q, i, j))
                        sp.dma_start(st_raw[j][:, :, :n], src[:, q * kc:(q + 1) * kc, bass.ds((2 * i + j) * P, n)]
                                     ).then_inc(st_ld[j], 16)
                        if q == chunks - 1:
                            sp.wait_ge(normed[j], 2 * i)
                            sp.dma_start(xr[j][:n], resid(2 * i + j)).then_inc(xld[j], 16)

                    for q in range(chunks):
                        for n in range(pieces):
                            m = q * pieces + n
                            if m >= 2:
                                sp.wait_ge(w_lod, m - 1)
                            sp.dma_start(w_raw[m % 2][:], wv[:, q * kc + n * kp:q * kc + (n + 1) * kp]
                                         ).then_inc(w_ld[m % 2], 16)
                        tiles_of(sp, q, load, nothing)

                @block.tensor
                def _(pe):
                    def product(pe, q, i, j, n):
                        pe.wait_ge(lo_d[j], use(q, i, j) + 1)
                        pe.wait_ge(drained[j], use(q, i, j))
                        for half in range(2):
                            for k in range(kc):
                                c = slice(half * 512, half * 512 + 512)
                                last = passes(banks[2 * j + half][:n, :], st_hi[j][:, k, :n], st_lo[j][:, k, :n],
                                              w_hi[:, k, c], w_lo[:, k, c], k == 0, k == kc - 1)
                        last.then_inc(prod[j], 1)

                    for q in range(chunks):
                        pe.wait_ge(w_lod, (q + 1) * pieces)
                        tiles_of(pe, q, nothing, product)

                @block.scalar
                def _(act):
                    nc.scalar.preload_act_table_set("natural_log_exp_and_others")
                    act.wait_ge(eps_set, 1)

                    def stage(act, q, i, j, n):
                        act.wait_ge(st_ld[j], 16 * use(q, i, j) + 16)
                        act.wait_ge(prod[j], use(q, i, j))
                        nc.scalar.activation(st_hi[j][:, :, :n], st_raw[j][:, :, :n], ACT.Copy).then_inc(hi_d[j], 1)

                    def finish(act, q, i, j, n):
                        t = 2 * i + j
                        if chunks == 1 or q < chunks - 1:
                            act.wait_ge(prod[j], use(q, i, j) + 1)
                            if chunks == 1:
                                act.wait_ge(stored[j], 16 * i)
                            for half in range(2):
                                c = slice(half * 512, half * 512 + 512)
                                dst = y[j][:n, c] if chunks == 1 else part[:n, bass.ds(t, 1), c].rearrange("p o c -> p (o c)")
                                last = nc.scalar.activation(dst, banks[2 * j + half][:n, :], ACT.Copy)
                            last.then_inc(drained[j], 1)
                        if q == chunks - 1:
                            act.wait_ge(drained[j], use(q, i, j) + 1)
                            act.wait_ge(stats[j], 3 * i)
                            act.wait_ge(stats[1 - j], 3 * i + (3 if j else 0))
                            nc.scalar.activation(junk[:n], y[j][:n], ACT.Square,
                                                 accum_out=stat[:n, j, 0:1]).then_inc(stats[j], 1)
                            act.wait_ge(stats[j], 3 * i + 1)
                            nc.scalar.activation(stat[:n, j, 1:2], stat[:n, j, 0:1], ACT.Ln, scale=1.0 / D,
                                                 bias=stat[:n, j, 3:4]).then_inc(stats[j], 1)
                            act.wait_ge(stats[j], 3 * i + 2)
                            nc.scalar.activation(stat[:n, j, 2:3], stat[:n, j, 1:2], ACT.Exp,
                                                 scale=-0.5).then_inc(stats[j], 1)
                            act.wait_ge(normed[j], 2 * i + 2)
                            act.dma_start(out(t), y[j][:n]).then_inc(stored[j], 16)

                    for q in range(chunks):
                        for n in range(pieces):
                            m = q * pieces + n
                            act.wait_ge(w_ld[m % 2], 16 * (m // 2 + 1))
                            if q and n == 0:
                                for j in range(2):
                                    act.wait_ge(prod[j], q * USES[j])
                            nc.scalar.activation(w_hi[:, n * kp:(n + 1) * kp], w_raw[m % 2][:], ACT.Copy).then_inc(w_hid, 1)
                        tiles_of(act, q, stage, finish)
                    for j in range(2):
                        act.wait_ge(stored[j], 16 * USES[j])

                @block.vector
                def _(v):
                    nc.vector.memset(stat[:, :, 3:4], EPS).then_inc(eps_set, 1)
                    v.wait_ge(const, 16)

                    def stage(v, q, i, j, n):
                        v.wait_ge(hi_d[j], use(q, i, j) + 1)
                        split_lo(v, st_lo[j][:, :, :n], st_raw[j][:, :, :n], st_hi[j][:, :, :n]).then_inc(lo_d[j], 1)

                    def finish(v, q, i, j, n):
                        t = 2 * i + j
                        if q < chunks - 1:
                            return
                        if chunks > 1:
                            v.wait_ge(prod[j], use(q, i, j) + 1)
                            v.wait_ge(stored[j], 16 * i)
                            for half in range(2):
                                c = slice(half * 512, half * 512 + 512)
                                last = nc.vector.tensor_tensor(
                                    y[j][:n, c], banks[2 * j + half][:n, :],
                                    part[:n, bass.ds(t, 1), c].rearrange("p o c -> p (o c)"), ALU.add)
                            last.then_inc(drained[j], 1)
                        v.wait_ge(stats[j], 3 * i + 3)
                        nc.vector.scalar_tensor_tensor(y[j][:n], y[j][:n], stat[:n, j, 2:3], wrow[:n], ALU.mult,
                                                       ALU.mult).then_inc(normed[j], 1)
                        v.wait_ge(normed[j], 2 * i + 1)
                        v.wait_ge(xld[j], 16 * i + 16)
                        nc.vector.tensor_tensor(y[j][:n], y[j][:n], xr[j][:n], ALU.add).then_inc(normed[j], 1)

                    for q in range(chunks):
                        for n in range(pieces):
                            m = q * pieces + n
                            v.wait_ge(w_hid, m + 1)
                            split_lo(v, w_lo[:, n * kp:(n + 1) * kp], w_raw[m % 2][:], w_hi[:, n * kp:(n + 1) * kp]
                                     ).then_inc(w_lod, 1)
                        tiles_of(v, q, stage, finish)

        bias_block()
        attention_block()
        merge_block()
        sample_attention_block()
        clear_semaphores()
        att_stack.close()

        hs = ExitStack()
        mask = sb(hs, "mask", [P, 2, P]); level_mask = sb(hs, "level_mask", [P, 6, P])
        eps_col = sb(hs, "eps_col", [P, 1])
        conv_state = sb(hs, "conv_state", [P, 24, 24]); conv_wt = sb(hs, "conv_wt", [P, 24, 4])
        pre = [sb(hs, f"pre{m}", [P, 3 + T]) for m in range(3)]
        load_constants_block()

        def heads_block():
            s = hs
            w_raw = [sb(s, f"w_raw{j}", [P, KT, P]) for j in range(2)]
            w_hi = [sb(s, f"w_hi{j}", [P, KT, P], FR) for j in range(2)]
            w_lo = [sb(s, f"w_lo{j}", [P, KT, P], FR) for j in range(2)]
            qkv = [sb(s, f"qkv{m}", [P, T]) for m in range(3)]
            qc, kc, vc = qkv
            zs, tanh = sb(s, "zs", [P, T]), sb(s, "tanh", [P, T])
            F8 = [P, NT, P]
            k_tok = sb(s, "k_tok", F8); vb = sb(s, "vb", F8); kbe = sb(s, "kbe", F8); kdec = sb(s, "kdec", F8)
            ot = k_tok
            ea = sb(s, "ea", F8); eq = sb(s, "eq", F8)
            sqb = sb(s, "sqb", [P, 4, P])
            wq = sb(s, "wq", [P, NT, 4, C])
            col = sb(s, "col", [P, 10, NT])
            t_sb = [sb(s, f"t_sb{b}", [P, 4, P]) for b in range(2)]
            u_sb = [sb(s, f"u_sb{b}", [P, 4, P]) for b in range(2)]
            x_sb = [sb(s, f"x_sb{b}", [P, 4, P]) for b in range(2)]
            u_val = sb(s, "u_val", F8)
            qe = u_val[:].rearrange("p a b -> p (a b)")
            vnew = [sb(s, f"vnew{j}", [P, P]) for j in range(2)]
            state = [sb(s, f"state{j}", [P, P]) for j in range(2)]
            gate = [sb(s, f"gate{m}", [P, T]) for m in range(2)]
            wld = [sem("w_loaded") for j in range(2)]
            whi = [ev("w_hi", 3) for j in range(2)]
            wlo = [ev("w_lo", 3) for j in range(2)]
            tile_done = [ev("tile_done", 3) for j in range(2)]
            group = [ev("group", 6) for g in range(2)]
            evac = [ev("evac", 6) for g in range(3)]
            thalf = ev("thalf", 3); silu = ev("silu", 4); conv = ev("conv_taps", 3 * 7)
            zt, gs = ev("zt"), ev("gate_sig", 2)
            gout = sem("gate_out")
            D1 = dict(k_ev=2, q_ev=2, v_ev=2, turned=6, sq=2, dcol=1, drow=1, ssq=4, lncol=1, ecol=1,
                      cols=1, diag=2, rb=4, ea_m=2, eq_m=2, ea_x=2, eq_x=2, qe_x=2, qew=1, gram=4, an=2, pt=2,
                      xm=12, xs=12, ym=12, tc=12, uc=12, kbe_m=1, kdec_m=1, uw=4, u_ev=2, w_ev=2,
                      sm=17, m1=16, vn=16, m2=16, m3=16, o_ev=16, osq=1, oss=1, oln=2, on=1, ot_tr=2, ob=4,
                      samp_m=1, cn=3)
            E = {k: ev(k, n) for k, n in D1.items()}
            out_dma = sem("ob_out"); st_dma = sem("state_out")

            def inc(ins, name):
                ins.then_inc(E[name].sem, 1)

            def wt(eng, name, i, k):
                eng.wait_ge(E[name].sem, E[name].at(i, k))

            with nc.Block() as block:
                @block.sync
                def _(sp):
                    with sp.Fori(0, HB) as i:
                        for m in range(6):
                            j, u = m % 2, m // 2
                            sp.wait_ge(wlo[j].sem, wlo[j].at(i, u))
                            c0 = (CONV0 + m * D) if m < 4 else GATE0 + (m - 4) * D
                            sp.dma_start(w_raw[j][:], w_in[:, :, bass.ds(c0 + i * P, P)]).then_inc(wld[j], 16)

                @block.tensor
                def _(pe):
                    with pe.Fori(0, HB) as i:
                        for m in range(6):
                            j, u = m % 2, m // 2
                            pe.wait_ge(wlo[j].sem, wlo[j].at(i, u + 1))
                            for g in range(3):
                                pe.wait_ge(evac[g].sem, evac[g].at(i, m))
                                c = slice(g * G3, (g + 1) * G3)
                                for k in range(KT):
                                    last = passes(banks[g][:, :G3], w_hi[j][:, k], w_lo[j][:, k],
                                                  xT_hi[:, k, c], xT_lo[:, k, c], k == 0, k == KT - 1)
                                last.then_inc(group[g].sem if g < 2 else tile_done[j].sem, 1)
                        wt(pe, "ob", i, 0)
                        for n, (src, b, need) in enumerate(((1, 0, 2), (1, 1, None), (0, 0, 1), (0, 1, None),
                                                            (2, 0, 3), (2, 1, None))):
                            if need:
                                pe.wait_ge(silu.sem, silu.at(i, need))
                            if n == 5:
                                wt(pe, "k_ev", i, 1)
                            for p in range(4):
                                c = (4 * b + p) * P
                                last = nc.tensor.transpose(banks[(3, 4, 5, 6, 7, 3)[n]][:, p * P:(p + 1) * P],
                                                           qkv[src][:, c:c + P], ident[:])
                            inc(last, "turned")
                        wt(pe, "k_ev", i, 2); wt(pe, "q_ev", i, 2); wt(pe, "v_ev", i, 1)
                        for n in range(4):
                            wt(pe, "diag", i, n // 2 + 1)
                            src = (kbe if n < 2 else kdec)[:, 4 * (n % 2):4 * (n % 2) + 4]
                            inc(nc.tensor.matmul(banks[4 + n][:], ident_ones[:], src.rearrange("p a b -> p (a b)"),
                                                 start=True, stop=True), "rb")
                        wt(pe, "v_ev", i, 2)
                        for n in range(4):
                            if n == 1:
                                wt(pe, "ea_m", i, 1)
                            if n == 2:
                                wt(pe, "ea_m", i, 2)
                            if n == 3:
                                wt(pe, "eq_m", i, 1); wt(pe, "qe_x", i, 1)
                            for p in range(4):
                                c = slice((4 * (n % 2) + p) * P, (4 * (n % 2) + p + 1) * P)
                                last = nc.tensor.matmul(banks[3 + n][:, p * P:(p + 1) * P], kc[:, c],
                                                        (kc if n < 2 else qc)[:, c], start=True, stop=True)
                            inc(last, "gram")
                        wt(pe, "an", i, 2); wt(pe, "pt", i, 2); wt(pe, "eq_m", i, 2); wt(pe, "qe_x", i, 2)
                        tb, ub = (7, 4), (3, 5)
                        for b in range(2):
                            for bank in (tb[b], ub[b]):
                                for p in range(4):
                                    nc.tensor.matmul(banks[bank][:, p * P:(p + 1) * P], ident[:], ident[:],
                                                     start=(p == 0), stop=False, skip_group_check=True)
                        for lev in range(6):
                            for b in range(2):
                                n = 2 * lev + b
                                if lev:
                                    wt(pe, "tc", i, n - 1)
                                if n:
                                    wt(pe, "xs", i, n)
                                for p in range(4):
                                    last = nc.tensor.matmul(banks[6][:, p * P:(p + 1) * P], ea[:, 4 * b + p],
                                                            t_sb[b][:, p] if lev else ident[:], start=True, stop=True)
                                inc(last, "xm")
                            for b in range(2):
                                n = 2 * lev + b
                                wt(pe, "xs", i, n + 1)
                                if lev:
                                    wt(pe, "uc", i, n - 1)
                                for p in range(4):
                                    cs = slice(p * P, (p + 1) * P)
                                    u = u_sb[b][:, p] if lev else ident[:]
                                    nc.tensor.matmul(banks[tb[b]][:, cs], u, x_sb[b][:, p], start=False,
                                                     stop=False, skip_group_check=True)
                                    last = nc.tensor.matmul(banks[ub[b]][:, cs], x_sb[b][:, p], u, start=False,
                                                            stop=False, skip_group_check=True)
                                inc(last, "ym")
                        wt(pe, "tc", i, 12); wt(pe, "uc", i, 12); wt(pe, "kbe_m", i, 1)
                        for b in range(2):
                            for p in range(4):
                                last = nc.tensor.matmul(banks[6 + b][:, p * P:(p + 1) * P], u_sb[b][:, p],
                                                        vb[:, 4 * b + p], start=True, stop=True)
                            inc(last, "uw")
                            for p in range(4):
                                last = nc.tensor.matmul(banks[4 - b][:, p * P:(p + 1) * P], kbe[:, 4 * b + p],
                                                        u_sb[b][:, p], start=True, stop=True)
                            inc(last, "uw")
                        wt(pe, "u_ev", i, 2); wt(pe, "w_ev", i, 2); wt(pe, "qew", i, 1); wt(pe, "kdec_m", i, 1)
                        for c in range(16):
                            p, r = c // 2, c % 2
                            ob, db = banks[5 + c % 2], banks[3 + c % 2]
                            rows = slice(64 * r, 64 * r + 64)
                            other = slice(64 - 64 * r, 128 - 64 * r)
                            wt(pe, "sm", i, c + 1)
                            if c >= 2:
                                wt(pe, "o_ev", i, c - 1)
                            inc(nc.tensor.matmul(ob[:, :P], wq[:, p, 2 * r:2 * r + 2].rearrange("p a b -> p (a b)"),
                                                 state[c % 2][:], start=True, stop=False, skip_group_check=True), "m1")
                            wt(pe, "vn", i, c + 1)
                            inc(nc.tensor.matmul(db[:, :P], kdec[rows, p], vnew[c % 2][rows],
                                                 start=True, stop=True), "m3")
                            inc(nc.tensor.matmul(ob[other, :P], eq[rows, p, rows], vnew[c % 2][rows],
                                                 start=False, stop=True, skip_group_check=True), "m2")
                        wt(pe, "sm", i, 17)
                        wt(pe, "on", i, 1)
                        for b in range(2):
                            for p in range(4):
                                last = nc.tensor.transpose(banks[3 + b][:, p * P:(p + 1) * P], ot[:, 4 * b + p],
                                                           ident[:])
                            inc(last, "ot_tr")

                @block.scalar
                def _(act):
                    with act.Fori(0, HB) as i:
                        for m in range(6):
                            j, u = m % 2, m // 2
                            act.wait_ge(tile_done[j].sem, tile_done[j].at(i, u))
                            act.wait_ge(wld[j], (i * 3 + u + 1) * 16)
                            split_weights_hi(act, w_hi[j][:], w_raw[j][:]).then_inc(whi[j].sem, 1)
                            if m < 3:
                                act.wait_ge(conv.sem, conv.at(i, 0))
                                act.wait_ge(E["cn"].sem, E["cn"].at(i, 0))
                            elif m == 3:
                                act.wait_ge(out_dma, i * 16)
                            elif m == 4:
                                act.wait_ge(silu.sem, silu.at(i, 4))
                            if m == 5:
                                act.wait_ge(gs.sem, gs.at(i, 1))
                            for g in range(3):
                                if g < 2:
                                    act.wait_ge(group[g].sem, group[g].at(i, m + 1))
                                else:
                                    act.wait_ge(tile_done[j].sem, tile_done[j].at(i, u + 1))
                                c = slice(g * G3, (g + 1) * G3)
                                if m < 3:
                                    x = nc.scalar.activation(pre[m][:, 3 + g * G3:3 + (g + 1) * G3],
                                                             banks[g][:, :G3], ACT.Copy)
                                elif m == 3:
                                    x = nc.scalar.activation(zs[:, c], banks[g][:, :G3], ACT.Copy, scale=0.5)
                                else:
                                    x = nc.scalar.activation(tanh[:, c], banks[g][:, :G3], ACT.Tanh, scale=0.5)
                                x.then_inc(evac[g].sem, 1)
                            if m < 3:
                                act.wait_ge(evac[2].sem, evac[2].at(i, m + 1))
                                inc(nc.scalar.activation(conv_new[:, bass.ds(m * HB + i, 1)],
                                                         pre[m][:, L:L + 3 + NS].unsqueeze(1), ACT.Copy), "cn")
                                act.wait_ge(conv.sem, conv.at(i, 7 * m + 7))
                                if m == 0:
                                    act.wait_ge(gs.sem, gs.at(i, 0))
                                else:
                                    act.wait_ge(silu.sem, silu.at(i, m))
                                nc.scalar.activation(tanh[:], qkv[m][:], ACT.Tanh).then_inc(thalf.sem, 1)
                            elif m == 3:
                                act.wait_ge(evac[2].sem, evac[2].at(i, 4))
                                act.wait_ge(silu.sem, silu.at(i, 3))
                                nc.scalar.activation(tanh[:], zs[:], ACT.Tanh).then_inc(zt.sem, 1)
                        for b in range(2):
                            wt(act, "turned", i, b + 1)
                            inc(nc.scalar.activation(k_tok[:, 4 * b:4 * b + 4].rearrange("p a b -> p (a b)"),
                                                     banks[3 + b][:], ACT.Copy), "k_ev")
                        for b in range(2):
                            wt(act, "turned", i, b + 3)
                            if b == 0:
                                wt(act, "ssq", i, 2)
                            else:
                                wt(act, "ssq", i, 3)
                            inc(nc.scalar.activation(sqb[:].rearrange("p a b -> p (a b)"), banks[5 + b][:],
                                                     ACT.Square), "q_ev")
                        wt(act, "ssq", i, 4)
                        inc(nc.scalar.activation(col[:, 0:2], col[:, 0:2], ACT.Ln, bias=eps_col[:]), "lncol")
                        wt(act, "cols", i, 1)
                        inc(nc.scalar.activation(col[:, 6:8], col[:, 4:6], ACT.Exp), "ecol")
                        for b in range(2):
                            wt(act, "ea_m", i, b + 1)
                            inc(nc.scalar.activation(ea[:, 4 * b:4 * b + 4], ea[:, 4 * b:4 * b + 4], ACT.Exp), "ea_x")
                        for b in range(2):
                            wt(act, "eq_m", i, b + 1)
                            inc(nc.scalar.activation(qe[:, 512 * b:512 * b + 512], banks[6 + b][:], ACT.Exp), "qe_x")
                        for b in range(2):
                            wt(act, "eq_m", i, b + 1)
                            inc(nc.scalar.activation(eq[:, 4 * b:4 * b + 4], eq[:, 4 * b:4 * b + 4], ACT.Exp), "eq_x")
                        for n in range(12):
                            b = n % 2
                            wt(act, "ym", i, n + 1)
                            inc(nc.scalar.activation(t_sb[b][:].rearrange("p a b -> p (a b)"),
                                                     banks[(7, 4)[b]][:], ACT.Copy), "tc")
                        for b in range(2):
                            wt(act, "uw", i, 2 * b + 1)
                            inc(nc.scalar.activation(u_val[:, 4 * b:4 * b + 4].rearrange("p a b -> p (a b)"),
                                                     banks[6 + b][:], ACT.Copy), "u_ev")
                        for c in range(16):
                            p, r = c // 2, c % 2
                            other = slice(64 - 64 * r, 128 - 64 * r)
                            wt(act, "m2", i, c + 1)
                            inc(nc.scalar.activation(ot[other, p], banks[5 + c % 2][other, :P], ACT.Copy), "o_ev")
                        wt(act, "oss", i, 1)
                        inc(nc.scalar.activation(col[:, 8], col[:, 8], ACT.Ln, scale=1.0 / DK, bias=eps_col[:]), "oln")
                        wt(act, "oln", i, 1)
                        inc(nc.scalar.activation(col[:, 8], col[:, 8], ACT.Exp, scale=-0.5), "oln")
                        for m in range(2):
                            act.wait_ge(gs.sem, gs.at(i, m + 1))
                            act.dma_start(gate_scr[m, bass.ds(i, 1)].rearrange("o p t -> (o p) t"),
                                          gate[m][:]).then_inc(gout, 16)
                        wt(act, "sm", i, 17)
                        act.dma_start(o["delta_p"][0, 0, bass.ds(i, 1)].rearrange("o p t -> (o p) t"),
                                      state[0][:]).then_inc(st_dma, 16)
                        wt(act, "ob", i, 4)
                        act.dma_start(ob_scr[bass.ds(i, 1)].rearrange("o p t -> (o p) t")[:, :L],
                                      zs[:, :L]).then_inc(out_dma, 16)
                    act.wait_ge(gout, HB * 32)
                    act.wait_ge(st_dma, HB * 16)
                    act.wait_ge(out_dma, HB * 16)

                @block.vector
                def _(v):
                    with v.Fori(0, HB) as i:
                        for m in range(6):
                            j, u = m % 2, m // 2
                            v.wait_ge(whi[j].sem, whi[j].at(i, u + 1))
                            split_lo(v, w_lo[j][:], w_raw[j][:], w_hi[j][:]).then_inc(wlo[j].sem, 1)
                            if m < 3:
                                v.wait_ge(evac[2].sem, evac[2].at(i, m + 1))
                                if m == 0:
                                    wt(v, "ob", i, 0)
                                x, y = pre[m], qkv[m]
                                ysm = y[:, L:].unsqueeze(2)
                                k8 = bass.ds(m * HB + i, 1)
                                st = conv_state[:, k8].rearrange("p o (b j) -> p (o b) j", j=3)
                                cw = conv_wt[:, k8].rearrange("p o j -> p (o j)")
                                nc.vector.tensor_scalar(y[:], x[:, 3:], cw[:, 3:4], None,
                                                        ALU.mult).then_inc(conv.sem, 1)
                                for n, tap in enumerate((2, 1, 0)):
                                    v.wait_ge(conv.sem, conv.at(i, 7 * m + 1 + 2 * n))
                                    nc.vector.scalar_tensor_tensor(
                                        y[:, L:].unsqueeze(2), st[:, :, tap:tap + 1], cw[:, tap:tap + 1], ysm,
                                        ALU.mult, ALU.add).then_inc(conv.sem, 1)
                                    nc.vector.scalar_tensor_tensor(
                                        y[:, :L], x[:, tap:tap + L], cw[:, tap:tap + 1], y[:, :L],
                                        ALU.mult, ALU.add).then_inc(conv.sem, 1)
                                v.wait_ge(thalf.sem, thalf.at(i, m + 1))
                                nc.vector.scalar_tensor_tensor(y[:], tanh[:], 1.0, y[:], ALU.add,
                                                               ALU.mult).then_inc(silu.sem, 1)
                            elif m == 3:
                                v.wait_ge(zt.sem, zt.at(i, 1))
                                nc.vector.scalar_tensor_tensor(zs[:], tanh[:], 1.0, zs[:], ALU.add,
                                                               ALU.mult).then_inc(silu.sem, 1)
                            else:
                                v.wait_ge(evac[2].sem, evac[2].at(i, m + 1))
                                v.wait_ge(gout, i * 32)
                                nc.vector.tensor_scalar(gate[m - 4][:], tanh[:], 0.5, 0.5, ALU.mult,
                                                        ALU.add).then_inc(gs.sem, 1)
                        v.wait_ge(silu.sem, silu.at(i, 4))
                        for n, x in enumerate((qc, kc, vc, zs)):
                            x = nc.vector.tensor_copy(samp[:, n, bass.ds(i, 1)], x[:, L:].unsqueeze(1))
                        inc(x, "samp_m")
                        for b in range(2):
                            wt(v, "k_ev", i, b + 1)
                            kt4 = k_tok[:, 4 * b:4 * b + 4]
                            wt(v, "ssq", i, b)
                            inc(nc.vector.tensor_tensor(sqb[:], kt4, kt4, ALU.mult), "sq")
                            wt(v, "sq", i, b + 1)
                            inc(nc.vector.reduce_sum(col[:, 0, 4 * b:4 * b + 4], sqb[:], AX.X), "ssq")
                        for b in range(2):
                            wt(v, "q_ev", i, b + 1)
                            inc(nc.vector.reduce_sum(col[:, 1, 4 * b:4 * b + 4], sqb[:], AX.X), "ssq")
                        beta_h = beta_all[:, bass.ds(i, 1)].rearrange("p o t -> p (o t)")
                        for b in range(2):
                            wt(v, "turned", i, b + 5)
                            bank = banks[(7, 3)[b]][:].rearrange("p (a b) -> p a b", a=4)
                            bt = beta_h[:, 4 * b:4 * b + 4].unsqueeze(2).to_broadcast([P, 4, P])
                            inc(nc.vector.tensor_tensor(vb[:, 4 * b:4 * b + 4], bank, bt, ALU.mult), "v_ev")
                        wt(v, "lncol", i, 1)
                        for dst, lr, st in ((3, 0, 1), (2, 1, 2), (5, 0, 3), (4, 0, 0)):
                            x = nc.vector.scalar_tensor_tensor(
                                col[:, dst], col[:, lr], -0.5,
                                stage_g[:, st, bass.ds(i, 1)].rearrange("p o t -> p (o t)"), ALU.mult, ALU.add)
                        inc(x, "cols")
                        wt(v, "cols", i, 1)
                        for dst, c in ((kbe, 4), (kdec, 2)):
                            inc(nc.vector.tensor_tensor(dst[:], ident[:].unsqueeze(1).to_broadcast(F8),
                                                        col[:, c].unsqueeze(2).to_broadcast(F8), ALU.mult), "diag")
                        for n in range(4):
                            wt(v, "rb", i, n + 1)
                            dst = ea if n < 2 else eq
                            for p in range(4):
                                q = 4 * (n % 2) + p
                                x = nc.vector.scalar_tensor_tensor(
                                    dst[:, q], banks[4 + n][:, p * P:(p + 1) * P], col[:, 3, q:q + 1],
                                    mask[:, n // 2], ALU.add, ALU.min)
                            inc(x, "ea_m" if n < 2 else "eq_m")
                        wt(v, "qe_x", i, 2)
                        inc(nc.vector.tensor_tensor(wq[:, :, 1:3], qc[:, :L].rearrange("p (a b c) -> p a b c", a=8, b=2),
                                                    qe.rearrange("p (a b c) -> p a b c", a=8, b=2), ALU.mult), "qew")
                        for b in range(2):
                            bs = slice(4 * b, 4 * b + 4)
                            wt(v, "gram", i, b + 1); wt(v, "ea_x", i, b + 1)
                            inc(nc.vector.scalar_tensor_tensor(
                                ea[:, bs].rearrange("p a b -> p (a b)"), banks[3 + b][:], -1.0,
                                ea[:, bs].rearrange("p a b -> p (a b)"), ALU.mult, ALU.mult), "an")
                        for b in range(2):
                            bs = slice(4 * b, 4 * b + 4)
                            wt(v, "gram", i, b + 3); wt(v, "eq_x", i, b + 1)
                            inc(nc.vector.tensor_tensor(
                                eq[:, bs].rearrange("p a b -> p (a b)"), banks[5 + b][:],
                                eq[:, bs].rearrange("p a b -> p (a b)"), ALU.mult), "pt")
                        wt(v, "ecol", i, 1)
                        for dst, c, name in ((kbe, 6, "kbe_m"), (kdec, 7, "kdec_m")):
                            inc(nc.vector.tensor_tensor(dst[:], k_tok[:], col[:, c].unsqueeze(2).to_broadcast(F8),
                                                        ALU.mult), name)
                        for lev in range(6):
                            for b in range(2):
                                wt(v, "xm", i, 2 * lev + b + 1)
                                inc(nc.vector.tensor_tensor(
                                    x_sb[b][:], banks[6][:].rearrange("p (a b) -> p a b", a=4),
                                    level_mask[:, lev].unsqueeze(1).to_broadcast([P, 4, P]), ALU.mult), "xs")
                            for b in range(2):
                                wt(v, "ym", i, 2 * lev + b + 1)
                                inc(nc.vector.tensor_copy(u_sb[b][:].rearrange("p a b -> p (a b)"),
                                                          banks[(3, 5)[b]][:]), "uc")
                        for b in range(2):
                            wt(v, "uw", i, 2 * b + 2)
                            inc(nc.vector.tensor_copy(
                                wq[:, 4 * b:4 * b + 4, 0:4:3],
                                banks[4 - b][:].rearrange("p (a b c) -> p a b c", a=4, b=2)), "w_ev")
                        v.wait_ge(st_dma, i * 16)
                        inc(nc.vector.memset(state[0][:], 0.0), "sm")
                        wt(v, "u_ev", i, 2)
                        for c in range(16):
                            p, r = c // 2, c % 2
                            rows = slice(64 * r, 64 * r + 64)
                            wt(v, "m1", i, c + 1)
                            inc(nc.vector.tensor_tensor(vnew[c % 2][rows], u_val[rows, p], banks[5 + c % 2][rows, :P],
                                                        ALU.subtract), "vn")
                            wt(v, "m3", i, c + 1)
                            eg = eglast[:, bass.ds(i, 1), c:c + 1].rearrange("p a b -> p (a b)")
                            inc(nc.vector.scalar_tensor_tensor(state[(c + 1) % 2][:], state[c % 2][:], eg,
                                                               banks[3 + c % 2][:, :P], ALU.mult, ALU.add), "sm")
                        wt(v, "o_ev", i, 16)
                        inc(nc.vector.tensor_tensor(u_val[:], ot[:], ot[:], ALU.mult), "osq")
                        wt(v, "osq", i, 1)
                        inc(nc.vector.reduce_sum(col[:, 8], u_val[:], AX.X), "oss")
                        wt(v, "oln", i, 2)
                        inc(nc.vector.tensor_tensor(ot[:], ot[:], col[:, 8].unsqueeze(2).to_broadcast(F8),
                                                    ALU.mult), "on")
                        for b in range(2):
                            wt(v, "ot_tr", i, b + 1)
                            bank = banks[3 + b][:].rearrange("p (a b c) -> p a b c", a=4, b=2)
                            zv = zs[:, 512 * b:512 * b + 512].rearrange("p (a b c) -> p a b c", a=4, b=2)
                            for r in range(2):
                                inc(nc.vector.scalar_tensor_tensor(zv[:, :, r], bank[:, :, 1 - r], norm_dv[:],
                                                                   zv[:, :, r], ALU.mult, ALU.mult), "ob")

        heads_block()
        hs.close()
        sample_delta_block()
        conv_out_block()
        clear_semaphores()
        mix_stack = ExitStack()
        oa_hi = sb(mix_stack, "oa_hi", [P, 2, T], FR); oa_lo = sb(mix_stack, "oa_lo", [P, 2, T], FR)
        split_ob_block()
        wa_v = a["w_branch_a"][0].rearrange("(k p) n -> p k n", p=P)
        wb_v = a["w_branch_b"][0].rearrange("(k p) n -> p k n", p=P)
        wf_v = a["w_ffn_in"][0].rearrange("(k p) n -> p k n", p=P)
        xT = (xT_hi, xT_lo)
        pair_block("mix", KT, 2, (oa_hi, oa_lo), xT, lambda n: wa_v[:, :, bass.ds(n * P, P)],
                   lambda n: wb_v[:, :, bass.ds(n * P, P)], True, mix_scr)
        mix_stack.close()

        def rows_of(prompt, sample):
            def get(t):
                return sample if isinstance(t, int) and t == NT else prompt[bass.ds(t * P, P)]
            return get

        row_block("wo", mix_scr, KT, 1, a["w_out"][0], a["norm_post_mix"][0], rows_of(xp, xs),
                  rows_of(x1_scr[:L], x1_scr[L:]))
        norm_block(rows_of(x1_scr[:L], x1_scr[L:]), a["norm_pre_ffn"][0], "_ffn")
        pair_block("ffn", FT, KT, xT, xT, lambda n: wf_v[:, :, bass.ds(n * P, P)],
                   lambda n: wf_v[:, :, bass.ds(FF + n * P, P)], False, act_scr)
        early.close()
        row_block("fo", act_scr, FT, 2, a["w_ffn_out"][0], a["norm_post_ffn"][0],
                  rows_of(x1_scr[:L], x1_scr[L:]),
                  rows_of(o["y_prompt"][0], o["y_sample"].rearrange("b s d -> (b s) d")))


def shape_constants():
    import numpy as np

    f = np.float32
    t = np.arange(P)
    i, j = t[:, None], t[None, :]
    same = i // C == j // C
    far = f(1e30)
    sums = np.stack([same & (i <= j), same, np.broadcast_to(i < C, (P, P)), np.broadcast_to(i >= C, (P, P))])
    mask = np.stack([np.where(same & (j > i), far, -far), np.where(same & (j >= i), far, -far)])
    levels = np.stack([(i // (2 * s) == j // (2 * s)) & ((i // s) % 2 == 1) & ((j // s) % 2 == 0)
                       for s in (1, 2, 4, 8, 16, 32)])
    onehot = np.zeros((33, NG, 3 * P), f)
    onehot_s = np.zeros((33, NG, P + 1), f)
    onehot[32], onehot_s[32] = -far, -far
    for g, dil in enumerate((1, 4, 16)):
        dist = np.arange(P + 1) * dil
        large = 16 + (np.log(np.maximum(dist, 1).astype(f) / 16) / np.log(2048 / 16) * 16).astype(np.int32)
        bucket = np.where(dist < 16, dist, np.minimum(large, 31)).astype(np.int32)
        step, last = (2, HD - 1) if g == 2 else (1, P)
        for n in range(last + 1):
            onehot[bucket[n], g, 2 * P - 1 - step * n] = 1
            onehot[32, g, 2 * P - 1 - step * n] = 0
        keys = HD if g == 2 else P
        for n in range(keys):
            onehot_s[bucket[keys - n], g, n] = 1
            onehot_s[32, g, n] = 0
        onehot_s[bucket[0], g, P] = 1
        onehot_s[32, g, P] = 0
    return {"c_ident": np.eye(P, dtype=f), "c_sums": sums.astype(f), "c_mask": mask.astype(f),
            "c_levels": levels.astype(f), "c_onehot": onehot, "c_onehot_s": onehot_s,
            "c_ones": np.ones((1, 16), f)}


_INS = ["x_prompt", "x_sample", "cache_kv_w128", "cache_kv_w512", "cache_kv_w2048", "state_delta", "state_conv",
        "rel_bias", "norm_pre_mix", "w_in", "conv_w", "a_log", "dt_bias", "norm_delta", "w_branch_a", "w_branch_b",
        "w_out", "norm_post_mix", "norm_pre_ffn", "w_ffn_in", "w_ffn_out", "norm_post_ffn"]
_OUTS = [("y_prompt", (1, L, D)), ("y_sample", (NS, 1, D)),
         ("kv128_p", (1, 1, 128, 2, HA, HD)), ("kv512_p", (1, 1, 512, 2, HA, HD)), ("kv2048_p", (1, 1, L, 2, HA, HD)),
         ("delta_p", (1, 1, HB, DK, DK)), ("conv_p", (1, 1, 3, 3 * D)),
         ("kv128_s", (1, NS, 1, 2, HA, HD)), ("kv512_s", (1, NS, 1, 2, HA, HD)), ("kv2048_s", (1, NS, 1, 2, HA, HD)),
         ("delta_s", (1, NS, HB, DK, DK)), ("conv_s", (1, NS, 3, 3 * D))]


def kernel(**inputs):
    import numpy as np
    import concourse.bacc as bacc
    from concourse.bass_utils import run_bass_kernel_spmd

    nc = bacc.Bacc("TRN2", target_bir_lowering=False, num_devices=1)
    arrays, a, o = {}, {}, {}
    given = {name: np.ascontiguousarray(inputs[name]) for name in _INS}
    given.update(shape_constants())
    for name, x in given.items():
        arrays[f"in_{name}"] = x
        a[name] = nc.dram_tensor(f"in_{name}", x.shape, FP, kind="ExternalInput").ap()
    for name, shape in _OUTS:
        o[name] = nc.dram_tensor(f"out_{name}", shape, FP, kind="ExternalOutput").ap()
    build(nc, a, o)
    r = run_bass_kernel_spmd(nc, [arrays], core_ids=[0])
    return tuple(r.results[0][f"out_{name}"] for name, _ in _OUTS)
```

```python
import math
from contextlib import ExitStack

import concourse.bass as bass
from concourse import mybir

FP = mybir.dt.float32
FR = mybir.dt.float32r
ACT = mybir.ActivationFunctionType
ALU = mybir.AluOpType
AX = mybir.AxisListType

P = 128
D = 1024
L = 1024
NS = 8
NT = L // P
T = L + NS
KT = D // P
NG, HA, HD = 3, 4, 64
HB, DK = 8, 128
C = 64
FF = 2816
FT = FF // P
G3 = T // 3
A_QKV = NG * 3 * HA * HD
CONV0 = A_QKV
Z0 = CONV0 + 3 * D
BA0 = Z0 + D
GATE0 = BA0 + 2 * HB
EPS = 1e-6
CS = 28


class Event:

    def __init__(self, sem, per=1, skip=0):
        self.sem, self.per, self.skip = sem, per, skip

    def at(self, turn, step=1):
        return turn * self.per + (step - self.skip)


class Filler:

    def __init__(self, steps, done=(), lag=1):
        self.steps, self.done, self.lag = steps, done, lag
        self.need = next(steps, None)

    def upto(self, n):
        while self.need is not None and self.need <= n:
            self.need = next(self.steps, None)

    def slot(self, p):
        self.upto(self.done[p - self.lag] if p >= self.lag else 0)

    def finish(self):
        self.upto(1 << 20)


def sums(per_slot):
    return [sum(per_slot[:p + 1]) for p in range(len(per_slot))]


def build(nc, a, o):
    ctx = ExitStack()
    with ctx:
        n_names = [0]

        def sb(stack, name, shape, dt=FP):
            return stack.enter_context(nc.sbuf_tensor(name, shape, dt))

        def pb(stack, name):
            return stack.enter_context(nc.psum_tensor(name, [P, 512], FP))

        live = []

        def sem(name):
            n_names[0] += 1
            live.append(nc.alloc_semaphore(name=f"{name}_{n_names[0]}"))
            return live[-1]

        def clear_semaphores():
            with nc.Block() as block:
                @block.gpsimd
                def _(pool):
                    for x in live:
                        pool.sem_clear(x)
            for x in live:
                nc.release_semaphore(x)
            live.clear()

        def ev(name, per=1, skip=0):
            return Event(sem(name), per, skip)

        def start(eng, amount, *sems):
            for x in sems:
                eng.sem_inc(x, amount)

        def dram(name, shape):
            return nc.dram_tensor(name, shape, FP, kind="Internal").ap()

        gate_scr = dram("gate_scr", (2, HB, P, T))
        ob_scr = dram("ob_scr", (HB, P, T))
        x1_scr = dram("x1_scr", (T, D))
        mix_scr = dram("mix_scr", (KT, P, T))
        act_scr = dram("act_scr", (FT, P, T))
        bias_scr = dram("bias_scr", (NG * HA, P, 3 * P))

        early = ExitStack()
        xT_hi = sb(early, "xT_hi", [P, KT, T], FR)
        xT_lo = sb(early, "xT_lo", [P, KT, T], FR)
        ident = sb(early, "ident", [P, P])
        norm_dv = sb(early, "norm_dv", [P, 1])
        conv_new = sb(early, "conv_new", [P, 24, 3 + NS])
        ident_ones = sb(early, "ones", [P, P])
        oaT = sb(early, "oaT", [P, 2, T])
        banks = [pb(ctx, f"bank{i}") for i in range(8)]

        def norm_block(row_tile, weight, tag=""):
            with ExitStack() as s:
                rows = [sb(s, f"rows{j}{tag}", [P, D]) for j in range(2)]
                normed = [sb(s, f"normed{j}{tag}", [P, D]) for j in range(2)]
                sq = sb(s, f"sq{tag}", [P, D])
                wrow = sb(s, f"wrow{tag}", [P, D])
                stat = sb(s, f"stat{tag}", [P, 2, 4])
                loaded = [ev("loaded"), ev("loaded")]
                const, squared = sem("const"), [ev("squared", 3, -1), ev("squared", 3, -1)]
                made = [ev("made", 1, -1), ev("made", 1, -1)]
                turned = [ev("turned", 2, -1), ev("turned", 2, -1)]
                hi_done = [ev("hi", 2), ev("hi", 2)]
                lo_done = [ev("lo", 2, -1), ev("lo", 2, -1)]
                eps = sem("eps")

                def tiles(eng, stage, finish):
                    def run(i, stage_next):
                        stage(eng, i, 1, P, i * 2 + 1)
                        finish(eng, i, 0, P, i * 2)
                        stage_next(i)
                        finish(eng, i, 1, P, i * 2 + 1)
                    stage(eng, 0, 0, P, 0)
                    with eng.Fori(0, NT // 2 - 1) as i:
                        run(i, lambda i: stage(eng, i + 1, 0, P, i * 2 + 2))
                    run(NT // 2 - 1, lambda i: stage(eng, NT // 2, 0, NS, NT))
                    finish(eng, NT // 2, 0, NS, NT)

                def nothing(*_):
                    pass

                def load(sp, i, j, n, t):
                    sp.wait_ge(made[j].sem, made[j].at(i, 0))
                    sp.dma_start(rows[j][:n], row_tile(t)).then_inc(loaded[j].sem, 16)

                def stats(act, i, j, n, t):
                    act.wait_ge(loaded[j].sem, i * 16 + 16)
                    if j == 0:
                        act.wait_ge(squared[1].sem, squared[1].at(i, 0))
                    else:
                        act.wait_ge(squared[0].sem, squared[0].at(i, 3))
                    nc.scalar.activation(sq[:n], rows[j][:n], ACT.Square,
                                         accum_out=stat[:n, j, 0:1]).then_inc(squared[j].sem, 1)
                    act.wait_ge(squared[j].sem, squared[j].at(i, 1))
                    nc.scalar.activation(stat[:n, j, 1:2], stat[:n, j, 0:1], ACT.Ln, scale=1.0 / D,
                                         bias=stat[:n, 0, 3:4]).then_inc(squared[j].sem, 1)
                    act.wait_ge(squared[j].sem, squared[j].at(i, 2))
                    nc.scalar.activation(stat[:n, j, 2:3], stat[:n, j, 1:2], ACT.Exp,
                                         scale=-0.5).then_inc(squared[j].sem, 1)

                def split_hi(act, i, j, n, t):
                    for half in range(2):
                        act.wait_ge(turned[j].sem, turned[j].at(i, half + 1))
                        src = banks[2 * j + half][:].rearrange("p (k c) -> p k c", k=4)[:, :, :n]
                        nc.scalar.activation(
                            xT_hi[:, 4 * half:4 * half + 4, bass.ds(t * P, n)], src,
                            ACT.Copy).then_inc(hi_done[j].sem, 1)

                def center(v, i, j, n, t):
                    v.wait_ge(squared[j].sem, squared[j].at(i, 3))
                    v.wait_ge(turned[j].sem, turned[j].at(i, 0))
                    nc.vector.scalar_tensor_tensor(normed[j][:n], rows[j][:n], stat[:n, j, 2:3],
                                                   wrow[:n], ALU.mult, ALU.mult).then_inc(made[j].sem, 1)

                def split(v, i, j, n, t):
                    for half in range(2):
                        v.wait_ge(hi_done[j].sem, hi_done[j].at(i, half + 1))
                        src = banks[2 * j + half][:].rearrange("p (k c) -> p k c", k=4)[:, :, :n]
                        at = (slice(None), slice(4 * half, 4 * half + 4), bass.ds(t * P, n))
                        nc.vector.tensor_tensor(xT_lo[at], src, xT_hi[at].bitcast(FP),
                                                ALU.subtract).then_inc(lo_done[j].sem, 1)

                def turn(pe, i, j, n, t):
                    pe.wait_ge(made[j].sem, made[j].at(i))
                    for half in range(2):
                        pe.wait_ge(lo_done[j].sem, lo_done[j].at(i, half - 1) if half else lo_done[j].at(i, 0))
                        for k in range(4):
                            last = nc.tensor.transpose(banks[2 * j + half][:, k * P:k * P + n],
                                                       normed[j][:n, (4 * half + k) * P:(4 * half + k + 1) * P],
                                                       ident[:n, :n])
                        last.then_inc(turned[j].sem, 1)

                with nc.Block() as block:
                    @block.sync
                    def _(sp):
                        sp.dma_start(wrow[:], weight.partition_broadcast(P)).then_inc(const, 16)
                        sp.dma_start(ident[:], a["c_ident"]).then_inc(const, 16)
                        tiles(sp, load, nothing)

                    @block.vector
                    def _(v):
                        start(v, 1, *(e.sem for e in made + lo_done))
                        nc.vector.memset(stat[:, :, 3:4], EPS).then_inc(eps, 1)
                        v.wait_ge(const, 32)
                        tiles(v, center, split)

                    @block.scalar
                    def _(act):
                        nc.scalar.preload_act_table_set("natural_log_exp_and_others")
                        start(act, 1, *(e.sem for e in squared))
                        act.wait_ge(eps, 1)
                        tiles(act, stats, split_hi)

                    @block.tensor
                    def _(pe):
                        start(pe, 1, *(e.sem for e in turned))
                        pe.wait_ge(const, 32)
                        tiles(pe, nothing, turn)

        xs = a["x_sample"].rearrange("b s d -> (b s) d")
        xp = a["x_prompt"][0]
        norm_block(lambda t: xs if isinstance(t, int) and t == NT else xp[bass.ds(t * P, P)],
                   a["norm_pre_mix"][0])

        beta_all = sb(early, "beta_all", [P, HB, NT + 1])
        gcol = sb(early, "gcol", [P, HB, NT + 1])
        stage_g = sb(early, "stage_g", [P, 4, HB, NT])
        eglast = sb(early, "eglast", [P, HB, 2 * NT])
        eg_s = sb(early, "eg_s", [P, 2, HB, NS])
        ob_s = sb(early, "ob_s", [P, HB, NS])
        samp = sb(early, "samp", [P, 4, HB, NS])

        def split_weights_hi(act, dst, src):
            return nc.scalar.activation(dst, src, ACT.Copy)

        def split_lo(v, dst, src, hi):
            return nc.vector.tensor_tensor(dst, src, hi.bitcast(FP), ALU.subtract)

        def passes(out, stat_hi, stat_lo, mov_hi, mov_lo, start, stop):
            nc.tensor.matmul(out, stat_lo, mov_hi, start=start, stop=False)
            nc.tensor.matmul(out, stat_hi, mov_lo, start=False, stop=False)
            return nc.tensor.matmul(out, stat_hi, mov_hi, start=False, stop=stop)

        w_in = a["w_in"][0].rearrange("(k p) n -> p k n", p=P)

        def beta_decay_steps(s):
            raw = sb(s, "ba_raw", [P, KT, 16]); hi = sb(s, "ba_hi", [P, KT, 16], FR)
            lo = sb(s, "ba_lo", [P, KT, 16], FR)
            ch = sb(s, "ba_ch", [16, T]); tok = sb(s, "ba_tok", [P, NT + 1, 16])
            par = sb(s, "ba_par", [P, 2, HB]); ea = sb(s, "ba_ea", [P, HB])
            x = sb(s, "ba_x", [P, 16, NT + 1]); t = sb(s, "ba_t", [P, 16, NT + 1])
            lnb = sb(s, "ba_lnb", [P, HB, NT + 1])
            tri = sb(s, "ba_tri", [P, 4, P])
            half = sb(s, "ba_half", [P, 2, HB, NT])
            gls = sb(s, "ba_gls", [P, HB, NT])
            smp = sb(s, "ba_smp", [NS, 2, HB, NS])
            ld, sp_hi, sp_lo, pj, evac, tr, tk = (sem(n) for n in ("ld", "shi", "slo", "pj", "ev", "tr", "tk"))
            dv, ac, mm = sem("dve_step"), sem("act_step"), sem("mm")

            def load(sp):
                with nc.allow_non_contiguous_dma(reason="16 columns"):
                    sp.dma_start(raw[:], w_in[:, :, BA0:BA0 + 16]).then_inc(ld, 16)
                sp.dma_start(par[:, 0], a["a_log"][0].partition_broadcast(P)).then_inc(ld, 16)
                sp.dma_start(par[:, 1], a["dt_bias"][0].partition_broadcast(P)).then_inc(ld, 16)
                sp.dma_start(tri[:], a["c_sums"].rearrange("n p f -> p n f")).then_inc(ld, 16)

            def pe_first(pe):
                pe.wait_ge(sp_lo, 1)
                for g in range(3):
                    c = slice(g * G3, (g + 1) * G3)
                    for k in range(KT):
                        last = passes(banks[g][:16, :G3], hi[:, k], lo[:, k], xT_hi[:, k, c], xT_lo[:, k, c],
                                      k == 0, k == KT - 1)
                    last.then_inc(pj, 1)

            def pe_second(pe):
                pe.wait_ge(evac, 3)
                for i in range(NT + 1):
                    n = P if i < NT else NS
                    last = nc.tensor.transpose(banks[3][:n, 16 * i:16 * i + 16], ch[:, i * P:i * P + n],
                                               ident[:16, :16])
                last.then_inc(tr, 1)
                pe.wait_ge(dv, 8)
                g_in = gcol[:, :, :NT]
                for i in range(4):
                    last = nc.tensor.matmul(banks[4][:, 64 * i:64 * i + 64], tri[:, i], g_in, start=True, stop=True)
                pe.wait_ge(dv, 9)
                last = nc.tensor.matmul(banks[4][:, 4 * HB * NT:4 * HB * NT + 2 * HB * NS], ident_ones[:NS],
                                        smp[:].rearrange("b n h c -> b (n h c)"), start=True, stop=True)
                last.then_inc(mm, 1)

            def act_first(act):
                act.wait_ge(ld, 64)
                split_weights_hi(act, hi[:], raw[:]).then_inc(sp_hi, 1)
                nc.scalar.activation(ea[:], par[:, 0], ACT.Exp).then_inc(ac, 1)
                for g in range(3):
                    act.wait_ge(pj, g + 1)
                    nc.scalar.activation(ch[:, g * G3:(g + 1) * G3], banks[g][:16, :G3], ACT.Copy).then_inc(evac, 1)

            def act_second(act):
                act.wait_ge(dv, 3)
                nc.scalar.activation(t[:], t[:], ACT.Exp).then_inc(ac, 1)
                act.wait_ge(ac, 2)
                nc.scalar.activation(t[:], t[:], ACT.Ln, bias=1.0).then_inc(ac, 1)
                act.wait_ge(dv, 6)
                nc.scalar.activation(beta_all[:], lnb[:], ACT.Exp).then_inc(ac, 1)
                act.wait_ge(dv, 12)
                nc.scalar.activation(eglast[:].rearrange("p h (c r) -> p r h c", r=2), half[:], ACT.Exp).then_inc(ac, 1)
                act.wait_ge(mm, 1)
                nc.scalar.activation(eg_s[:].rearrange("p n h b -> p (n h b)"), banks[4][:, 4 * HB * NT:4 * HB * NT + 2 * HB * NS], ACT.Copy).then_inc(ac, 1)
                act.wait_ge(ac, 6)
                nc.scalar.activation(eg_s[:, 0], eg_s[:, 0], ACT.Exp).then_inc(ac, 1)

            def dve_first(v):
                v.wait_ge(sp_hi, 1)
                split_lo(v, lo[:], raw[:], hi[:]).then_inc(sp_lo, 1)
                nc.vector.memset(x[:], 0.0).then_inc(dv, 1)

            def dve_second(v):
                v.wait_ge(dv, 1)
                v.wait_ge(tr, 1)
                src = banks[3][:, :16 * NT].rearrange("p (i c) -> p c i", c=16)
                nc.vector.tensor_copy(x[:, :, :NT], src)
                nc.vector.tensor_copy(x[:NS, :, NT], banks[3][:NS, 16 * NT:16 * NT + 16]).then_inc(dv, 1)
                v.wait_ge(dv, 2)
                nc.vector.tensor_scalar(x[:, :HB], x[:, :HB], -1.0, None, ALU.mult)
                nc.vector.tensor_tensor(x[:, HB:], x[:, HB:], par[:, 1].unsqueeze(2).to_broadcast([P, HB, NT + 1]),
                                        ALU.add).then_inc(tk, 1)
                v.wait_ge(tk, 1)
                nc.vector.scalar_tensor_tensor(t[:], x[:], -1.0, x[:], ALU.mult, ALU.min).then_inc(dv, 1)
                v.wait_ge(dv, 3)
                nc.vector.tensor_scalar(x[:], x[:], 0.0, None, ALU.max).then_inc(dv, 1)
                v.wait_ge(dv, 4)
                v.wait_ge(ac, 3)
                nc.vector.tensor_tensor(x[:], x[:], t[:], ALU.add).then_inc(dv, 1)
                v.wait_ge(dv, 5)
                nc.vector.tensor_scalar(lnb[:], x[:, :HB], -1.0, None, ALU.mult).then_inc(dv, 1)
                nc.vector.tensor_scalar(ea[:], ea[:], -1.0, None, ALU.mult).then_inc(dv, 1)
                v.wait_ge(dv, 7)
                nc.vector.tensor_tensor(gcol[:], x[:, HB:], ea[:].unsqueeze(2).to_broadcast([P, HB, NT + 1]),
                                        ALU.mult).then_inc(dv, 1)
                v.wait_ge(dv, 8)
                v.wait_ge(ac, 4)
                eye = ident[:NS, :NS].unsqueeze(1).to_broadcast([NS, HB, NS])
                nc.vector.tensor_tensor(smp[:, 0], gcol[:NS, :, NT:].to_broadcast([NS, HB, NS]), eye, ALU.mult)
                nc.vector.tensor_tensor(smp[:, 1], beta_all[:NS, :, NT:].to_broadcast([NS, HB, NS]), eye,
                                        ALU.mult).then_inc(dv, 1)
                v.wait_ge(mm, 1)
                part = [banks[4][:, 64 * i:64 * i + 64].rearrange("p (h c) -> p h c", h=HB) for i in range(4)]
                nc.vector.tensor_copy(stage_g[:, 1], part[0]).then_inc(dv, 1)
                nc.vector.tensor_copy(half[:, 0], part[2])
                nc.vector.tensor_copy(half[:, 1], part[3])
                nc.vector.tensor_copy(gls[:], part[1]).then_inc(dv, 1)
                v.wait_ge(dv, 11)
                nc.vector.tensor_scalar(stage_g[:, 2], stage_g[:, 1], -0.5 * math.log(DK), None, ALU.add).then_inc(dv, 1)
                nc.vector.tensor_tensor(stage_g[:, 0], stage_g[:, 1], lnb[:, :, :NT], ALU.add)
                nc.vector.tensor_tensor(stage_g[:, 3], gls[:], stage_g[:, 1], ALU.subtract).then_inc(dv, 1)
                v.wait_ge(dv, 13)
                nc.vector.tensor_scalar(stage_g[:, 1], stage_g[:, 1], -1.0, None, ALU.mult).then_inc(dv, 1)

            def over(eng):
                eng.wait_ge(dv, 14)
                eng.wait_ge(ac, 7)

            return load, pe_first, pe_second, act_first, act_second, dve_first, dve_second, over

        with nc.Block() as block:
            ones_set = sem("ones_set")

            @block.vector
            def _(v):
                nc.vector.memset(ident_ones[:], 1.0).then_inc(ones_set, 1)
                v.wait_ge(ones_set, 1)

        att_scr = dram("att_scr", (NG, L, HA * (HD + 2)))
        HS = HD + 2
        att_stack = ExitStack()
        kv_s = sb(att_stack, "kv_s", [NS, NG, 2 * HA * HD])
        qT_s = sb(att_stack, "qT_s", [P, NG, 2, NS])

        def key_rows(g, t):
            if g == 0:
                return lambda x: x[:, t * P:(t + 1) * P]
            if g == 1:
                c, n = t // 2, t % 2
                return lambda x: x[:, c + 4 * P * n:c + 4 * P * n + 4 * P - 3:4]
            return lambda x: x[:, t:L - NT + t + 1:NT]

        def dram_rows(g, t, x):
            if g == 0:
                return x[t * P:(t + 1) * P]
            if g == 1:
                c, n = t // 2, t % 2
                return x[c + 4 * P * n:c + 4 * P * n + 4 * P - 3:4]
            return x[t::NT]

        def bias_steps(s):
            table = sb(s, "bias_table", [33, NG * HA]); onehot = sb(s, "onehot", [33, NG, 3 * P])
            wide = sb(s, "bias_wide", [33, NG * HA, P])
            res = sb(s, "bias_res", [P, NG * HA, 3 * P])
            ld, spread, mm, cp, out = sem("b_ld"), sem("b_spread"), sem("b_mm"), sem("b_cp"), sem("b_out")

            def load(sp):
                sp.dma_start(table[:32], a["rel_bias"]).then_inc(ld, 16)
                sp.dma_start(table[32:33], a["c_ones"][0:1, :NG * HA]).then_inc(ld, 16)
                sp.dma_start(onehot[:], a["c_onehot"]).then_inc(ld, 16)

            def store(sp):
                sp.wait_ge(cp, NG * HA)
                sp.dma_start(bias_scr.rearrange("n p x -> p n x"), res[:]).then_inc(out, 16)
                sp.wait_ge(out, 16)

            def products(pe):
                pe.wait_ge(spread, 1)
                for n in range(NG * HA):
                    if n >= 8:
                        pe.wait_ge(cp, n - 7)
                    nc.tensor.matmul(banks[n % 8][:, :3 * P], wide[:, n], onehot[:, n // HA],
                                     start=True, stop=True).then_inc(mm, 1)

            def copies(v):
                v.wait_ge(ld, 48)
                nc.vector.tensor_copy(wide[:], table[:].unsqueeze(2).to_broadcast([33, NG * HA, P])).then_inc(spread, 1)
                for n in range(NG * HA):
                    v.wait_ge(mm, n + 1)
                    nc.vector.tensor_copy(res[:, n], banks[n % 8][:, :3 * P]).then_inc(cp, 1)

            def over(eng, stored):
                eng.wait_ge(cp, NG * HA)
                if stored:
                    eng.wait_ge(out, 16)

            return load, store, products, copies, over

        def attention_block():
            with ExitStack() as s, nc.Block() as block:
                KV, Q = 2 * HA * HD, HA * HD
                kv_hi = sb(s, "a_kv_hi", [P, KT, KV], FR); q_hi = sb(s, "a_q_hi", [P, KT, Q], FR)
                with ExitStack() as place:
                    kv_raw = sb(place, "a_kv_raw", [P, KT, KV]); q_raw = sb(place, "a_q_raw", [P, KT, Q])
                kv_lo = sb(s, "a_kv_lo", [P, KT, KV], FR); q_lo = sb(s, "a_q_lo", [P, KT, Q], FR)
                kv0, kT0 = sb(s, "a_kv0", [P, NT, KV]), sb(s, "a_kT0", [P, 2, L])
                with ExitStack() as place:
                    (bias_load, bias_store, bias_products, bias_copies, bias_over) = bias_steps(place)
                    (beta_load, beta_pe, beta_pe2, beta_act, beta_act2, beta_dve, beta_dve2,
                     beta_over) = beta_decay_steps(place)
                kv2 = kv0, sb(s, "a_kv1", [P, NT, KV])
                kT2 = kT0, sb(s, "a_kT1", [P, 2, L])
                qT = sb(s, "a_qT", [P, 2, T])
                bias = sb(s, "a_bias", [P, HA, 2 * P])
                sc = [sb(s, f"a_sc{j}", [P, HA, 2 * P]) for j in range(2)]
                pT = sb(s, "a_pT", [P, HA * 2 * P])
                os_ = sb(s, "a_os", [P, 2, HA, HS]); nm = sb(s, "a_nm", [P, 2, HA])
                N = dict(kv_hi=1, kv_lo=1, q_hi=1, q_lo=1, kvd=9, kv_ev=9, ktd=8, kt_ev=8, qd=6, q_ev=6, qs=1,
                         sd=8, st=16, mx=8, nm=8, ex=8, ptd=8, pt_ev=8, pv=8, oe=8)
                E = {k: ev("a_" + k, n) for k, n in N.items()}
                kv_ld, q_ld, bld = sem("a_kv_ld"), sem("a_q_ld"), sem("a_bld")
                kvo = [sem("a_kvo") for _ in range(NG)]
                oso = [sem("a_oso") for _ in range(2)]
                KVO = (2, 5, 9)
                done = sums(NT * [KT + 1])
                SPLIT_Q = 4

                def inc(ins, name):
                    ins.then_inc(E[name].sem, 1)

                def wt(eng, name, g, k):
                    if E[name].at(g, k) > 0:
                        eng.wait_ge(E[name].sem, E[name].at(g, k))

                def blocks(g, t):
                    if g == 2 or (g == 0 and t == 0) or (g == 1 and t % 2 == 0):
                        return [t]
                    return [t - 1, t]

                def no_steps():
                    return iter(())

                def groups(eng, kv_steps, beside, q_part, tile, lag):
                    Filler(kv_steps(0)).finish()
                    beside(eng)
                    for g in range(NG):
                        q_part(g)
                        fill = Filler(kv_steps(g + 1) if g + 1 < NG else no_steps(), done, lag)
                        for t in range(NT):
                            tile(g, t, fill)
                        fill.finish()

                @block.sync
                def _(sp):
                    def load(g, part):
                        c0 = g * 3 * HA * HD
                        if part == "kv":
                            wt(sp, "kvd", g, 0)
                            sp.dma_start(kv_raw[:], w_in[:, :, c0 + Q:c0 + Q + KV]).then_inc(kv_ld, 16)
                        else:
                            wt(sp, "qd", g, 0)
                            sp.dma_start(q_raw[:], w_in[:, :, c0:c0 + Q]).then_inc(q_ld, 16)

                    bias_load(sp)
                    beta_load(sp)
                    load(0, "kv"); load(0, "q")
                    bias_store(sp)
                    beta_over(sp)
                    for g in range(NG):
                        wt(sp, "st", g, 0)
                        sp.dma_start(bias[:], bass.AP(bias_scr.tensor, g * HA * P * 3 * P + P - 1,
                                                      [[3 * P - 1, P], [P * 3 * P, HA], [1, 2 * P]])).then_inc(bld, 16)
                        out = o[("kv128_p", "kv512_p", "kv2048_p")[g]][0, 0].rearrange("r s h d -> r (s h d)")
                        kv = kv2[g % 2]
                        for t in range(NT + 1):
                            if t == NT:
                                wt(sp, "kv_ev", g, t + 1)
                                dst = o[("kv128_s", "kv512_s", "kv2048_s")[g]][0, :, 0].rearrange("b s h d -> b (s h d)")
                                sp.dma_start(dst, kv_s[:, g]).then_inc(kvo[g], 16)
                            elif g == 2:
                                wt(sp, "kv_ev", g, t + 1)
                                sp.dma_start(dram_rows(2, t, out), kv[:, t]).then_inc(kvo[g], 16)
                            elif (g == 0 and t == NT - 1):
                                wt(sp, "kv_ev", g, t + 1)
                                sp.dma_start(out, kv[:, t]).then_inc(kvo[g], 16)
                            elif g == 1 and t % 2:
                                wt(sp, "kv_ev", g, t + 1)
                                sp.dma_start(out[t // 2::4], kv[:, t]).then_inc(kvo[g], 16)
                        if g + 1 < NG:
                            load(g + 1, "kv"); load(g + 1, "q")
                        for t in range(NT):
                            wt(sp, "oe", g, t + 1)
                            wt(sp, "ex", g, t + 1)
                            sp.dma_start(dram_rows(g, t, att_scr[g]),
                                         os_[:, t % 2].rearrange("p h w -> p (h w)")).then_inc(oso[t % 2], 16)
                    for j in range(2):
                        sp.wait_ge(oso[j], NG * NT // 2 * 16)
                    for g in range(NG):
                        sp.wait_ge(kvo[g], KVO[g] * 16)

                @block.tensor
                def _(pe):
                    def turn_keys(g, t):
                        wt(pe, "kv_ev", g, t + 1)
                        wt(pe, "kt_ev", g, t)
                        for m in range(2):
                            last = nc.tensor.transpose(banks[7][:, m * P:(m + 1) * P],
                                                       kv2[g % 2][:, t, m * P:(m + 1) * P], ident[:])
                        inc(last, "ktd")

                    def kv_steps(g):
                        for t in range(NT + 1):
                            n = P if t < NT else NS
                            sel = key_rows(g, t) if t < NT else (lambda x: x[:, L:])
                            for k in range(KT):
                                yield t * KT + k + 1
                                if k == 0:
                                    wt(pe, "kv_lo", g, 1)
                                    wt(pe, "q_ev", g, 0)
                                    wt(pe, "kv_ev", g, max(t - 1, 0))
                                last = passes(banks[5 + t % 2][:n, :], sel(xT_hi[:, k]), sel(xT_lo[:, k]),
                                              kv_hi[:, k], kv_lo[:, k], k == 0, k == KT - 1)
                                if k == 1 and t >= 2:
                                    turn_keys(g, t - 2)
                            inc(last, "kvd")
                        yield (NT + 1) * KT + 2
                        turn_keys(g, NT - 1)

                    def scores(g, t):
                        wt(pe, "st", g, 2 * t)
                        ks = blocks(g, t)
                        sel = key_rows(g, t)
                        for h in range(HA):
                            m, r = h // 2, 64 * (h % 2)
                            dst = banks[h % 2][:, m * 256 + 256 - P * len(ks):m * 256 + 256]
                            last = nc.tensor.matmul(dst, sel(qT[r:r + 64, m]),
                                                    kT2[g % 2][r:r + 64, m, ks[0] * P:(t + 1) * P],
                                                    start=True, stop=True)
                        inc(last, "sd")

                    def q_part(g):
                        wt(pe, "q_lo", g, 1)
                        wt(pe, "kv_ev", g, 9); wt(pe, "kt_ev", g, 8)
                        for m in range(2):
                            for c in range(3):
                                n = 3 * m + c
                                if n >= 3:
                                    wt(pe, "q_ev", g, n - 2)
                                cs = slice(c * G3, (c + 1) * G3)
                                for k in range(KT):
                                    last = passes(banks[5 + c][:, :G3], q_hi[:, k, m * P:(m + 1) * P],
                                                  q_lo[:, k, m * P:(m + 1) * P], xT_hi[:, k, cs], xT_lo[:, k, cs],
                                                  k == 0, k == KT - 1)
                                inc(last, "qd")
                        wt(pe, "q_ev", g, 6)
                        scores(g, 0)

                    def tile(g, t, fill):
                        if t + 1 < NT:
                            scores(g, t + 1)
                        nk = len(blocks(g, t))
                        fill.upto(done[t] - 4)
                        wt(pe, "ex", g, t + 1)
                        wt(pe, "pt_ev", g, t)
                        for h in range(HA):
                            for b in range(nk):
                                x = (h * nk + b) * P
                                last = nc.tensor.transpose(banks[2 + x // 512][:, x % 512:x % 512 + P],
                                                           sc[t % 2][:, h, (2 - nk + b) * P:(3 - nk + b) * P], ident[:])
                        inc(last, "ptd")
                        fill.slot(t)
                        wt(pe, "pt_ev", g, t + 1)
                        wt(pe, "oe", g, t)
                        for h in range(HA):
                            for b, kt_ in enumerate(blocks(g, t)):
                                last = nc.tensor.matmul(banks[4][:, h * P:(h + 1) * P],
                                                        pT[:, (h * nk + b) * P:(h * nk + b + 1) * P],
                                                        kv2[g % 2][:, kt_, 256 + (h // 2) * P:256 + (h // 2 + 1) * P],
                                                        start=(b == 0), stop=(b == nk - 1))
                        inc(last, "pv")

                    def beta_rest(pe):
                        beta_pe2(pe)
                        beta_over(pe)

                    bias_products(pe)
                    bias_over(pe, False)
                    beta_pe(pe)
                    groups(pe, kv_steps, beta_rest, q_part, tile, 0)

                @block.scalar
                def _(act):
                    nc.scalar.preload_act_table_set("natural_log_exp_and_others")

                    def split_kv(g):
                        act.wait_ge(kv_ld, (g + 1) * 16)
                        wt(act, "kvd", g, 0)
                        inc(nc.scalar.activation(kv_hi[:], kv_raw[:], ACT.Copy), "kv_hi")

                    def split_q(g):
                        act.wait_ge(q_ld, (g + 1) * 16)
                        wt(act, "qd", g, 0)
                        inc(nc.scalar.activation(q_hi[:], q_raw[:], ACT.Copy), "q_hi")

                    def exps(g, t):
                        wt(act, "nm", g, t + 1)
                        nk = len(blocks(g, t))
                        for h in range(HA):
                            x = sc[t % 2][:, h, (2 - nk) * P:]
                            last = nc.scalar.activation(x, x, ACT.Exp, bias=nm[:, t % 2, h:h + 1],
                                                        accum_out=os_[:, t % 2, h, HD:HD + 1])
                        inc(last, "ex")

                    def kv_steps(g):
                        for t in range(NT + 1):
                            yield (t + 1) * KT
                            if t == 0 and g >= 2:
                                act.wait_ge(kvo[g - 2], KVO[g - 2] * 16)
                            wt(act, "pv", max(g - 1, 0), 0)
                            wt(act, "kvd", g, t + 1)
                            dst = kv2[g % 2][:, t] if t < NT else kv_s[:, g]
                            inc(nc.scalar.activation(dst, banks[5 + t % 2][:P if t < NT else NS, :], ACT.Copy), "kv_ev")

                    def q_part(g):
                        wt(act, "sd", g, 0)
                        wt(act, "qs", g, 0)
                        for n in range(6):
                            wt(act, "qd", g, n + 1)
                            c = n % 3
                            inc(nc.scalar.activation(qT[:, n // 3, c * G3:(c + 1) * G3], banks[5 + c][:, :G3],
                                                     ACT.Copy), "q_ev")
                            if n == 3 and g + 1 < NG:
                                split_kv(g + 1)
                        wt(act, "q_ev", g, 6)
                        inc(nc.scalar.activation(qT_s[:, g], qT[:, :, L:], ACT.Copy), "qs")
                        exps(g, 0)

                    def tile(g, t, fill):
                        if t == SPLIT_Q and g + 1 < NG:
                            split_q(g + 1)
                        if t + 1 < NT:
                            exps(g, t + 1)
                        fill.slot(t)
                        wt(act, "ptd", g, t + 1)
                        nk = len(blocks(g, t))
                        wt(act, "pv", g, t)
                        for b in range(nk):
                            last = nc.scalar.activation(pT[:, 512 * b:512 * b + 512], banks[2 + b][:], ACT.Copy)
                        inc(last, "pt_ev")

                    def beta_rest(act):
                        split_q(0)
                        beta_act2(act)
                        beta_over(act)
                        bias_over(act, True)

                    beta_act(act)
                    split_kv(0)
                    groups(act, kv_steps, beta_rest, q_part, tile, 1)

                @block.vector
                def _(v):
                    def out_copy(g, t):
                        wt(v, "pv", g, t + 1)
                        for e in range(2):
                            src = banks[4][:].rearrange("p (m e w) -> p m e w", m=2, e=2)[:, :, e, 64 * e:64 * e + 64]
                            last = nc.vector.tensor_copy(os_[:, t % 2, e::2, :HD], src)
                        inc(last, "oe")

                    def split_kv(g):
                        wt(v, "kv_hi", g, 1)
                        inc(split_lo(v, kv_lo[:], kv_raw[:], kv_hi[:]), "kv_lo")

                    def split_q(g):
                        wt(v, "q_hi", g, 1)
                        inc(split_lo(v, q_lo[:], q_raw[:], q_hi[:]), "q_lo")

                    def kv_steps(g):
                        for t in range(NT):
                            yield (t + 2) * KT + 2
                            wt(v, "ktd", g, t + 1)
                            wt(v, "sd", max(g - 1, 0), 0)
                            inc(nc.vector.tensor_copy(kT2[g % 2][:, :, t * P:(t + 1) * P],
                                                      banks[7][:, :256].rearrange("p (m c) -> p m c", m=2)), "kt_ev")

                    def q_part(g):
                        if g + 1 < NG:
                            split_kv(g + 1)
                        v.wait_ge(bld, (g + 1) * 16)

                    def tile(g, t, fill):
                        if t == SPLIT_Q + 1 and g + 1 < NG:
                            split_q(g + 1)
                        nk = len(blocks(g, t))
                        ks = slice((2 - nk) * P, 2 * P)
                        wt(v, "sd", g, t + 1)
                        wt(v, "ptd", g, max(t - 1, 0))
                        for e in range(2):
                            src = banks[e][:].rearrange("p (h k) -> p h k", h=2)[:, :, ks]
                            inc(nc.vector.scalar_tensor_tensor(sc[t % 2][:, e::2, ks], src, HD ** -0.5,
                                                               bias[:, e::2, ks], ALU.mult, ALU.add), "st")
                        wt(v, "st", g, 2 * t + 2)
                        if g or t >= 2:
                            v.wait_ge(oso[t % 2], (g * NT // 2 + t // 2) * 16)
                        inc(nc.vector.reduce_max(os_[:, t % 2, :, HD + 1], sc[t % 2][:, :, ks], AX.X), "mx")
                        wt(v, "mx", g, t + 1)
                        wt(v, "ex", g, max(t - 1, 0))
                        inc(nc.vector.tensor_scalar(nm[:, t % 2], os_[:, t % 2, :, HD + 1], -1.0, None, ALU.mult), "nm")
                        fill.slot(t)
                        if t:
                            out_copy(g, t - 1)
                        if t == NT - 1:
                            out_copy(g, t)

                    def beta_rest(v):
                        split_q(0)
                        beta_dve2(v)
                        beta_over(v)

                    bias_copies(v)
                    beta_dve(v)
                    split_kv(0)
                    groups(v, kv_steps, beta_rest, q_part, tile, 1)

        def merge_steps(s):
            x = sb(s, "m_x", [P, NG, NT, HA, HS]); top = sb(s, "m_top", [P, NT, HA])
            f = sb(s, "m_f", [P, NG, NT, HA]); z = sb(s, "m_z", [P, NG, NT, HA])
            y = sb(s, "m_y", [P, NT, HA, HD]); y2 = sb(s, "m_y2", [P, NT, HA, HD])
            ld, dv, ac, tr = sem("m_ld"), sem("m_dv"), sem("m_ac"), sem("m_tr")

            def load(sp):
                for g in range(NG):
                    sp.dma_start(x[:, g].rearrange("p t h w -> p t (h w)"),
                                 att_scr[g].rearrange("(t p) w -> p t w", p=P)).then_inc(ld, 16)

            def exps(act):
                act.wait_ge(dv, 3)
                nc.scalar.activation(f[:], f[:], ACT.Exp).then_inc(ac, 1)

            def turn(pe):
                pe.wait_ge(dv, 12)
                for m in range(2):
                    for t in range(NT):
                        last = nc.tensor.transpose(banks[3 + 2 * m + t // 4][:, (t % 4) * P:(t % 4 + 1) * P],
                                                   y[:, t, 2 * m:2 * m + 2].rearrange("p h d -> p (h d)"), ident[:])
                last.then_inc(tr, 1)

            n = [0]

            def merge(v):
                def step(ins):
                    n[0] += 1
                    ins.then_inc(dv, 1)
                    v.wait_ge(dv, n[0])
                v.wait_ge(ld, 48)
                mx = x[:, :, :, :, HD + 1]
                step(nc.vector.tensor_tensor(top[:], mx[:, 0], mx[:, 1], ALU.max))
                step(nc.vector.tensor_tensor(top[:], top[:], mx[:, 2], ALU.max))
                for g in range(NG):
                    last = nc.vector.tensor_tensor(f[:, g], mx[:, g], top[:], ALU.subtract)
                step(last)
                v.wait_ge(ac, 1)
                for g in range(NG):
                    last = nc.vector.tensor_tensor(z[:, g], f[:, g], x[:, g, :, :, HD], ALU.mult)
                step(last)
                step(nc.vector.tensor_tensor(top[:], z[:, 0], z[:, 1], ALU.add))
                step(nc.vector.tensor_tensor(top[:], top[:], z[:, 2], ALU.add))
                step(nc.vector.reciprocal(top[:], top[:]))
                for g in range(NG):
                    last = nc.vector.tensor_tensor(f[:, g], f[:, g], top[:], ALU.mult)
                step(last)
                F4 = [P, NT * HA, HD]

                def part(g):
                    return (x[:, g, :, :, :HD].rearrange("p t h d -> p (t h) d"),
                            f[:, g].rearrange("p t h -> p (t h)").unsqueeze(2).to_broadcast(F4))
                yy, yy2 = y[:].rearrange("p t h d -> p (t h) d"), y2[:].rearrange("p t h d -> p (t h) d")
                nc.vector.tensor_tensor(yy, *part(0), ALU.mult)
                step(nc.vector.tensor_tensor(yy2, *part(1), ALU.mult))
                step(nc.vector.tensor_tensor(yy, yy, yy2, ALU.add))
                step(nc.vector.tensor_tensor(yy2, *part(2), ALU.mult))
                step(nc.vector.tensor_tensor(yy, yy, yy2, ALU.add))

            def take(v):
                v.wait_ge(tr, 1)
                for m in range(2):
                    for b in range(2):
                        last = nc.vector.tensor_copy(oaT[:, m, 512 * b:512 * b + 512], banks[3 + 2 * m + b][:])
                last.then_inc(dv, 1)
                v.wait_ge(dv, n[0] + 1)

            return load, exps, turn, merge, take


        class Chain:

            def __init__(self, eng, sem_):
                self.eng, self.sem, self.n, self.marks = eng, sem_, 0, {}

            def step(self, ins, mark=None):
                self.n += 1
                ins.then_inc(self.sem, 1)
                self.eng.wait_ge(self.sem, self.n)
                if mark:
                    self.marks[mark] = self.n

            def reached(self, eng, mark):
                eng.wait_ge(self.sem, self.marks[mark])

        def sample_attention_block():
            with ExitStack() as s, nc.Block() as block:
                merge_load, merge_exps, merge_turn, merge, merge_take = merge_steps(s)
                W5 = 2 * HA * HD
                R = NS * HA
                NKEY = (P, P, 64)
                cache = [sb(s, f"sa_cache{g}", [P, NS, W5]) for g in range(NG)]
                q_row = sb(s, "sa_qrow", [NS, NG, HA * HD]); sel = sb(s, "sa_sel", [NS, NS, P])
                prod = sb(s, "sa_prod", [P, NS, HA * HD]); sc = sb(s, "sa_sc", [P, NG, R])
                S = sb(s, "sa_S", [R, NG, P + 1]); bias = sb(s, "sa_bias", [R, NG, P + 1])
                self_r = sb(s, "sa_selfr", [R, NG]); pself_r = sb(s, "sa_pselfr", [R, NG])
                table = sb(s, "sa_table", [33, NG * HA]); trep = sb(s, "sa_trep", [33, NG, NS, HA])
                onehot = sb(s, "sa_onehot", [33, NG, P + 1])
                sprod = sb(s, "sa_sprod", [NS, NG, HA * HD]); self_ = sb(s, "sa_self", [NS, NG, HA])
                by_row = sb(s, "sa_by_row", [NS, NS, HA])
                of_row = sb(s, "sa_of_row", [R, NS]); pdiag = sb(s, "sa_pdiag", [R, NG, R])
                pd = sb(s, "sa_pd", [NS, NG, 2, NS, 2])
                st = sb(s, "sa_st", [R, 4]); pT = sb(s, "sa_pT", [P, NG, R])
                cache_ld = [sem("sa_cache_ld") for _ in range(NG)]
                const_ld, moved, expd = sem("sa_const"), sem("sa_moved"), sem("sa_exp")
                q_turned, q_spread, sc_turned = sem("sa_qt"), sem("sa_qs"), sem("sa_sct")
                p_turned, pv_done, dve = sem("sa_pt"), sem("sa_pv"), sem("sa_dve")
                scr = dram("sa_scr", (NS, NG, HA))
                self_spread = sem("sa_self_spread")
                ch = [None]

                @block.vector
                def _(v):
                    c = ch[0] = Chain(v, dve)
                    v.wait_ge(const_ld, 48)
                    c.step(nc.vector.tensor_copy(sel[:], ident[:NS, :NS].unsqueeze(2).to_broadcast([NS, NS, P])))
                    nc.vector.tensor_copy(by_row[:], ident[:NS, :NS].unsqueeze(2).to_broadcast([NS, NS, HA]))
                    for g in range(NG):
                        last = nc.vector.tensor_copy(trep[:, g], table[:, g * HA:(g + 1) * HA].unsqueeze(1)
                                                     .to_broadcast([33, NS, HA]))
                    c.step(last)
                    v.wait_ge(q_turned, 1)
                    nc.vector.memset(S[:], 0.0)
                    nc.vector.tensor_copy(q_row[:, 0:2].rearrange("p g c -> p (g c)"), banks[0][:NS, :])
                    c.step(nc.vector.tensor_copy(q_row[:, 2], banks[1][:NS, :256]), "q_row")
                    c.step(nc.vector.tensor_tensor(sprod[:], q_row[:], kv_s[:, :, :256], ALU.mult))
                    c.step(nc.vector.reduce_sum(self_[:].rearrange("p g h -> p (g h)"),
                                                sprod[:].rearrange("p g (h d) -> p (g h) d", h=HA), AX.X), "self")
                    for g in range(NG):
                        k = NKEY[g]
                        v.wait_ge(cache_ld[g], 16)
                        v.wait_ge(q_spread, 1 + g)
                        for b in range(4):
                            last = nc.vector.tensor_tensor(
                                prod[:k, 2 * b:2 * b + 2], cache[g][:k, 2 * b:2 * b + 2, :256],
                                banks[2 + b][:k, :].rearrange("p (b c) -> p b c", b=2), ALU.mult)
                        c.step(last, f"prod{g}")
                        c.step(nc.vector.reduce_sum(sc[:k, g], prod[:k].rearrange("p b (h d) -> p (b h) d", h=HA),
                                                    AX.X), "sc")
                    v.wait_ge(sc_turned, 1)
                    v.wait_ge(moved, 16 * 9)
                    nc.vector.tensor_copy(of_row[:], banks[7][:R, 400:400 + NS])
                    for g in range(NG):
                        nc.vector.tensor_copy(S[:, g, :NKEY[g]], banks[6][:R, g * P:g * P + NKEY[g]])
                        nc.vector.tensor_copy(S[:, g, P:], self_r[:, g:g + 1])
                        last = nc.vector.tensor_copy(bias[:, g], banks[7][:R, g * 132:g * 132 + P + 1])
                    c.step(last)
                    c.step(nc.vector.scalar_tensor_tensor(S[:], S[:], HD ** -0.5, bias[:], ALU.mult, ALU.add))
                    c.step(nc.vector.reduce_max(st[:, 0:1], S[:].rearrange("p g c -> p (g c)"), AX.X))
                    c.step(nc.vector.tensor_scalar(st[:, 1:2], st[:, 0:1], -1.0, None, ALU.mult), "max")
                    v.wait_ge(expd, 1)
                    c.step(nc.vector.reciprocal(st[:, 3:4], st[:, 2:3]))
                    c.step(nc.vector.tensor_scalar(S[:], S[:], st[:, 3:4], None, ALU.mult))
                    c.step(nc.vector.tensor_copy(pself_r[:], S[:, :, P]), "probs")
                    c.step(nc.vector.tensor_tensor(pdiag[:], ident[:R, :R].unsqueeze(1).to_broadcast([R, NG, R]),
                                                   pself_r[:].unsqueeze(2).to_broadcast([R, NG, R]), ALU.mult), "pdiag")
                    v.wait_ge(p_turned, 1)
                    for g in range(NG):
                        last = nc.vector.tensor_copy(pT[:NKEY[g], g], banks[0][:NKEY[g], g * R:(g + 1) * R])
                    v.wait_ge(self_spread, 1)
                    for g in range(NG):
                        src = banks[7][:NS, g * R:(g + 1) * R].rearrange("p (b m e) -> p m b e", m=2, e=2)
                        last = nc.vector.tensor_copy(pd[:, g], src)
                    c.step(last, "pT")
                    merge(v)
                    v.wait_ge(pv_done, 1)
                    for m in range(2):
                        for e in range(2):
                            rows = slice(64 * e, 64 * e + 64)
                            src = banks[1 + m][rows, :2 * NS].rearrange("p (b e) -> p b e", e=2)[:, :, e]
                            last = nc.vector.tensor_copy(oaT[rows, m, L:], src)
                    c.step(last)
                    merge_take(v)
                c = ch[0]

                @block.sync
                def _(sp):
                    sp.dma_start(table[:32], a["rel_bias"]).then_inc(const_ld, 16)
                    sp.dma_start(table[32:33], a["c_ones"][0:1, :NG * HA]).then_inc(const_ld, 16)
                    sp.dma_start(onehot[:], a["c_onehot_s"]).then_inc(const_ld, 16)
                    for g, (name, step) in enumerate((("cache_kv_w128", 1), ("cache_kv_w512", 4), ("cache_kv_w2048", 16))):
                        rows = a[name][0].rearrange("b r s h d -> r b (s h d)")[::step]
                        sp.dma_start(cache[g][:NKEY[g]], rows).then_inc(cache_ld[g], 16)
                    merge_load(sp)
                    with nc.allow_non_contiguous_dma(reason="96 scores change partitions"):
                        c.reached(sp, "self")
                        sp.dma_start(scr[:], self_[:]).then_inc(moved, 16)
                        sp.wait_ge(moved, 16)
                        for b in range(NS):
                            sp.dma_start(self_r[HA * b:HA * b + HA], scr[b].rearrange("g h -> h g")).then_inc(moved, 16)
                        sp.wait_ge(moved, 16 * 9)

                @block.tensor
                def _(pe):
                    for g in range(NG):
                        for m in range(2):
                            x = (2 * g + m) * P
                            last = nc.tensor.transpose(banks[x // 512][:NS, x % 512:x % 512 + P], qT_s[:, g, m], ident[:])
                    last.then_inc(q_turned, 1)
                    c.reached(pe, "q_row")
                    for g in range(NG):
                        if g:
                            c.reached(pe, f"prod{g - 1}")
                        for b in range(NS):
                            last = nc.tensor.matmul(banks[2 + b // 2][:, (b % 2) * 256:(b % 2) * 256 + 256], sel[:, b],
                                                    q_row[:, g], start=True, stop=True)
                        last.then_inc(q_spread, 1)
                    c.reached(pe, "sc")
                    for g in range(NG):
                        k = NKEY[g]
                        nc.tensor.transpose(banks[6][:R, g * P:g * P + k], sc[:k, g], ident[:k, :k])
                        last = nc.tensor.matmul(banks[7][:R, g * 132:g * 132 + P + 1],
                                                trep[:, g].rearrange("p b h -> p (b h)"), onehot[:, g],
                                                start=True, stop=True)
                    nc.tensor.transpose(banks[7][:R, 400:400 + NS], by_row[:].rearrange("p b h -> p (b h)"),
                                        ident[:NS, :NS]).then_inc(sc_turned, 1)
                    c.reached(pe, "probs")
                    for g in range(NG):
                        k = NKEY[g]
                        last = nc.tensor.transpose(banks[0][:k, g * R:(g + 1) * R], S[:, g, :k], ident[:R, :R])
                    last.then_inc(p_turned, 1)
                    c.reached(pe, "pdiag")
                    nc.tensor.matmul(banks[7][:NS, :NG * R], of_row[:], pdiag[:].rearrange("p g r -> p (g r)"),
                                     start=True, stop=True).then_inc(self_spread, 1)
                    c.reached(pe, "pT")
                    for m in range(2):
                        bank = banks[1 + m]
                        for g in range(NG):
                            nc.tensor.matmul(bank[:, :2 * NS], kv_s[:, g, 256 + m * P:256 + (m + 1) * P],
                                             pd[:, g, m].rearrange("p b e -> p (b e)"), start=(g == 0), stop=False,
                                             skip_group_check=True)
                        for b in range(NS):
                            for g in range(NG):
                                k = NKEY[g]
                                last = nc.tensor.matmul(bank[:, 2 * b:2 * b + 2],
                                                        cache[g][:k, b, 256 + m * P:256 + (m + 1) * P],
                                                        pT[:k, g, HA * b + 2 * m:HA * b + 2 * m + 2], start=False,
                                                        stop=(b == NS - 1 and g == NG - 1), skip_group_check=True)
                    last.then_inc(pv_done, 1)
                    merge_turn(pe)

                @block.scalar
                def _(act):
                    nc.scalar.preload_act_table_set("natural_log_exp_and_others")
                    c.reached(act, "max")
                    nc.scalar.activation(S[:], S[:], ACT.Exp, bias=st[:, 1:2], accum_out=st[:, 2:3]).then_inc(expd, 1)
                    merge_exps(act)

        def sample_delta_block():
            with ExitStack() as s, nc.Block() as block:
                U = HB * NS
                S0 = sb(s, "sd_S0", [P, U, P])
                sq = sb(s, "sd_sq", [P, 2, U]); r = sb(s, "sd_r", [P, 2, U]); kq = sb(s, "sd_kq", [P, U, 2])
                skq = sb(s, "sd_skq", [P, U, 2]); qk = sb(s, "sd_qk", [P, U]); vn = sb(s, "sd_vn", [P, U])
                ov = sb(s, "sd_ov", [P, U]); t1 = sb(s, "sd_t1", [P, U]); k_c = sb(s, "sd_kc", [P, U])
                vn_r = sb(s, "sd_vnr", [U, P]); k_r = sb(s, "sd_kr", [U, P])
                blk = [sb(s, f"sd_blk{j}", [U, 4, P]) for j in range(2)]
                ld, norm_mm, lnexp, sk_mm, qk_mm, turned, rms_mm, rank1, blkd, st_out = (
                    sem("sd_" + x) for x in ("ld", "norm", "lnexp", "sk", "qk", "tr", "rms", "r1", "blk", "out"))
                dve = sem("sd_dve")
                add_done = sem("sd_add")
                eps2 = sb(s, "sd_eps", [P, 1])
                rows = sb(s, "co_rows", [3 + NS, 3 * D])
                conv_turned, conv_rows, conv_out = sem("co_tr"), sem("co_cp"), sem("co_out")
                buf = [sb(s, f"so_buf{j}", [P, L]) for j in range(4)]
                ob_ld = [sem("so_ld") for _ in range(4)]
                hi_d, lo_d = sem("so_hi"), sem("so_lo")
                ch = [None]
                flat = lambda x: x.rearrange("p h b -> p (h b)")
                q_, k_, v_, z_ = (flat(samp[:, n]) for n in range(4))
                eg, beta = flat(eg_s[:, 0]), flat(eg_s[:, 1])

                @block.vector
                def _(v):
                    c = ch[0] = Chain(v, dve)
                    nc.vector.memset(eps2[:], EPS)
                    v.wait_ge(conv_turned, 1)
                    for b in range(6):
                        last = nc.vector.tensor_copy(rows[:, 512 * b:512 * b + 512], banks[2 + b][:3 + NS, :])
                    last.then_inc(conv_rows, 1)
                    nc.vector.tensor_tensor(sq[:, 0], q_, q_, ALU.mult)
                    c.step(nc.vector.tensor_tensor(sq[:, 1], k_, k_, ALU.mult), "sq")
                    v.wait_ge(lnexp, 2)
                    nc.vector.scalar_tensor_tensor(kq[:, :, 1], q_, DK ** -0.5, r[:, 0], ALU.mult, ALU.mult)
                    nc.vector.tensor_tensor(k_c[:], k_, r[:, 1], ALU.mult)
                    c.step(nc.vector.tensor_tensor(kq[:, :, 0], k_, r[:, 1], ALU.mult), "kq")
                    c.step(nc.vector.tensor_tensor(sq[:, 0], kq[:, :, 0], kq[:, :, 1], ALU.mult), "qk")
                    v.wait_ge(hi_d, 1)
                    split_lo(v, oa_lo[:], oaT[:], oa_hi[:]).then_inc(lo_d, 1)
                    for h in range(HB):
                        v.wait_ge(hi_d, h + 2)
                        split_lo(v, xT_lo[:, h, :L], buf[h % 4][:], xT_hi[:, h, :L]).then_inc(lo_d, 1)
                    v.wait_ge(qk_mm, 1)
                    nc.vector.tensor_copy(qk[:], banks[1][:, :U])
                    for h in range(HB):
                        v.wait_ge(sk_mm, h + 1)
                        hs_ = slice(h * NS, (h + 1) * NS)
                        decay = nc.vector.tensor_tensor(S0[:, hs_], S0[:, hs_],
                                                        eg[:, hs_].unsqueeze(2).to_broadcast([P, NS, P]), ALU.mult)
                    c.step(decay)
                    c.step(nc.vector.tensor_copy(skq[:].rearrange("p u e -> p (u e)"), banks[2][:, :2 * U]))
                    c.step(nc.vector.tensor_tensor(t1[:], skq[:, :, 0], eg, ALU.mult))
                    c.step(nc.vector.tensor_tensor(t1[:], v_, t1[:], ALU.subtract))
                    c.step(nc.vector.tensor_tensor(vn[:], t1[:], beta, ALU.mult), "vn")
                    nc.vector.tensor_tensor(ov[:], skq[:, :, 1], eg, ALU.mult)
                    c.step(nc.vector.tensor_tensor(t1[:], vn[:], qk[:], ALU.mult))
                    c.step(nc.vector.tensor_tensor(ov[:], ov[:], t1[:], ALU.add))
                    c.step(nc.vector.tensor_tensor(sq[:, 1], ov[:], ov[:], ALU.mult), "o2")
                    v.wait_ge(lnexp, 4)
                    c.step(nc.vector.tensor_tensor(ov[:], ov[:], r[:, 0], ALU.mult))
                    c.step(nc.vector.scalar_tensor_tensor(flat(ob_s[:]), ov[:], norm_dv[:], z_, ALU.mult, ALU.mult),
                           "ob_s")
                    v.wait_ge(turned, 1)
                    nc.vector.tensor_copy(vn_r[:], banks[3][:U, :P])
                    c.step(nc.vector.tensor_copy(k_r[:], banks[3][:U, P:2 * P]))
                    v.wait_ge(hi_d, HB + 2)
                    split_lo(v, xT_lo[:, :, L:], ob_s[:], xT_hi[:, :, L:]).then_inc(lo_d, 1)
                    for n in range(U // 4):
                        if n >= 2:
                            v.wait_ge(rank1, n - 1)
                        nc.vector.tensor_tensor(blk[n % 2][:], vn_r[:].unsqueeze(1).to_broadcast([U, 4, P]),
                                                ident[:U, 4 * n:4 * n + 4].unsqueeze(2).to_broadcast([U, 4, P]),
                                                ALU.mult).then_inc(blkd, 1)
                        if n:
                            v.wait_ge(rank1, n)
                            nc.vector.tensor_tensor(S0[:, 4 * n - 4:4 * n], S0[:, 4 * n - 4:4 * n],
                                                    banks[4 + (n - 1) % 2][:].rearrange("p (u c) -> p u c", u=4),
                                                    ALU.add).then_inc(add_done, 1)
                    n = U // 4
                    v.wait_ge(rank1, n)
                    nc.vector.tensor_tensor(S0[:, 4 * n - 4:4 * n], S0[:, 4 * n - 4:4 * n],
                                            banks[4 + (n - 1) % 2][:].rearrange("p (u c) -> p u c", u=4),
                                            ALU.add).then_inc(add_done, 1)
                c = ch[0]

                @block.sync
                def _(sp):
                    for h in range(HB):
                        sp.dma_start(S0[:, h * NS:(h + 1) * NS],
                                     a["state_delta"][0, :, h].rearrange("b k v -> k b v")).then_inc(ld, 16)
                    for h in range(HB):
                        if h >= 4:
                            sp.wait_ge(lo_d, h - 2)
                        sp.dma_start(buf[h % 4][:], ob_scr[h, :, :L]).then_inc(ob_ld[h % 4], 16)
                    for h in range(HB):
                        sp.wait_ge(add_done, 2 * h + 2)
                        sp.dma_start(o["delta_s"][0, :, h].rearrange("b k v -> k b v"),
                                     S0[:, h * NS:(h + 1) * NS]).then_inc(st_out, 16)
                    sp.wait_ge(st_out, HB * 16)

                @block.tensor
                def _(pe):
                    for k in range(24):
                        last = nc.tensor.transpose(banks[2 + k // 4][:3 + NS, (k % 4) * P:(k % 4 + 1) * P],
                                                   conv_new[:, k], ident[:])
                    last.then_inc(conv_turned, 1)
                    c.reached(pe, "sq")
                    nc.tensor.matmul(banks[0][:, :2 * U], ident_ones[:], sq[:].rearrange("p n u -> p (n u)"),
                                     start=True, stop=True).then_inc(norm_mm, 1)
                    c.reached(pe, "kq")
                    c.reached(pe, "qk")
                    nc.tensor.matmul(banks[1][:, :U], ident_ones[:], sq[:, 0], start=True, stop=True).then_inc(qk_mm, 1)
                    pe.wait_ge(ld, HB * 16)
                    pe.wait_ge(conv_rows, 1)
                    for u in range(U):
                        last = nc.tensor.matmul(banks[2][:, 2 * u:2 * u + 2], S0[:, u], kq[:, u], start=True, stop=True)
                        if u % NS == NS - 1:
                            last.then_inc(sk_mm, 1)
                    c.reached(pe, "vn")
                    nc.tensor.transpose(banks[3][:U, :P], vn[:], ident[:])
                    nc.tensor.transpose(banks[3][:U, P:2 * P], k_c[:], ident[:]).then_inc(turned, 1)
                    c.reached(pe, "o2")
                    nc.tensor.matmul(banks[6][:, :U], ident_ones[:], sq[:, 1], start=True, stop=True).then_inc(rms_mm, 1)
                    for n in range(U // 4):
                        pe.wait_ge(blkd, n + 1)
                        if n >= 2:
                            pe.wait_ge(add_done, n - 1)
                        nc.tensor.matmul(banks[4 + n % 2][:], k_r[:], blk[n % 2][:].rearrange("p u c -> p (u c)"),
                                         start=True, stop=True).then_inc(rank1, 1)

                @block.scalar
                def _(act):
                    nc.scalar.preload_act_table_set("natural_log_exp_and_others")
                    act.wait_ge(norm_mm, 1)
                    nc.scalar.activation(r[:].rearrange("p n u -> p (n u)"), banks[0][:, :2 * U], ACT.Ln,
                                         bias=eps2[:]).then_inc(lnexp, 1)
                    act.wait_ge(lnexp, 1)
                    nc.scalar.activation(r[:], r[:], ACT.Exp, scale=-0.5).then_inc(lnexp, 1)
                    act.dma_start(o["conv_s"][0, :, 0:2], a["state_conv"][0, :, 1:3]).then_inc(conv_out, 16)
                    act.wait_ge(conv_rows, 1)
                    act.dma_start(o["conv_p"][0, 0], rows[:3]).then_inc(conv_out, 16)
                    act.dma_start(o["conv_s"][0, :, 2], rows[3:]).then_inc(conv_out, 16)
                    split_weights_hi(act, oa_hi[:], oaT[:]).then_inc(hi_d, 1)
                    for h in range(HB):
                        act.wait_ge(ob_ld[h % 4], 16 * (h // 4 + 1))
                        split_weights_hi(act, xT_hi[:, h, :L], buf[h % 4][:]).then_inc(hi_d, 1)
                    act.wait_ge(rms_mm, 1)
                    nc.scalar.activation(r[:, 0], banks[6][:, :U], ACT.Ln, scale=1.0 / DK, bias=eps2[:]).then_inc(lnexp, 1)
                    act.wait_ge(lnexp, 3)
                    nc.scalar.activation(r[:, 0], r[:, 0], ACT.Exp, scale=-0.5).then_inc(lnexp, 1)
                    c.reached(act, "ob_s")
                    split_weights_hi(act, xT_hi[:, :, L:], ob_s[:]).then_inc(hi_d, 1)
                    act.wait_ge(conv_out, 48)

        def pair_block(name, turns, nk_a, rhs_a, rhs_b, w_a, w_b, gates, out_scr):
            nk = nk_a + KT
            with ExitStack() as s, nc.Block() as block:
                raw = [sb(s, f"{name}_raw{j}", [P, nk, P]) for j in range(2)]
                hi = [sb(s, f"{name}_hi{j}", [P, nk, P], FR) for j in range(2)]
                lo = [sb(s, f"{name}_lo{j}", [P, nk, P], FR) for j in range(2)]
                ta = [sb(s, f"{name}_ta{j}", [P, T]) for j in range(2)]
                tb = [sb(s, f"{name}_tb{j}", [P, T]) for j in range(2)] if gates else ta
                y = [sb(s, f"{name}_y{j}", [P, T]) for j in range(2)]
                y2 = [sb(s, f"{name}_y2{j}", [P, T]) for j in range(2)] if gates else ta
                loaded = [sem("p_loaded") for _ in range(2)]; gate_in = [sem("p_gates") for _ in range(2)]
                hi_done = [sem("p_hi") for _ in range(2)]; lo_done = [sem("p_lo") for _ in range(2)]
                group = [sem("p_group") for _ in range(2)]; tile_done = [sem("p_tile") for _ in range(2)]
                drained = [sem("p_drained") for _ in range(3)]
                joined = [sem("p_joined") for _ in range(2)]; stored = [sem("p_stored") for _ in range(2)]
                tanh_done, silu_done = sem("p_tanh"), sem("p_silu")
                cs = [slice(c * G3, (c + 1) * G3) for c in range(3)]

                def turns_of(eng, split, join):
                    split(eng, 0, 0)
                    with eng.Fori(0, turns // 2 - 1) as i:
                        split(eng, i, 1)
                        join(eng, i, 0)
                        split(eng, i + 1, 0)
                        join(eng, i, 1)
                    split(eng, turns // 2 - 1, 1)
                    join(eng, turns // 2 - 1, 0)
                    join(eng, turns // 2 - 1, 1)

                def group_done(eng, i, j, c):
                    if c < 2:
                        eng.wait_ge(group[c], 2 * i + j + 1)
                    else:
                        eng.wait_ge(tile_done[j], 1 + i + 1)

                @block.sync
                def _(sp):
                    with sp.Fori(0, turns // 2) as i:
                        for j in range(2):
                            n = 2 * i + j
                            sp.wait_ge(lo_done[j], 1 + i)
                            sp.dma_start(raw[j][:, :nk_a], w_a(n)).then_inc(loaded[j], 16)
                            sp.dma_start(raw[j][:, nk_a:], w_b(n)).then_inc(loaded[j], 16)
                            if gates:
                                sp.wait_ge(joined[j], 1 + i)
                                for g, dst in ((0, ta[j]), (1, tb[j])):
                                    sp.dma_start(dst[:], gate_scr[g, bass.ds(n, 1)].rearrange("o p t -> (o p) t")
                                                 ).then_inc(gate_in[j], 16)

                @block.tensor
                def _(pe):
                    start(pe, 1, *tile_done)
                    with pe.Fori(0, turns // 2) as i:
                        for j in range(2):
                            n = 2 * i + j
                            pe.wait_ge(lo_done[j], 1 + i + 1)
                            for c in range(3):
                                pe.wait_ge(drained[c], 1 + n)
                                for k in range(nk_a):
                                    passes(banks[c][:, :G3], hi[j][:, k], lo[j][:, k], rhs_a[0][:, k, cs[c]],
                                           rhs_a[1][:, k, cs[c]], k == 0, k == nk_a - 1)
                                for k in range(KT):
                                    last = passes(banks[3 + c][:, :G3], hi[j][:, nk_a + k], lo[j][:, nk_a + k],
                                                  rhs_b[0][:, k, cs[c]], rhs_b[1][:, k, cs[c]], k == 0, k == KT - 1)
                                last.then_inc(group[c] if c < 2 else tile_done[j], 1)

                def act_split(act, i, j):
                    act.wait_ge(tile_done[j], 1 + i)
                    act.wait_ge(loaded[j], 32 * i + 32)
                    nc.scalar.activation(hi[j][:], raw[j][:], ACT.Copy).then_inc(hi_done[j], 1)

                def act_join(act, i, j):
                    if not gates:
                        act.wait_ge(joined[j], 1 + i)
                        for c in range(3):
                            group_done(act, i, j, c)
                            nc.scalar.activation(ta[j][:, cs[c]], banks[c][:, :G3], ACT.Tanh, scale=0.5
                                                 ).then_inc(tanh_done, 1)
                    act.wait_ge(joined[j], 1 + i + 1)
                    act.dma_start(out_scr[bass.ds(2 * i + j, 1)].rearrange("o p t -> (o p) t"), y[j][:]
                                  ).then_inc(stored[j], 16)

                @block.scalar
                def _(act):
                    nc.scalar.preload_act_table(ACT.Tanh)
                    start(act, 16, *stored)
                    turns_of(act, act_split, act_join)
                    for j in range(2):
                        act.wait_ge(stored[j], 16 + 16 * (turns // 2))

                def dve_split(v, i, j):
                    v.wait_ge(hi_done[j], i + 1)
                    split_lo(v, lo[j][:], raw[j][:], hi[j][:]).then_inc(lo_done[j], 1)

                def dve_join(v, i, j):
                    n = 2 * i + j
                    v.wait_ge(stored[j], 16 + 16 * i)
                    if gates:
                        v.wait_ge(gate_in[j], 32 * i + 32)
                    for c in range(3):
                        if gates:
                            group_done(v, i, j, c)
                            nc.vector.tensor_tensor(y[j][:, cs[c]], banks[c][:, :G3], ta[j][:, cs[c]], ALU.mult)
                            nc.vector.tensor_tensor(y2[j][:, cs[c]], banks[3 + c][:, :G3], tb[j][:, cs[c]],
                                                    ALU.mult).then_inc(drained[c], 1)
                        else:
                            v.wait_ge(tanh_done, 3 * n + c + 1)
                            nc.vector.scalar_tensor_tensor(y[j][:, cs[c]], ta[j][:, cs[c]], 1.0, banks[c][:, :G3],
                                                           ALU.add, ALU.mult).then_inc(silu_done, 1)
                            v.wait_ge(silu_done, 3 * n + c + 1)
                            last = nc.vector.scalar_tensor_tensor(y[j][:, cs[c]], y[j][:, cs[c]], 0.5,
                                                                  banks[3 + c][:, :G3], ALU.mult, ALU.mult
                                                                  ).then_inc(drained[c], 1)
                    v.wait_ge(drained[2], 1 + n + 1)
                    if gates:
                        nc.vector.tensor_tensor(y[j][:], y[j][:], y2[j][:], ALU.add).then_inc(joined[j], 1)
                    else:
                        nc.vector.tensor_copy(mark[:], mark[:]).then_inc(joined[j], 1)

                mark = sb(s, f"{name}_mark", [P, 1])
                marked = sem("p_mark")

                @block.vector
                def _(v):
                    start(v, 1, *lo_done, *joined, *drained)
                    nc.vector.memset(mark[:], 0.0).then_inc(marked, 1)
                    v.wait_ge(marked, 1)
                    turns_of(v, dve_split, dve_join)

        def row_block(name, src_scr, nk, chunks, weight, norm_w, resid, out, next_norm=None):
            kc = nk // chunks
            kp = 1
            pieces = kc // kp
            with ExitStack() as s, nc.Block() as block:
                slots = 4
                w_raw = [sb(s, f"{name}_wr{j}", [P, kp, D]) for j in range(slots)]
                w_hi = sb(s, f"{name}_wh", [P, kc, D], FR); w_lo = sb(s, f"{name}_wl", [P, kc, D], FR)
                st_raw = [sb(s, f"{name}_sr{j}", [P, kc, P]) for j in range(2)]
                st_hi = [sb(s, f"{name}_sh{j}", [P, kc, P], FR) for j in range(2)]
                st_lo = [sb(s, f"{name}_sl{j}", [P, kc, P], FR) for j in range(2)]
                part = sb(s, f"{name}_part", [P, NT + 1, D]) if chunks > 1 else None
                y = [sb(s, f"{name}_y{j}", [P, D]) for j in range(2)]
                xr = [sb(s, f"{name}_x{j}", [P, D]) for j in range(2)]
                junk = sb(s, f"{name}_junk", [P, D])
                wrow = sb(s, f"{name}_wrow", [P, D]); stat = sb(s, f"{name}_stat", [P, 2, 4])
                w_ld = [sem("r_wld") for _ in range(slots)]; w_hid, w_lod = sem("r_whi"), sem("r_wlo")
                st_ld = [sem("r_stld") for _ in range(2)]
                hi_d = [sem("r_hi") for _ in range(2)]; lo_d = [sem("r_lo") for _ in range(2)]
                prod = [sem("r_prod") for _ in range(2)]; drained = [sem("r_drained") for _ in range(2)]
                xld = [sem("r_xld") for _ in range(2)]; const = sem("r_const")
                normed = [sem("r_norm") for _ in range(2)]
                stats = [sem("r_stats") for _ in range(2)]; stored = [sem("r_stored") for _ in range(2)]
                eps_set = sem("r_eps")
                if next_norm is not None:
                    next_rows, next_w = w_raw[:2], w_raw[slots - 1]
                    next_stat = sb(s, f"{name}_stat2", [P, 2, 4])
                    next_const, next_stats = sem("n_const"), [sem("n_stats") for _ in range(2)]
                    next_made, next_turned = [sem("n_made") for _ in range(2)], [sem("n_turned") for _ in range(2)]
                    next_hi, next_lo = [sem("n_hi") for _ in range(2)], [sem("n_lo") for _ in range(2)]
                USES = (NT // 2 + 1, NT // 2)
                src = src_scr.rearrange("k p t -> p k t")
                wv = weight.rearrange("(k p) n -> p k n", p=P)

                def nothing(*_):
                    pass

                def tiles_of(eng, q, stage, weights, finish, turn_in=nothing):
                    stage(eng, q, 0, 0, P)
                    stage(eng, q, 0, 1, P)
                    weights(eng, q)
                    stage(eng, q, 1, 0, P)
                    finish(eng, q, 0, 0, P)
                    finish(eng, q, 0, 1, P)
                    with eng.Fori(1, NT // 2 - 1) as i:
                        stage(eng, q, i, 1, P)
                        finish(eng, q, i, 0, P)
                        turn_in(eng, i - 1, 0, P)
                        stage(eng, q, i + 1, 0, P)
                        finish(eng, q, i, 1, P)
                        turn_in(eng, i - 1, 1, P)
                    i = NT // 2 - 1
                    stage(eng, q, i, 1, P)
                    finish(eng, q, i, 0, P)
                    turn_in(eng, i - 1, 0, P)
                    stage(eng, q, i + 1, 0, NS)
                    finish(eng, q, i, 1, P)
                    turn_in(eng, i - 1, 1, P)
                    finish(eng, q, i + 1, 0, NS)
                    turn_in(eng, i, 0, P)
                    turn_in(eng, i, 1, P)
                    turn_in(eng, i + 1, 0, NS)

                def use(q, i, j):
                    return q * USES[j] + i

                @block.sync
                def _(sp):
                    def load(sp, q, i, j, n):
                        sp.wait_ge(lo_d[j], 1 + use(q, i, j))
                        sp.dma_start(st_raw[j][:, :, :n], src[:, q * kc:(q + 1) * kc, bass.ds((2 * i + j) * P, n)]
                                     ).then_inc(st_ld[j], 16)
                        if q == chunks - 1:
                            sp.wait_ge(normed[j], 1 + 2 * i)
                            sp.dma_start(xr[j][:n], resid(2 * i + j)).then_inc(xld[j], 16)

                    def load_weights(sp, q):
                        for n in range(pieces):
                            m = q * pieces + n
                            if m >= slots:
                                sp.wait_ge(w_lod, m - slots + 1)
                            sp.dma_start(w_raw[m % slots][:], wv[:, q * kc + n * kp:q * kc + (n + 1) * kp]
                                         ).then_inc(w_ld[m % slots], 16)

                        if q == 0:
                            sp.dma_start(wrow[:], norm_w.partition_broadcast(P)).then_inc(const, 16)
                        if next_norm is not None:
                            sp.wait_ge(w_lod, pieces)
                            sp.dma_start(next_w[:, 0], next_norm.partition_broadcast(P)).then_inc(next_const, 16)

                    for q in range(chunks):
                        tiles_of(sp, q, load, load_weights, nothing)

                @block.tensor
                def _(pe):
                    def product(pe, q, i, j, n):
                        pe.wait_ge(lo_d[j], 1 + use(q, i, j) + 1)
                        pe.wait_ge(drained[j], 1 + use(q, i, j))
                        for half in range(2):
                            for k in range(kc):
                                c = slice(half * 512, half * 512 + 512)
                                last = passes(banks[2 * j + half][:n, :], st_hi[j][:, k, :n], st_lo[j][:, k, :n],
                                              w_hi[:, k, c], w_lo[:, k, c], k == 0, k == kc - 1)
                        last.then_inc(prod[j], 1)

                    def first_two(pe, q):
                        for j in range(2):
                            pe.wait_ge(lo_d[j], 1 + use(q, 0, j) + 1)
                            pe.wait_ge(drained[j], 1 + use(q, 0, j))
                        for k in range(kc):
                            pe.wait_ge(w_lod, q * pieces + k // kp + 1)
                            for j in range(2):
                                for half in range(2):
                                    c = slice(half * 512, half * 512 + 512)
                                    last = passes(banks[2 * j + half][:], st_hi[j][:, k], st_lo[j][:, k],
                                                  w_hi[:, k, c], w_lo[:, k, c], k == 0, k == kc - 1)
                                if k == kc - 1:
                                    last.then_inc(prod[j], 1)

                    def turn(pe, i, j, n):
                        if next_norm is None:
                            return
                        pe.wait_ge(next_made[j], 1 + i + 1)
                        pe.wait_ge(next_lo[j], 1 + 2 * i)
                        for k in range(KT):
                            last = nc.tensor.transpose(banks[4 + 2 * j + k // 4][:, (k % 4) * P:(k % 4) * P + n],
                                                       next_rows[j][:n, 0, k * P:(k + 1) * P], ident[:n, :n])
                        last.then_inc(next_turned[j], 1)

                    start(pe, 1, *prod)
                    if next_norm is not None:
                        start(pe, 1, *next_turned)
                    for q in range(chunks):
                        first_two(pe, q)
                        with pe.Fori(1, NT // 2) as i:
                            for j in range(2):
                                product(pe, q, i, j, P)
                                turn(pe, i - 1, j, P)
                        product(pe, q, NT // 2, 0, NS)
                        turn(pe, NT // 2 - 1, 0, P)
                        turn(pe, NT // 2 - 1, 1, P)
                        turn(pe, NT // 2, 0, NS)

                @block.scalar
                def _(act):
                    nc.scalar.preload_act_table_set("natural_log_exp_and_others")
                    start(act, 1, *stats)
                    start(act, 16, *stored)
                    if chunks == 1:
                        start(act, 1, *drained)
                    act.wait_ge(eps_set, 1)

                    def stage(act, q, i, j, n):
                        act.wait_ge(st_ld[j], 16 * use(q, i, j) + 16)
                        act.wait_ge(prod[j], 1 + use(q, i, j))
                        nc.scalar.activation(st_hi[j][:, :, :n], st_raw[j][:, :, :n], ACT.Copy).then_inc(hi_d[j], 1)

                    def finish(act, q, i, j, n):
                        t = 2 * i + j
                        if chunks == 1 or q < chunks - 1:
                            act.wait_ge(prod[j], 1 + use(q, i, j) + 1)
                            if chunks == 1:
                                act.wait_ge(stored[j], 16 + 16 * i)
                            if next_norm is not None:
                                act.wait_ge(next_made[j], 1 + i)
                            for half in range(2):
                                c = slice(half * 512, half * 512 + 512)
                                dst = y[j][:n, c] if chunks == 1 else part[:n, bass.ds(t, 1), c].rearrange("p o c -> p (o c)")
                                last = nc.scalar.activation(dst, banks[2 * j + half][:n, :], ACT.Copy)
                            last.then_inc(drained[j], 1)
                        if q == chunks - 1:
                            act.wait_ge(drained[j], 1 + use(q, i, j) + 1)
                            act.wait_ge(stats[j], 1 + 3 * i)
                            act.wait_ge(stats[1 - j], 1 + 3 * i + (3 if j else 0))
                            nc.scalar.activation(junk[:n], y[j][:n], ACT.Square,
                                                 accum_out=stat[:n, j, 0:1]).then_inc(stats[j], 1)
                            act.wait_ge(stats[j], 1 + 3 * i + 1)
                            nc.scalar.activation(stat[:n, j, 1:2], stat[:n, j, 0:1], ACT.Ln, scale=1.0 / D,
                                                 bias=stat[:n, j, 3:4]).then_inc(stats[j], 1)
                            act.wait_ge(stats[j], 1 + 3 * i + 2)
                            nc.scalar.activation(stat[:n, j, 2:3], stat[:n, j, 1:2], ACT.Exp,
                                                 scale=-0.5).then_inc(stats[j], 1)
                            act.wait_ge(normed[j], 1 + 2 * i + 2)
                            act.dma_start(out(t), y[j][:n]).then_inc(stored[j], 16)
                            if next_norm is not None:
                                nc.scalar.activation(junk[:n], y[j][:n], ACT.Square,
                                                     accum_out=next_stat[:n, j, 0:1]).then_inc(next_stats[j], 1)
                                act.wait_ge(next_stats[j], 3 * i + 1)
                                nc.scalar.activation(next_stat[:n, j, 1:2], next_stat[:n, j, 0:1], ACT.Ln,
                                                     scale=1.0 / D, bias=stat[:n, j, 3:4]).then_inc(next_stats[j], 1)
                                act.wait_ge(next_stats[j], 3 * i + 2)
                                nc.scalar.activation(next_stat[:n, j, 2:3], next_stat[:n, j, 1:2], ACT.Exp,
                                                     scale=-0.5).then_inc(next_stats[j], 1)

                    def turn_in(act, i, j, n):
                        if next_norm is None:
                            return
                        act.wait_ge(next_turned[j], 1 + i + 1)
                        for half in range(2):
                            src = banks[4 + 2 * j + half][:].rearrange("p (k c) -> p k c", k=4)[:, :, :n]
                            nc.scalar.activation(xT_hi[:, 4 * half:4 * half + 4, bass.ds((2 * i + j) * P, n)], src,
                                                 ACT.Copy).then_inc(next_hi[j], 1)

                    def split_weights(act, q):
                        for n in range(pieces):
                            m = q * pieces + n
                            act.wait_ge(w_ld[m % slots], 16 * (m // slots + 1))
                            if q and n == 0:
                                for j in range(2):
                                    act.wait_ge(prod[j], 1 + q * USES[j])
                            nc.scalar.activation(w_hi[:, n * kp:(n + 1) * kp], w_raw[m % slots][:], ACT.Copy).then_inc(w_hid, 1)

                    for q in range(chunks):
                        tiles_of(act, q, stage, split_weights, finish, turn_in)
                    for j in range(2):
                        act.wait_ge(stored[j], 16 + 16 * USES[j])

                @block.vector
                def _(v):
                    start(v, 1, *lo_d, *normed)
                    if next_norm is not None:
                        start(v, 1, *next_made, *next_lo)
                    if chunks > 1:
                        start(v, 1, *drained)
                    nc.vector.memset(stat[:, :, 3:4], EPS).then_inc(eps_set, 1)

                    def stage(v, q, i, j, n):
                        v.wait_ge(hi_d[j], use(q, i, j) + 1)
                        split_lo(v, st_lo[j][:, :, :n], st_raw[j][:, :, :n], st_hi[j][:, :, :n]).then_inc(lo_d[j], 1)

                    def finish(v, q, i, j, n):
                        t = 2 * i + j
                        if q < chunks - 1:
                            return
                        if chunks > 1:
                            v.wait_ge(prod[j], 1 + use(q, i, j) + 1)
                            v.wait_ge(stored[j], 16 + 16 * i)
                            for half in range(2):
                                c = slice(half * 512, half * 512 + 512)
                                last = nc.vector.tensor_tensor(
                                    y[j][:n, c], banks[2 * j + half][:n, :],
                                    part[:n, bass.ds(t, 1), c].rearrange("p o c -> p (o c)"), ALU.add)
                            last.then_inc(drained[j], 1)
                        v.wait_ge(const, 16)
                        v.wait_ge(stats[j], 1 + 3 * i + 3)
                        nc.vector.scalar_tensor_tensor(y[j][:n], y[j][:n], stat[:n, j, 2:3], wrow[:n], ALU.mult,
                                                       ALU.mult).then_inc(normed[j], 1)
                        v.wait_ge(normed[j], 1 + 2 * i + 1)
                        v.wait_ge(xld[j], 16 * i + 16)
                        nc.vector.tensor_tensor(y[j][:n], y[j][:n], xr[j][:n], ALU.add).then_inc(normed[j], 1)
                        if next_norm is not None:
                            v.wait_ge(normed[j], 1 + 2 * i + 2)
                            v.wait_ge(w_lod, pieces)
                            v.wait_ge(next_const, 16)
                            v.wait_ge(next_stats[j], 3 * i + 3)
                            v.wait_ge(next_turned[j], 1 + i)
                            nc.vector.scalar_tensor_tensor(next_rows[j][:n, 0], y[j][:n], next_stat[:n, j, 2:3],
                                                           next_w[:n, 0], ALU.mult, ALU.mult
                                                           ).then_inc(next_made[j], 1)

                    def turn_in(v, i, j, n):
                        if next_norm is None:
                            return
                        for half in range(2):
                            v.wait_ge(next_hi[j], 2 * i + half + 1)
                            src = banks[4 + 2 * j + half][:].rearrange("p (k c) -> p k c", k=4)[:, :, :n]
                            at = (slice(None), slice(4 * half, 4 * half + 4), bass.ds((2 * i + j) * P, n))
                            nc.vector.tensor_tensor(xT_lo[at], src, xT_hi[at].bitcast(FP),
                                                    ALU.subtract).then_inc(next_lo[j], 1)

                    def split_weights(v, q):
                        for n in range(pieces):
                            m = q * pieces + n
                            v.wait_ge(w_hid, m + 1)
                            split_lo(v, w_lo[:, n * kp:(n + 1) * kp], w_raw[m % slots][:], w_hi[:, n * kp:(n + 1) * kp]
                                     ).then_inc(w_lod, 1)

                    for q in range(chunks):
                        tiles_of(v, q, stage, split_weights, finish, turn_in)

        attention_block()
        sample_attention_block()
        clear_semaphores()
        att_stack.close()

        def constant_steps(s):
            rows = sb(s, "cs_rows", [CS, 3 * D])
            ld, tr, ev_ = sem("cs_ld"), sem("cs_tr"), sem("cs_ev")

            def load(sp):
                sp.dma_start(rows[:24], a["state_conv"][0].rearrange("b j c -> (b j) c")).then_inc(ld, 16)
                sp.dma_start(rows[24:28], a["conv_w"][0]).then_inc(ld, 16)
                sp.dma_start(mask[:], a["c_mask"].rearrange("n p f -> p n f")).then_inc(ld, 16)
                sp.dma_start(level_mask[:], a["c_levels"].rearrange("n p f -> p n f")).then_inc(ld, 16)
                sp.dma_start(norm_dv[:], a["norm_delta"].rearrange("o d -> d o")).then_inc(ld, 16)

            def turn(pe):
                pe.wait_ge(ld, 80)
                for k in range(24):
                    last = nc.tensor.transpose(banks[3 + k // 12][:, (k % 12) * CS:(k % 12 + 1) * CS],
                                               rows[:, k * P:(k + 1) * P], ident[:CS, :CS])
                last.then_inc(tr, 1)

            def take(v):
                nc.vector.memset(eps_col[:], EPS).then_inc(ev_, 1)
                for m in range(3):
                    nc.vector.memset(pre[m][:, 0:3], 0.0)
                v.wait_ge(tr, 1)
                for b in range(2):
                    src = banks[3 + b][:, :12 * CS].rearrange("p (k c) -> p k c", c=CS)
                    nc.vector.tensor_copy(conv_state[:, 12 * b:12 * b + 12], src[:, :, :24])
                    last = nc.vector.tensor_scalar(conv_wt[:, 12 * b:12 * b + 12], src[:, :, 24:], 0.5, None,
                                                   ALU.mult)
                last.then_inc(ev_, 1)
                v.wait_ge(ev_, 2)

            def over(eng):
                eng.wait_ge(ev_, 2)

            return load, turn, take, over

        hs = ExitStack()
        mask = sb(hs, "mask", [P, 2, P]); level_mask = sb(hs, "level_mask", [P, 6, P])
        eps_col = sb(hs, "eps_col", [P, 1])
        conv_state = sb(hs, "conv_state", [P, 24, 24]); conv_wt = sb(hs, "conv_wt", [P, 24, 4])
        pre = [sb(hs, f"pre{m}", [P, 3 + T]) for m in range(3)]

        def heads_block():
            s = hs
            w_raw = [sb(s, f"w_raw{j}", [P, KT, P]) for j in range(2)]
            w_hi = [sb(s, f"w_hi{j}", [P, KT, P], FR) for j in range(2)]
            w_lo = [sb(s, f"w_lo{j}", [P, KT, P], FR) for j in range(2)]
            qkv = [sb(s, f"qkv{m}", [P, T]) for m in range(3)]
            qc, kc, vc = qkv
            zs, tanh, z_half = sb(s, "zs", [P, T]), sb(s, "tanh", [P, T]), sb(s, "z_half", [P, T])
            F8 = [P, NT, P]
            with ExitStack() as place:
                constants_load, constants_turn, constants_take, constants_over = constant_steps(place)
            k_tok = sb(s, "k_tok", F8); vb = sb(s, "vb", F8); kbe = sb(s, "kbe", F8); kdec = sb(s, "kdec", F8)
            ot = k_tok
            ea = sb(s, "ea", F8); eq = sb(s, "eq", F8)
            sqb = sb(s, "sqb", [P, 4, P])
            wq = sb(s, "wq", [P, NT, 4, C])
            col = sb(s, "col", [P, 10, NT])
            t_sb = [sb(s, f"t_sb{b}", [P, 4, P]) for b in range(2)]
            u_sb = [sb(s, f"u_sb{b}", [P, 4, P]) for b in range(2)]
            x_sb = [sb(s, f"x_sb{b}", [P, 4, P]) for b in range(2)]
            u_val = sb(s, "u_val", F8)
            qe = u_val[:].rearrange("p a b -> p (a b)")
            vnew = [sb(s, f"vnew{j}", [P, P]) for j in range(2)]
            state = [sb(s, f"state{j}", [P, P]) for j in range(2)]
            gate = [sb(s, f"gate{m}", [P, T]) for m in range(2)]
            ident_b = sb(s, "ident_b", [P, P], mybir.dt.bfloat16)
            ob_out = eq[:].rearrange("p a b -> p (a b)")
            wld = [sem("w_loaded") for j in range(2)]
            whi = [ev("w_hi", 3, 1) for j in range(2)]
            wlo = [ev("w_lo", 3, 1) for j in range(2)]
            tile_done = [ev("tile_done", 3, 1) for j in range(2)]
            group = [ev("group", 6, 2) for g in range(2)]
            evac = [ev("evac", 6, 2) for g in range(3)]
            thalf = ev("thalf", 4); silu = ev("silu", 4); conv = ev("conv_taps", 3 * 7)
            gs = ev("gate_sig", 2, 2)
            gout = sem("gate_out")
            D1 = dict(k_ev=2, q_ev=2, v_ev=2, turned=6, sq=2, dcol=1, drow=1, ssq=4, lncol=1, ecol=1,
                      cols=1, diag=2, rb=4, ea_m=2, eq_m=2, ea_x=2, eq_x=2, qe_x=2, qew=1, gram=4, an=2, pt=2,
                      xm=12, xs=12, ym=12, tc=10, uc=12, kbe_m=1, kdec_m=1, uw=4, u_ev=2, w_ev=2,
                      sm=17, m1=16, vn=16, m2=16, m3=16, o_ev=16, osq=1, oss=1, oln=2, on=1, ot_tr=2, ob=4,
                      samp_m=1, cn=3)
            E = {k: ev(k, n, -1 if k in ("ob", "ssq") else 0) for k, n in D1.items()}
            out_dma = sem("ob_out"); st_dma = sem("state_out"); identity = sem("identity")
            tiles = (GATE0, GATE0 + D, CONV0, CONV0 + D, CONV0 + 2 * D, Z0)
            NTILE, QT, ZT = 6, 2, 5
            STEPS = 3 * KT
            per_slot = [20, 4, 8, 8] + 6 * [4] + [4] + 16 * [4] + [10, 2]
            done = sums(per_slot)
            INVERSE, SCAN, TAIL = 4, 11, 27

            def pipelined(eng, project, recur, lag=1):
                Filler(project(eng, 0, None)).finish()
                with eng.Fori(0, HB - 1) as i:
                    fill = Filler(project(eng, i + 1, i), done, lag)
                    recur(eng, i, fill)
                    fill.finish()
                fill = Filler(project(eng, HB, HB - 1), done, lag)
                recur(eng, HB - 1, fill)
                fill.finish()

            def turn_tiles(h):
                if isinstance(h, int):
                    return (QT, NTILE) if h == 0 else (0, QT)
                return 0, NTILE

            def wait(eng, event, turn, step):
                if not (isinstance(turn, int) and event.at(turn, step) <= 0):
                    eng.wait_ge(event.sem, event.at(turn, step))

            def inc(ins, name):
                ins.then_inc(E[name].sem, 1)

            def wt(eng, name, i, k):
                wait(eng, E[name], i, k)

            def project_pe(pe, h, prev):
                for m in range(*turn_tiles(h)):
                    j, u = m % 2, m // 2
                    for g in range(3):
                        c = slice(g * G3, (g + 1) * G3)
                        for k in range(KT):
                            yield m * STEPS + g * KT + k + 1
                            if k == 0 and g == 0:
                                wait(pe, wlo[j], h, u + 1)
                            if k == 0:
                                wait(pe, evac[g], h, m)
                            last = passes(banks[g][:, :G3], w_hi[j][:, k], w_lo[j][:, k],
                                          xT_hi[:, k, c], xT_lo[:, k, c], k == 0, k == KT - 1)
                        last.then_inc(group[g].sem if g < 2 else tile_done[j].sem, 1)

            def project_act(act, h, prev):
                def hi(m):
                    j, u = m % 2, m // 2
                    wait(act, tile_done[j], h, u)
                    act.wait_ge(wld[j], (h * 3 + u) * 16)
                    split_weights_hi(act, w_hi[j][:], w_raw[j][:]).then_inc(whi[j].sem, 1)

                def read_out(m, g):
                    j, u, c = m % 2, m // 2, slice(g * G3, (g + 1) * G3)
                    if g == 0:
                        if m < QT:
                            act.wait_ge(gout, 16 + prev * 32)
                        elif m < ZT:
                            wait(act, conv, h, 0); wt(act, "cn", h, 0)
                        else:
                            wait(act, silu, h, 0)
                    if g < 2:
                        wait(act, group[g], h, m + 1)
                    else:
                        wait(act, tile_done[j], h, u + 1)
                    src = banks[g][:, :G3]
                    if m < QT:
                        x = nc.scalar.activation(gate[m][:, c], src, ACT.Tanh, scale=0.5)
                    elif m < ZT:
                        x = nc.scalar.activation(pre[m - QT][:, 3 + g * G3:3 + (g + 1) * G3], src, ACT.Copy)
                    else:
                        x = nc.scalar.activation(z_half[:, c], src, ACT.Copy, scale=0.5)
                    x.then_inc(evac[g].sem, 1)

                def gate_out(m):
                    wait(act, gs, h, m + 1)
                    act.dma_start(gate_scr[m, bass.ds(prev, 1)].rearrange("o p t -> (o p) t"),
                                  gate[m][:]).then_inc(gout, 16)

                def tanh_of(m):
                    wait(act, conv, h, 7 * (m - QT) + 7)
                    wait(act, silu, h, m - QT)
                    nc.scalar.activation(tanh[:], qkv[m - QT][:], ACT.Tanh).then_inc(thalf.sem, 1)

                first, end = turn_tiles(h)
                yield 0
                hi(first)
                yield 1
                hi(first + 1)
                for m in range(first, end + 1):
                    n = m * STEPS
                    if m < end:
                        yield n + KT
                        read_out(m, 0)
                    if first < m <= QT:
                        yield n + KT + 1
                        gate_out(m - 1)
                    if m < end:
                        yield n + 2 * KT
                        read_out(m, 1)
                    if QT < m <= ZT:
                        yield n + 2 * KT + 2
                        tanh_of(m - 1)
                    if m < end:
                        yield n + 3 * KT
                        read_out(m, 2)
                    if m + 2 < end:
                        yield n + 3 * KT
                        hi(m + 2)
                    if QT <= m < min(ZT, end):
                        wait(act, evac[2], h, m + 1)
                        inc(nc.scalar.activation(conv_new[:, bass.ds((m - QT) * HB + h, 1)],
                                                 pre[m - QT][:, L:L + 3 + NS].unsqueeze(1), ACT.Copy), "cn")

            def project_dve(v, h, prev):
                def lo(m):
                    j, u = m % 2, m // 2
                    wait(v, whi[j], h, u + 1)
                    split_lo(v, w_lo[j][:], w_raw[j][:], w_hi[j][:]).then_inc(wlo[j].sem, 1)

                def silu_of(m):
                    y = qkv[m - QT]
                    wait(v, thalf, h, m - QT + 1)
                    nc.vector.scalar_tensor_tensor(y[:], tanh[:], 1.0, y[:], ALU.add,
                                                   ALU.mult).then_inc(silu.sem, 1)

                first, end = turn_tiles(h)
                yield 0
                lo(first)
                yield 1
                lo(first + 1)
                for m in range(first, end + 1):
                    n = m * STEPS
                    if QT < m <= ZT:
                        cm = m - 1 - QT
                        yield n
                        wait(v, evac[2], h, m)
                        if prev is not None:
                            wt(v, "gram", prev, 4); wt(v, "qew", prev, 1); wt(v, "samp_m", prev, 1)
                        x, y = pre[cm], qkv[cm]
                        ysm = y[:, L:].unsqueeze(2)
                        k8 = bass.ds(cm * HB + h, 1)
                        st = conv_state[:, k8].rearrange("p o (b j) -> p (o b) j", j=3)
                        cw = conv_wt[:, k8].rearrange("p o j -> p (o j)")
                        nc.vector.tensor_scalar(y[:], x[:, 3:], cw[:, 3:4], None,
                                                ALU.mult).then_inc(conv.sem, 1)
                        for k, tap in enumerate((2, 1, 0)):
                            yield n + 4 * (k + 1)
                            wait(v, conv, h, 7 * cm + 1 + 2 * k)
                            nc.vector.scalar_tensor_tensor(
                                y[:, L:].unsqueeze(2), st[:, :, tap:tap + 1], cw[:, tap:tap + 1], ysm,
                                ALU.mult, ALU.add).then_inc(conv.sem, 1)
                            nc.vector.scalar_tensor_tensor(
                                y[:, :L], x[:, tap:tap + L], cw[:, tap:tap + 1], y[:, :L],
                                ALU.mult, ALU.add).then_inc(conv.sem, 1)
                    if QT < m <= ZT:
                        yield n + 2 * KT + 4
                        silu_of(m - 1)
                    if m + 2 < end:
                        yield n + 3 * KT
                        lo(m + 2)
                    if m < min(QT, end):
                        yield n + 3 * KT + 1
                        wait(v, evac[2], h, m + 1)
                        nc.vector.tensor_scalar(gate[m][:], gate[m][:], 0.5, 0.5, ALU.mult,
                                                ALU.add).then_inc(gs.sem, 1)

            def recur_pe(pe, i, fill):
                wt(pe, "ob", i, 0)
                for n, (src, b, need) in enumerate(((1, 0, 2), (1, 1, None), (0, 0, 1), (0, 1, None),
                                                    (2, 0, 3), (2, 1, None))):
                    if need:
                        pe.wait_ge(silu.sem, silu.at(i, need))
                    if n == 5:
                        wt(pe, "k_ev", i, 1)
                    for p in range(4):
                        c = (4 * b + p) * P
                        last = nc.tensor.transpose(banks[(3, 4, 5, 6, 7, 3)[n]][:, p * P:(p + 1) * P],
                                                   qkv[src][:, c:c + P], ident[:])
                    inc(last, "turned")
                fill.slot(0)
                wt(pe, "k_ev", i, 2); wt(pe, "q_ev", i, 2); wt(pe, "v_ev", i, 1)
                for n in range(4):
                    if n == 2:
                        fill.slot(1)
                    wt(pe, "diag", i, n // 2 + 1)
                    src = (kbe if n < 2 else kdec)[:, 4 * (n % 2):4 * (n % 2) + 4]
                    inc(nc.tensor.matmul(banks[4 + n][:], ident_ones[:], src.rearrange("p a b -> p (a b)"),
                                         start=True, stop=True), "rb")
                wt(pe, "v_ev", i, 2)
                for n in range(4):
                    if n == 1:
                        wt(pe, "ea_m", i, 1)
                    if n == 2:
                        fill.slot(2)
                        wt(pe, "ea_m", i, 2)
                    if n == 3:
                        wt(pe, "eq_m", i, 1); wt(pe, "qe_x", i, 1)
                    for p in range(4):
                        c = slice((4 * (n % 2) + p) * P, (4 * (n % 2) + p + 1) * P)
                        last = nc.tensor.matmul(banks[3 + n][:, p * P:(p + 1) * P], kc[:, c],
                                                (kc if n < 2 else qc)[:, c], start=True, stop=True)
                    inc(last, "gram")
                fill.slot(3)
                wt(pe, "an", i, 2); wt(pe, "pt", i, 2); wt(pe, "eq_m", i, 2); wt(pe, "qe_x", i, 2)
                tb, ub = (7, 4), (3, 5)
                for b in range(2):
                    for bank in (tb[b], ub[b]):
                        nc.tensor.matmul(banks[bank][:].rearrange("p (a b) -> p a b", a=4), ident_b[:],
                                         ident_b[:].unsqueeze(1).to_broadcast([P, 4, P]),
                                         start=True, stop=False, skip_group_check=True)
                for lev in range(6):
                    for b in range(2):
                        n = 2 * lev + b
                        if lev:
                            wt(pe, "tc", i, n - 1)
                        fill.upto(done[INVERSE + lev] - 4 + b + 1)
                        if n:
                            wt(pe, "xs", i, n)
                        for p in range(4):
                            bank = banks[6][:, p * P:(p + 1) * P]
                            if lev:
                                last = nc.tensor.matmul(bank, ea[:, 4 * b + p], t_sb[b][:, p],
                                                        start=True, stop=True)
                            else:
                                last = nc.tensor.transpose(bank, ea[:, 4 * b + p], ident[:])
                        inc(last, "xm")
                    for b in range(2):
                        n = 2 * lev + b
                        fill.upto(done[INVERSE + lev] - 2 + b + 1)
                        wt(pe, "xs", i, n + 1)
                        if lev:
                            wt(pe, "uc", i, n - 1)
                        for p in range(4):
                            cs = slice(p * P, (p + 1) * P)
                            u = u_sb[b][:, p] if lev else ident[:]
                            if lev < 5:
                                nc.tensor.matmul(banks[tb[b]][:, cs], u, x_sb[b][:, p], start=False,
                                                 stop=False, skip_group_check=True)
                            last = nc.tensor.matmul(banks[ub[b]][:, cs], x_sb[b][:, p], u, start=False,
                                                    stop=False, skip_group_check=True)
                        inc(last, "ym")
                fill.slot(SCAN - 1)
                wt(pe, "tc", i, 10); wt(pe, "uc", i, 12); wt(pe, "kbe_m", i, 1)
                for b in range(2):
                    for p in range(4):
                        last = nc.tensor.matmul(banks[6 + b][:, p * P:(p + 1) * P], u_sb[b][:, p],
                                                vb[:, 4 * b + p], start=True, stop=True)
                    inc(last, "uw")
                    for p in range(4):
                        last = nc.tensor.matmul(banks[4 - b][:, p * P:(p + 1) * P], kbe[:, 4 * b + p],
                                                u_sb[b][:, p], start=True, stop=True)
                    inc(last, "uw")
                wt(pe, "u_ev", i, 2); wt(pe, "w_ev", i, 2); wt(pe, "qew", i, 1); wt(pe, "kdec_m", i, 1)
                for c in range(16):
                    p, r = c // 2, c % 2
                    ob, db = banks[5 + c % 2], banks[3 + c % 2]
                    rows = slice(64 * r, 64 * r + 64)
                    other = slice(64 - 64 * r, 128 - 64 * r)
                    wt(pe, "sm", i, c + 1)
                    if c >= 2:
                        wt(pe, "o_ev", i, c - 1)
                    inc(nc.tensor.matmul(ob[:, :P], wq[:, p, 2 * r:2 * r + 2].rearrange("p a b -> p (a b)"),
                                         state[c % 2][:], start=True, stop=False, skip_group_check=True), "m1")
                    fill.upto(done[SCAN + c] - 2)
                    wt(pe, "vn", i, c + 1)
                    inc(nc.tensor.matmul(db[:, :P], kdec[rows, p], vnew[c % 2][rows],
                                         start=True, stop=True), "m3")
                    inc(nc.tensor.matmul(ob[other, :P], eq[rows, p, rows], vnew[c % 2][rows],
                                         start=False, stop=True, skip_group_check=True), "m2")
                    fill.slot(SCAN + c)
                fill.slot(TAIL)
                wt(pe, "sm", i, 17)
                wt(pe, "on", i, 1)
                for b in range(2):
                    for p in range(4):
                        last = nc.tensor.transpose(banks[3 + b][:, p * P:(p + 1) * P], ot[:, 4 * b + p],
                                                   ident[:])
                    inc(last, "ot_tr")
                fill.slot(TAIL + 1)

            def recur_act(act, i, fill):
                fill.slot(0)
                for b in range(2):
                    wt(act, "turned", i, b + 1)
                    inc(nc.scalar.activation(k_tok[:, 4 * b:4 * b + 4].rearrange("p a b -> p (a b)"),
                                             banks[3 + b][:], ACT.Copy), "k_ev")
                for b in range(2):
                    wt(act, "turned", i, b + 3)
                    if b == 0:
                        wt(act, "ssq", i, 2)
                    else:
                        wt(act, "ssq", i, 3)
                    inc(nc.scalar.activation(sqb[:].rearrange("p a b -> p (a b)"), banks[5 + b][:],
                                             ACT.Square), "q_ev")
                wt(act, "ssq", i, 4)
                inc(nc.scalar.activation(col[:, 0:2], col[:, 0:2], ACT.Ln, bias=eps_col[:]), "lncol")
                fill.slot(1)
                wt(act, "cols", i, 1)
                inc(nc.scalar.activation(col[:, 6:8], col[:, 4:6], ACT.Exp), "ecol")
                wait(act, silu, i, 3); wait(act, evac[2], i, NTILE)
                nc.scalar.activation(tanh[:], z_half[:], ACT.Tanh).then_inc(thalf.sem, 1)
                fill.slot(2)
                for b in range(2):
                    wt(act, "ea_m", i, b + 1)
                    inc(nc.scalar.activation(ea[:, 4 * b:4 * b + 4], ea[:, 4 * b:4 * b + 4], ACT.Exp), "ea_x")
                for b in range(2):
                    wt(act, "eq_m", i, b + 1)
                    inc(nc.scalar.activation(qe[:, 512 * b:512 * b + 512], banks[6 + b][:], ACT.Exp), "qe_x")
                for b in range(2):
                    wt(act, "eq_m", i, b + 1)
                    inc(nc.scalar.activation(eq[:, 4 * b:4 * b + 4], eq[:, 4 * b:4 * b + 4], ACT.Exp), "eq_x")
                fill.slot(3)
                for n in range(10):
                    b = n % 2
                    if b == 0:
                        fill.slot(INVERSE + n // 2)
                    wt(act, "ym", i, n + 1)
                    inc(nc.scalar.activation(t_sb[b][:].rearrange("p a b -> p (a b)"),
                                             banks[(7, 4)[b]][:], ACT.Copy), "tc")
                fill.slot(SCAN - 1)
                for b in range(2):
                    wt(act, "uw", i, 2 * b + 1)
                    inc(nc.scalar.activation(u_val[:, 4 * b:4 * b + 4].rearrange("p a b -> p (a b)"),
                                             banks[6 + b][:], ACT.Copy), "u_ev")
                for c in range(16):
                    p, r = c // 2, c % 2
                    other = slice(64 - 64 * r, 128 - 64 * r)
                    fill.slot(SCAN + c)
                    wt(act, "m2", i, c + 1)
                    inc(nc.scalar.activation(ot[other, p], banks[5 + c % 2][other, :P], ACT.Copy), "o_ev")
                fill.slot(TAIL)
                nc.scalar.preload_act_table_set("natural_log_exp_and_others")
                wt(act, "oss", i, 1)
                inc(nc.scalar.activation(col[:, 8], col[:, 8], ACT.Ln, scale=1.0 / DK, bias=eps_col[:]), "oln")
                wt(act, "oln", i, 1)
                inc(nc.scalar.activation(col[:, 8], col[:, 8], ACT.Exp, scale=-0.5), "oln")
                wt(act, "sm", i, 17)
                act.dma_start(o["delta_p"][0, 0, bass.ds(i, 1)].rearrange("o p t -> (o p) t"),
                              state[0][:]).then_inc(st_dma, 16)
                fill.slot(TAIL + 1)
                wt(act, "ob", i, 4)
                act.dma_start(ob_scr[bass.ds(i, 1)].rearrange("o p t -> (o p) t")[:, :L],
                              ob_out).then_inc(out_dma, 16)

            def recur_dve(v, i, fill):
                fill.slot(0)
                for b in range(2):
                    wt(v, "k_ev", i, b + 1)
                    kt4 = k_tok[:, 4 * b:4 * b + 4]
                    wt(v, "ssq", i, b)
                    inc(nc.vector.tensor_tensor(sqb[:], kt4, kt4, ALU.mult), "sq")
                    wt(v, "sq", i, b + 1)
                    inc(nc.vector.reduce_sum(col[:, 0, 4 * b:4 * b + 4], sqb[:], AX.X), "ssq")
                for b in range(2):
                    wt(v, "q_ev", i, b + 1)
                    inc(nc.vector.reduce_sum(col[:, 1, 4 * b:4 * b + 4], sqb[:], AX.X), "ssq")
                beta_h = beta_all[:, bass.ds(i, 1)].rearrange("p o t -> p (o t)")
                for b in range(2):
                    wt(v, "turned", i, b + 5)
                    bank = banks[(7, 3)[b]][:].rearrange("p (a b) -> p a b", a=4)
                    bt = beta_h[:, 4 * b:4 * b + 4].unsqueeze(2).to_broadcast([P, 4, P])
                    inc(nc.vector.tensor_tensor(vb[:, 4 * b:4 * b + 4], bank, bt, ALU.mult), "v_ev")
                fill.slot(1)
                wt(v, "lncol", i, 1)
                for dst, lr, st in ((3, 0, 1), (2, 1, 2), (5, 0, 3), (4, 0, 0)):
                    x = nc.vector.scalar_tensor_tensor(
                        col[:, dst], col[:, lr], -0.5,
                        stage_g[:, st, bass.ds(i, 1)].rearrange("p o t -> p (o t)"), ALU.mult, ALU.add)
                inc(x, "cols")
                wt(v, "cols", i, 1)
                for dst, c in ((kbe, 4), (kdec, 2)):
                    inc(nc.vector.tensor_tensor(dst[:], ident[:].unsqueeze(1).to_broadcast(F8),
                                                col[:, c].unsqueeze(2).to_broadcast(F8), ALU.mult), "diag")
                wait(v, thalf, i, 4)
                wt(v, "ob", i, 0)
                nc.vector.scalar_tensor_tensor(zs[:], tanh[:], 1.0, z_half[:], ALU.add,
                                               ALU.mult).then_inc(silu.sem, 1)
                fill.slot(2)
                for n in range(4):
                    if n == 2:
                        v.wait_ge(out_dma, 16 + i * 16)
                    wt(v, "rb", i, n + 1)
                    dst = ea if n < 2 else eq
                    for p in range(4):
                        q = 4 * (n % 2) + p
                        x = nc.vector.scalar_tensor_tensor(
                            dst[:, q], banks[4 + n][:, p * P:(p + 1) * P], col[:, 3, q:q + 1],
                            mask[:, n // 2], ALU.add, ALU.min)
                    inc(x, "ea_m" if n < 2 else "eq_m")
                wt(v, "qe_x", i, 2)
                inc(nc.vector.tensor_tensor(wq[:, :, 1:3], qc[:, :L].rearrange("p (a b c) -> p a b c", a=8, b=2),
                                            qe.rearrange("p (a b c) -> p a b c", a=8, b=2), ALU.mult), "qew")
                for b in range(2):
                    bs = slice(4 * b, 4 * b + 4)
                    wt(v, "gram", i, b + 1); wt(v, "ea_x", i, b + 1)
                    inc(nc.vector.scalar_tensor_tensor(
                        ea[:, bs].rearrange("p a b -> p (a b)"), banks[3 + b][:], -1.0,
                        ea[:, bs].rearrange("p a b -> p (a b)"), ALU.mult, ALU.mult), "an")
                for b in range(2):
                    bs = slice(4 * b, 4 * b + 4)
                    wt(v, "gram", i, b + 3); wt(v, "eq_x", i, b + 1)
                    inc(nc.vector.tensor_tensor(
                        eq[:, bs].rearrange("p a b -> p (a b)"), banks[5 + b][:],
                        eq[:, bs].rearrange("p a b -> p (a b)"), ALU.mult), "pt")
                wait(v, silu, i, 4)
                for n, x in enumerate((qc, kc, vc, zs)):
                    x = nc.vector.tensor_copy(samp[:, n, bass.ds(i, 1)], x[:, L:].unsqueeze(1))
                inc(x, "samp_m")
                fill.slot(3)
                wt(v, "ecol", i, 1)
                for dst, c, name in ((kbe, 6, "kbe_m"), (kdec, 7, "kdec_m")):
                    inc(nc.vector.tensor_tensor(dst[:], k_tok[:], col[:, c].unsqueeze(2).to_broadcast(F8),
                                                ALU.mult), name)
                for lev in range(6):
                    fill.slot(INVERSE + lev)
                    for b in range(2):
                        wt(v, "xm", i, 2 * lev + b + 1)
                        inc(nc.vector.tensor_tensor(
                            x_sb[b][:], banks[6][:].rearrange("p (a b) -> p a b", a=4),
                            level_mask[:, lev].unsqueeze(1).to_broadcast([P, 4, P]), ALU.mult), "xs")
                    for b in range(2):
                        wt(v, "ym", i, 2 * lev + b + 1)
                        inc(nc.vector.tensor_copy(u_sb[b][:].rearrange("p a b -> p (a b)"),
                                                  banks[(3, 5)[b]][:]), "uc")
                fill.slot(SCAN - 1)
                for b in range(2):
                    wt(v, "uw", i, 2 * b + 2)
                    inc(nc.vector.tensor_copy(
                        wq[:, 4 * b:4 * b + 4, 0:4:3],
                        banks[4 - b][:].rearrange("p (a b c) -> p a b c", a=4, b=2)), "w_ev")
                v.wait_ge(st_dma, 16 + i * 16)
                inc(nc.vector.memset(state[0][:], 0.0), "sm")
                wt(v, "u_ev", i, 2)
                for c in range(16):
                    p, r = c // 2, c % 2
                    rows = slice(64 * r, 64 * r + 64)
                    wt(v, "m1", i, c + 1)
                    inc(nc.vector.tensor_tensor(vnew[c % 2][rows], u_val[rows, p], banks[5 + c % 2][rows, :P],
                                                ALU.subtract), "vn")
                    wt(v, "m3", i, c + 1)
                    eg = eglast[:, bass.ds(i, 1), c:c + 1].rearrange("p a b -> p (a b)")
                    inc(nc.vector.scalar_tensor_tensor(state[(c + 1) % 2][:], state[c % 2][:], eg,
                                                       banks[3 + c % 2][:, :P], ALU.mult, ALU.add), "sm")
                    fill.slot(SCAN + c)
                wt(v, "o_ev", i, 16)
                inc(nc.vector.tensor_tensor(u_val[:], ot[:], ot[:], ALU.mult), "osq")
                wt(v, "osq", i, 1)
                inc(nc.vector.reduce_sum(col[:, 8], u_val[:], AX.X), "oss")
                wt(v, "oln", i, 2)
                inc(nc.vector.tensor_tensor(ot[:], ot[:], col[:, 8].unsqueeze(2).to_broadcast(F8),
                                            ALU.mult), "on")
                fill.slot(TAIL)
                for b in range(2):
                    wt(v, "ot_tr", i, b + 1)
                    bank = banks[3 + b][:].rearrange("p (a b c) -> p a b c", a=4, b=2)
                    zv = zs[:, 512 * b:512 * b + 512].rearrange("p (a b c) -> p a b c", a=4, b=2)
                    out = ob_out[:, 512 * b:512 * b + 512].rearrange("p (a b c) -> p a b c", a=4, b=2)
                    for r in range(2):
                        inc(nc.vector.scalar_tensor_tensor(out[:, :, r], bank[:, :, 1 - r], norm_dv[:],
                                                           zv[:, :, r], ALU.mult, ALU.mult), "ob")

            with nc.Block() as block:
                @block.sync
                def _(sp):
                    constants_load(sp)

                    def load(h, prev):
                        for m in range(*turn_tiles(h)):
                            j, u = m % 2, m // 2
                            wait(sp, wlo[j], h, u)
                            sp.dma_start(w_raw[j][:], w_in[:, :, bass.ds(tiles[m] + (prev if m < QT else h) * P, P)]
                                         ).then_inc(wld[j], 16)

                    load(0, None)
                    with sp.Fori(0, HB - 1) as i:
                        load(i + 1, i)
                    load(HB, HB - 1)

                @block.tensor
                def _(pe):
                    pe.wait_ge(identity, 1)
                    constants_turn(pe)
                    constants_over(pe)
                    pipelined(pe, project_pe, recur_pe, lag=0)

                @block.scalar
                def _(act):
                    start(act, 16, gout, st_dma, out_dma)
                    constants_over(act)
                    pipelined(act, project_act, recur_act)
                    act.wait_ge(gout, 16 + HB * 32)
                    act.wait_ge(st_dma, 16 + HB * 16)
                    act.wait_ge(out_dma, 16 + HB * 16)

                @block.vector
                def _(v):
                    nc.vector.tensor_copy(ident_b[:], ident[:]).then_inc(identity, 1)
                    constants_take(v)
                    start(v, 1, E["ob"].sem, E["ssq"].sem)
                    pipelined(v, project_dve, recur_dve)

        heads_block()
        hs.close()
        mix_stack = ExitStack()
        oa_hi = sb(mix_stack, "oa_hi", [P, 2, T], FR); oa_lo = sb(mix_stack, "oa_lo", [P, 2, T], FR)
        sample_delta_block()
        clear_semaphores()
        wa_v = a["w_branch_a"][0].rearrange("(k p) n -> p k n", p=P)
        wb_v = a["w_branch_b"][0].rearrange("(k p) n -> p k n", p=P)
        wf_v = a["w_ffn_in"][0].rearrange("(k p) n -> p k n", p=P)
        xT = (xT_hi, xT_lo)
        pair_block("mix", KT, 2, (oa_hi, oa_lo), xT, lambda n: wa_v[:, :, bass.ds(n * P, P)],
                   lambda n: wb_v[:, :, bass.ds(n * P, P)], True, mix_scr)
        mix_stack.close()

        def rows_of(prompt, sample):
            def get(t):
                return sample if isinstance(t, int) and t == NT else prompt[bass.ds(t * P, P)]
            return get

        row_block("wo", mix_scr, KT, 1, a["w_out"][0], a["norm_post_mix"][0], rows_of(xp, xs),
                  rows_of(x1_scr[:L], x1_scr[L:]), a["norm_pre_ffn"][0])
        pair_block("ffn", FT, KT, xT, xT, lambda n: wf_v[:, :, bass.ds(n * P, P)],
                   lambda n: wf_v[:, :, bass.ds(FF + n * P, P)], False, act_scr)
        early.close()
        row_block("fo", act_scr, FT, 2, a["w_ffn_out"][0], a["norm_post_ffn"][0],
                  rows_of(x1_scr[:L], x1_scr[L:]),
                  rows_of(o["y_prompt"][0], o["y_sample"].rearrange("b s d -> (b s) d")))


def shape_constants():
    import numpy as np

    f = np.float32
    t = np.arange(P)
    i, j = t[:, None], t[None, :]
    same = i // C == j // C
    far = f(1e30)
    sums = np.stack([same & (i <= j), same, np.broadcast_to(i < C, (P, P)), np.broadcast_to(i >= C, (P, P))])
    mask = np.stack([np.where(same & (j > i), far, -far), np.where(same & (j >= i), far, -far)])
    levels = np.stack([(i // (2 * s) == j // (2 * s)) & ((i // s) % 2 == 1) & ((j // s) % 2 == 0)
                       for s in (1, 2, 4, 8, 16, 32)])
    onehot = np.zeros((33, NG, 3 * P), f)
    onehot_s = np.zeros((33, NG, P + 1), f)
    onehot[32], onehot_s[32] = -far, -far
    for g, dil in enumerate((1, 4, 16)):
        dist = np.arange(P + 1) * dil
        large = 16 + (np.log(np.maximum(dist, 1).astype(f) / 16) / np.log(2048 / 16) * 16).astype(np.int32)
        bucket = np.where(dist < 16, dist, np.minimum(large, 31)).astype(np.int32)
        step, last = (2, HD - 1) if g == 2 else (1, P)
        for n in range(last + 1):
            onehot[bucket[n], g, 2 * P - 1 - step * n] = 1
            onehot[32, g, 2 * P - 1 - step * n] = 0
        keys = HD if g == 2 else P
        for n in range(keys):
            onehot_s[bucket[keys - n], g, n] = 1
            onehot_s[32, g, n] = 0
        onehot_s[bucket[0], g, P] = 1
        onehot_s[32, g, P] = 0
    return {"c_ident": np.eye(P, dtype=f), "c_sums": sums.astype(f), "c_mask": mask.astype(f),
            "c_levels": levels.astype(f), "c_onehot": onehot, "c_onehot_s": onehot_s,
            "c_ones": np.ones((1, 16), f)}


_INS = ["x_prompt", "x_sample", "cache_kv_w128", "cache_kv_w512", "cache_kv_w2048", "state_delta", "state_conv",
        "rel_bias", "norm_pre_mix", "w_in", "conv_w", "a_log", "dt_bias", "norm_delta", "w_branch_a", "w_branch_b",
        "w_out", "norm_post_mix", "norm_pre_ffn", "w_ffn_in", "w_ffn_out", "norm_post_ffn"]
_OUTS = [("y_prompt", (1, L, D)), ("y_sample", (NS, 1, D)),
         ("kv128_p", (1, 1, 128, 2, HA, HD)), ("kv512_p", (1, 1, 512, 2, HA, HD)), ("kv2048_p", (1, 1, L, 2, HA, HD)),
         ("delta_p", (1, 1, HB, DK, DK)), ("conv_p", (1, 1, 3, 3 * D)),
         ("kv128_s", (1, NS, 1, 2, HA, HD)), ("kv512_s", (1, NS, 1, 2, HA, HD)), ("kv2048_s", (1, NS, 1, 2, HA, HD)),
         ("delta_s", (1, NS, HB, DK, DK)), ("conv_s", (1, NS, 3, 3 * D))]


def kernel(**inputs):
    import numpy as np
    import concourse.bacc as bacc
    from concourse.bass_utils import run_bass_kernel_spmd

    nc = bacc.Bacc("TRN2", target_bir_lowering=False, num_devices=1)
    arrays, a, o = {}, {}, {}
    given = {name: np.ascontiguousarray(inputs[name]) for name in _INS}
    given.update(shape_constants())
    for name, x in given.items():
        arrays[f"in_{name}"] = x
        a[name] = nc.dram_tensor(f"in_{name}", x.shape, FP, kind="ExternalInput").ap()
    for name, shape in _OUTS:
        o[name] = nc.dram_tensor(f"out_{name}", shape, FP, kind="ExternalOutput").ap()
    build(nc, a, o)
    r = run_bass_kernel_spmd(nc, [arrays], core_ids=[0])
    return tuple(r.results[0][f"out_{name}"] for name, _ in _OUTS)
```
